# Optimizing a Trainium2 kernel written in Bass

```python
import jax, jax.numpy as jnp
from jax import lax
import numpy as np

D_MODEL = 1024
BATCH = 1
SEQ = 256
DEPTH = 2

CHUNK = 64
EPS = 1e-6
ROPE_THETA = 10000.0

A_HEADS = 4
A_DK = 128
A_DV = 128
A_WIDTH = A_HEADS * A_DV
B_GROUPS = 4
B_GROUP_DIM = 128
B_WIDTH = B_GROUPS * B_GROUP_DIM
B_BLOCK = 128
C_HEADS = 4
C_HEAD_DIM = 128
C_WIDTH = C_HEADS * C_HEAD_DIM
IDX_HEADS = 8
IDX_DIM = 64
DSA_TOPK_MAX = 256
Q_BLOCK = 128
N_BRANCH = 3
BRANCH_WIDTH = 512
PEER_HEADS = 8
PEER_N_KEYS = 128
PEER_N_EXPERTS = PEER_N_KEYS * PEER_N_KEYS
PEER_KEY_DIM = 128
PEER_TOPK = 16
PEER_BLOCK = 128

IN_SIZES = (A_HEADS * A_DK, A_HEADS * A_DK, A_WIDTH, A_WIDTH,
            B_WIDTH, B_WIDTH,
            C_WIDTH, C_WIDTH, C_WIDTH,
            IDX_HEADS * IDX_DIM, IDX_DIM, IDX_HEADS,
            N_BRANCH * D_MODEL)
N_IN = sum(IN_SIZES)

kernel_name = "hybrid_hgrn2_gmlp_dsa_peer_trunk"

def rmsnorm(x, gain):
    xf = x.astype(jnp.float32)
    y = xf * lax.rsqrt(jnp.mean(xf * xf, axis=-1, keepdims=True) + EPS)
    return (y * gain.astype(jnp.float32)).astype(x.dtype)

def rope(x, positions):
    half = x.shape[-1] // 2
    inv = ROPE_THETA ** (-jnp.arange(half, dtype=jnp.float32) / half)
    ang = positions.astype(jnp.float32)[..., None] * inv
    cos = jnp.cos(ang)[:, :, None, :]
    sin = jnp.sin(ang)[:, :, None, :]
    x1 = x[..., :half].astype(jnp.float32)
    x2 = x[..., half:].astype(jnp.float32)
    out = jnp.concatenate([x1 * cos - x2 * sin, x2 * cos + x1 * sin], axis=-1)
    return out.astype(x.dtype)

def hgrn2_mixer(q, f_logit, i, g, lb, norm_gain):
    B, S, _ = q.shape
    nc = S // CHUNK
    f32 = jnp.float32
    lbf = lb.astype(f32)
    z = f_logit.astype(f32)
    logf = jnp.logaddexp(jnp.log(lbf), jnp.log1p(-lbf) + jax.nn.log_sigmoid(z))
    key = (1.0 - lbf) * jax.nn.sigmoid(-z)
    qf = jax.nn.silu(q.astype(f32)) * (A_DK ** -0.5)
    vf = i.astype(f32)

    def to_chunks(t, d):
        return t.reshape(B, nc, CHUNK, A_HEADS, d).transpose(1, 0, 3, 2, 4)

    tri = jnp.tril(jnp.ones((CHUNK, CHUNK), dtype=bool))

    def step(state, inp):
        qc, kc, vc, lfc = inp
        b = jnp.cumsum(lfc, axis=2)
        diff = b[:, :, :, None, :] - b[:, :, None, :, :]
        decay = jnp.exp(jnp.where(tri[:, :, None], diff, -jnp.inf))
        attn = jnp.einsum('bhtd,bhtsd,bhsd->bhts', qc, decay, kc)
        o = attn @ vc + jnp.einsum('bhtd,bhde->bhte', qc * jnp.exp(b), state)
        b_last = b[:, :, -1:, :]
        state = (jnp.exp(b_last[:, :, 0, :, None]) * state
                 + jnp.einsum('bhsd,bhse->bhde', kc * jnp.exp(b_last - b), vc))
        return state, o

    state0 = jnp.zeros((B, A_HEADS, A_DK, A_DV), f32)
    _, o = lax.scan(step, state0, (to_chunks(qf, A_DK), to_chunks(key, A_DK),
                                   to_chunks(vf, A_DV), to_chunks(logf, A_DK)))
    o = o.transpose(1, 0, 3, 2, 4).reshape(B, S, A_HEADS, A_DV)
    o = rmsnorm(o, norm_gain)
    gate = jax.nn.silu(g.astype(f32)).reshape(B, S, A_HEADS, A_DV)
    return (o * gate).reshape(B, S, A_WIDTH).astype(g.dtype)

def gmlp_mixer(u, v, norm_gain, w_s, b_s):
    B, S, _ = u.shape
    u = jax.nn.gelu(u)
    v = rmsnorm(jax.nn.gelu(v), norm_gain)
    nb = S // B_BLOCK
    vb = v.reshape(B, nb, B_BLOCK, B_GROUPS, B_GROUP_DIM)
    w = w_s * jnp.tril(jnp.ones((B_BLOCK, B_BLOCK), w_s.dtype))
    mixed = jnp.einsum('gts,bnsgc->bntgc', w, vb) + b_s.T[None, None, :, :, None]
    return u * mixed.reshape(B, S, B_WIDTH)

def dsa_mixer(q, k, v, qi, ki, wi, positions):
    B, S, _ = q.shape
    f32 = jnp.float32
    topk = min(DSA_TOPK_MAX, S // 4)
    q = rope(q.reshape(B, S, C_HEADS, C_HEAD_DIM), positions)
    k = rope(k.reshape(B, S, C_HEADS, C_HEAD_DIM), positions)
    v = v.reshape(B, S, C_HEADS, C_HEAD_DIM)
    qi = rope(qi.reshape(B, S, IDX_HEADS, IDX_DIM), positions)
    ki = rope(ki.reshape(B, S, 1, IDX_DIM), positions)[:, :, 0].astype(f32)
    wi = wi.astype(f32) * (IDX_HEADS ** -0.5)
    nq = S // Q_BLOCK
    key_chunk = jnp.arange(S) // CHUNK
    b_idx = jnp.arange(B)[:, None, None]

    def blocks(t):
        return t.reshape(B, nq, Q_BLOCK, *t.shape[2:]).swapaxes(0, 1)

    def attend(inp):
        q_blk, qi_blk, wi_blk, blk = inp
        q_chunk = (blk * Q_BLOCK + jnp.arange(Q_BLOCK)) // CHUNK
        admissible = key_chunk[None, :] <= q_chunk[:, None]
        logits = jnp.einsum('bthd,bsd->bths', qi_blk.astype(f32), ki) * (IDX_DIM ** -0.5)
        score = jnp.einsum('bth,bths->bts', wi_blk, jax.nn.relu(logits))
        score = jnp.where(admissible[None], score, -jnp.inf)
        _, sel = lax.top_k(score, topk)
        valid = key_chunk[sel] <= q_chunk[None, :, None]
        k_sel = k[b_idx, sel]
        v_sel = v[b_idx, sel]
        s = jnp.einsum('bthd,btkhd->bthk', q_blk.astype(f32), k_sel.astype(f32)) * (C_HEAD_DIM ** -0.5)
        s = jnp.where(valid[:, :, None, :], s, -jnp.inf)
        p = jax.nn.softmax(s, axis=-1)
        return jnp.einsum('bthk,btkhd->bthd', p.astype(v.dtype), v_sel)

    out = lax.map(attend, (blocks(q), blocks(qi), blocks(wi), jnp.arange(nq)))
    return out.swapaxes(0, 1).reshape(B, S, C_WIDTH)

def peer_ffn(h, w_q, sub_keys, u_tab, v_tab):
    B, S, _ = h.shape
    f32 = jnp.float32
    qry = (h @ w_q).reshape(B, S, PEER_HEADS, 2, PEER_KEY_DIM)
    sc = jnp.einsum('bshpd,hpnd->bshpn', qry.astype(f32), sub_keys.astype(f32))
    top_v, top_i = lax.top_k(sc, PEER_TOPK)
    cand = (top_v[..., 0, :, None] + top_v[..., 1, None, :]).reshape(B, S, PEER_HEADS, PEER_TOPK * PEER_TOPK)
    cand_id = (top_i[..., 0, :, None] * PEER_N_KEYS + top_i[..., 1, None, :]).reshape(B, S, PEER_HEADS, PEER_TOPK * PEER_TOPK)
    best_v, best_pos = lax.top_k(cand, PEER_TOPK)
    expert = jnp.take_along_axis(cand_id, best_pos, axis=-1)
    gate = jax.nn.softmax(best_v, axis=-1)
    nb = S // PEER_BLOCK

    def blocks(t):
        return t.reshape(B, nb, PEER_BLOCK, *t.shape[2:]).swapaxes(0, 1)

    def experts(inp):
        h_blk, e_blk, g_blk = inp
        act = jax.nn.gelu(jnp.einsum('btd,bthkd->bthk', h_blk, u_tab[e_blk]))
        return jnp.einsum('bthk,bthkd->btd', (g_blk * act).astype(h.dtype), v_tab[e_blk])

    out = lax.map(experts, (blocks(h), blocks(expert), blocks(gate)))
    return out.swapaxes(0, 1).reshape(B, S, D_MODEL)

def setup_inputs(seed: int = 0) -> dict:
    key = jax.random.key(seed)
    ks = jax.random.split(key, 17)
    f32 = jnp.float32
    nrm = lambda k, shape, s: jax.random.normal(k, shape, f32) * s
    x = jax.random.normal(ks[0], (BATCH, SEQ, D_MODEL), f32)
    offset = jax.random.randint(ks[1], (BATCH, 1), 0, 4096, dtype=jnp.int32)
    positions = (offset + jnp.arange(SEQ, dtype=jnp.int32)[None, :]).astype(jnp.int32)
    return {
        "x": x,
        "positions": positions,
        "norm1_gain": 1.0 + nrm(ks[2], (DEPTH, D_MODEL), 0.05),
        "w_in": nrm(ks[3], (DEPTH, D_MODEL, N_IN), D_MODEL ** -0.5),
        "hgrn_lb_logits": nrm(ks[4], (DEPTH, A_HEADS * A_DK), 0.5),
        "hgrn_norm_gain": 1.0 + nrm(ks[5], (DEPTH, A_DV), 0.05),
        "gmlp_norm_gain": 1.0 + nrm(ks[6], (DEPTH, B_WIDTH), 0.05),
        "gmlp_w_s": nrm(ks[7], (DEPTH, B_GROUPS, B_BLOCK, B_BLOCK), B_BLOCK ** -0.5),
        "gmlp_b_s": nrm(ks[8], (DEPTH, B_GROUPS, B_BLOCK), 0.02),
        "w_branch": nrm(ks[9], (DEPTH, N_BRANCH, BRANCH_WIDTH, D_MODEL), BRANCH_WIDTH ** -0.5),
        "w_out": nrm(ks[10], (DEPTH, D_MODEL, D_MODEL), D_MODEL ** -0.5),
        "norm2_gain": 1.0 + nrm(ks[11], (DEPTH, D_MODEL), 0.05),
        "peer_w_q": nrm(ks[12], (DEPTH, D_MODEL, PEER_HEADS * 2 * PEER_KEY_DIM), D_MODEL ** -0.5),
        "peer_sub_keys": nrm(ks[13], (DEPTH, PEER_HEADS, 2, PEER_N_KEYS, PEER_KEY_DIM), PEER_KEY_DIM ** -0.5),
        "peer_u": nrm(ks[14], (DEPTH, PEER_N_EXPERTS, D_MODEL), D_MODEL ** -0.5),
        "peer_v": nrm(ks[15], (DEPTH, PEER_N_EXPERTS, D_MODEL), (PEER_HEADS * PEER_TOPK) ** -0.5),
        "final_gain": 1.0 + nrm(ks[16], (D_MODEL,), 0.05),
    }

def reference(x, positions, norm1_gain, w_in, hgrn_lb_logits, hgrn_norm_gain,
              gmlp_norm_gain, gmlp_w_s, gmlp_b_s, w_branch, w_out, norm2_gain,
              peer_w_q, peer_sub_keys, peer_u, peer_v, final_gain):
    B, S, _ = x.shape
    split_at = np.cumsum(IN_SIZES)[:-1].tolist()
    p = jax.nn.softmax(hgrn_lb_logits.astype(jnp.float32), axis=0)
    c = jnp.cumsum(p, axis=0)
    lb_all = c - c[0:1]
    for l in range(DEPTH):
        h = rmsnorm(x, norm1_gain[l])
        proj = h @ w_in[l]
        (aq, af, ai, ag, bu, bv, cq, ck, cv, iq, ik, iw, gl) = jnp.split(proj, split_at, axis=-1)
        y_a = hgrn2_mixer(aq, af, ai, ag, lb_all[l], hgrn_norm_gain[l])
        y_b = gmlp_mixer(bu, bv, gmlp_norm_gain[l], gmlp_w_s[l], gmlp_b_s[l])
        y_c = dsa_mixer(cq, ck, cv, iq, ik, iw, positions)
        branches = jnp.stack([y_a, y_b.astype(y_a.dtype), y_c.astype(y_a.dtype)], axis=2)
        branch_proj = jnp.einsum('bsnw,nwd->bsnd', branches, w_branch[l])
        gates = jax.nn.sigmoid(gl.reshape(B, S, N_BRANCH, D_MODEL))
        x = x + jnp.sum(gates * branch_proj, axis=2) @ w_out[l]
        x = x + peer_ffn(rmsnorm(x, norm2_gain[l]), peer_w_q[l], peer_sub_keys[l], peer_u[l], peer_v[l])
    return rmsnorm(x, final_gain)


_drawn_inputs = setup_inputs


def setup_inputs(seed=0):
    import zlib

    import numpy as np

    out = dict(_drawn_inputs(seed))
    spreads = {}
    factors = {'hgrn_lb_logits': 3.384, 'gmlp_b_s': 4.459, 'norm2_gain': 3.387}
    for name, (base, spread) in spreads.items():
        noise = np.random.default_rng([zlib.crc32(name.encode()), seed]).standard_normal(out[name].shape)
        drawn = base * np.exp(spread * noise) if base else spread * noise
        out[name] = __import__('jax').numpy.asarray(drawn.astype(out[name].dtype))
    for name, factor in factors.items():
        out[name] = (out[name] * factor).astype(out[name].dtype)
    return out
```

```python
import numpy as np
import concourse.bass as bass
from concourse import mybir
from contextlib import ExitStack

F32 = mybir.dt.float32
I32 = mybir.dt.int32
U32 = mybir.dt.uint32
U8 = mybir.dt.uint8
ALU = mybir.AluOpType
ACT = mybir.ActivationFunctionType
AX = mybir.AxisListType

P = 128
LAYERS = 2
D = 1024
S = 256
TILES = S // P
KC = D // P
HEADS = 4
W = HEADS * P
IDX_HEADS, IDX_DIM = 8, 64
BRANCHES = 3
CHUNK = 64
EPS = 1e-6
DSA_TOPK = min(256, S // 4)
PEER_HEADS, KEYS, TOPK = 8, 128, 16
HP = PEER_HEADS * 2
CAND = TOPK * TOPK
PICKS = PEER_HEADS * TOPK

BLOCKS = ["iq", "cq", "ck", "af", "aq", "ag", "ai", "cv", "bu", "bv"] + [f"gate{n}" for n in range(6)]
BRANCH_ITEM = len(BLOCKS)
OUT_ITEM = BRANCH_ITEM + BRANCHES
QRY_ITEM = OUT_ITEM + 2
KEY_ITEM = QRY_ITEM + 4
UV_ITEM = KEY_ITEM + 1
UV_ITEMS = KEYS // 2
ITEMS = UV_ITEM + UV_ITEMS
SLOTS = 3
ITEM = 4096
assert ITEMS % SLOTS == 0

HALVES = [64, 32, 16, 8, 4, 2, 1]
NLEV = len(HALVES)

NEG = -1.0e38
MARK = -3.0e38
MASKED = -1.0e30
TINY = -3.0e38

SMALL_COLS = IDX_DIM + IDX_HEADS


class Plan:

    def __init__(self, sems):
        self.sems = sems
        self.n = 0
        self.turn = {"wide": 0, "side": 4}
        self.last = [None] * 8
        self.reads = {}
        self.index, self.bank, self.read, self.before, self.base = {}, {}, {}, {}, {}
        for l in range(LAYERS):
            self.layer(l)

    def add(self, banks, l, signal, *names):
        for name in names:
            b = self.turn[banks]
            self.turn[banks] = (b + 1) % 4 + (0 if banks == "wide" else 4)
            self.reads[signal] = self.reads.get(signal, 0) + 1
            self.index[l, name], self.bank[l, name] = self.n, b
            self.read[l, name] = (self.sems[signal], self.reads[signal])
            self.before[l, name] = self.last[b]
            self.last[b] = (l, name)
            self.n += 1

    def block(self, l, signal, *names):
        for name in names:
            self.add("wide", l, signal, f"{name}0", f"{name}1")

    def layer(self, l):
        side = lambda signal, *names: self.add("side", l, signal, *names)
        wide = lambda signal, *names: self.add("wide", l, signal, *names)
        side("hT_ready", "n1.00", "n1.01", "n1.10", "n1.11")
        self.block(l, "roped", "iq")
        side("roped", "small0", "small1")
        self.block(l, "roped", "cq", "ck")
        self.block(l, "blocks_out", "af", "aq")
        side("idxT_out", "iqT0", "iqT1", "ikT")
        self.block(l, "blocks_out", "ag", "ai")
        side("relued", *[f"logit{t}{n}" for t in range(TILES) for n in range(4)])
        side("attnT_out", "cqT0", "cqT1", "ckT0", "ckT1")
        self.block(l, "blocks_out", "cv", "bu", "bv", "gate0")
        side("pairs_out", "diag0", "diag1")
        side("cross_out", "cross")
        self.block(l, "blocks_out", "gate1")
        for k in range(NLEV):
            if k in (1, 3, 5):
                self.block(l, "blocks_out", f"gate{2 + k // 2}")
            side("pairs_out", f"lev{k}0", f"lev{k}1")
        side("masked", "att00", "att01", "att10", "att11")
        side("yb_out", "mix0", "mix1")
        self.block(l, "blocks_out", "gate5")
        side("pT_out", "pT0", "pT10", "pT11")
        side("o_out", "hout0", "hout1")
        side("yc_out", "aout0", "aout1")
        side("yT_out", *[f"y{n}{t}" for n in range(BRANCHES) for t in range(TILES)])
        for n in range(BRANCHES):
            wide("gated", *[f"br{n}{half}{t}" for half in range(2) for t in range(TILES)])
        side("mT_out", "mT00", "mT01", "mT10", "mT11")
        wide("x_done", *[f"out{half}{t}" for half in range(2) for t in range(TILES)])
        side("hT_ready", "n2.00", "n2.01", "n2.10", "n2.11")
        self.block(l, "qry_out", *[f"qry{n}" for n in range(4)])
        side("sc_out", *[f"sc{t}{n}" for t in range(TILES) for n in range(4)])
        side("picksT_out", "IT", "JT", "gT")
        self.base[l, "G"] = self.n
        self.n += S
        self.base[l, "UV"] = self.n
        self.n += 2 * KEYS
        self.reads["x_done"] += 4

    def last_of(self, l, b):
        return max((index, n) for n, index in self.index.items() if n[0] == l and self.bank[n] == b)[1]

    def s_index(self, l, j):
        return self.base[l, "UV"] + (2 * j - 1 if j else 0)

    def v_index(self, l, j):
        return self.base[l, "UV"] + (2 * j + 2 if j < KEYS - 1 else 2 * KEYS - 1)

    def item_last(self, l, item):
        if item < BRANCH_ITEM:
            return self.index[l, f"{BLOCKS[item]}1"]
        if item < OUT_ITEM:
            return self.index[l, f"br{item - BRANCH_ITEM}11"]
        if item < QRY_ITEM:
            return self.index[l, f"out{item - OUT_ITEM}1"]
        if item < KEY_ITEM:
            return self.index[l, f"qry{item - QRY_ITEM}1"]
        return self.index[l, f"sc{TILES - 1}3"]


def trunk_kernel(nc, x, pos, stream, small, wsT, bsT, cols, lbl, hgain, ggain, fgain, consts, masks, out):
    ctx = ExitStack()
    with ctx:
        def sb(name, shape, dt=F32):
            return ctx.enter_context(nc.sbuf_tensor(name, shape, dt))

        def sem(name):
            return ctx.enter_context(nc.semaphore(name))

        ring = sb("ring", [P, SLOTS, ITEM])
        xs = sb("xs", [P, TILES, D])
        hT = sb("hT", [P, KC, S])
        const = sb("const", [P, 2 * P + 96])
        ident, iota, freq = const[:, 0:P], const[:, P:2 * P], const[:, 2 * P:]
        mask = sb("mask", [P, NLEV, P], U8)
        zero64 = sb("zero64", [P, CHUNK])
        trig = sb("trig", [P, 2, TILES, 96])
        gcol = sb("gcol", [P, 2 * LAYERS, KC])
        lb = sb("lb", [P, 8, HEADS])
        stat = sb("stat", [P, 96])
        picks = sb("picks", [P, 3, S])
        hot = sb("hot", [P, 8, 2, P])
        IT, JT, gT = picks[:, 0, :], picks[:, 1, :], picks[:, 2, :]
        act_ring = hot[:, 0:2, :, :].rearrange("p a b c -> p a (b c)")
        w_ring = hot[:, 2:4, :, :].rearrange("p a b c -> p a (b c)")

        arena = sb("arena", [P, KEYS * S])
        G = arena[:, :].rearrange("p (j t) -> p j t", j=KEYS)
        at = [0]

        def take(n):
            at[0] += n
            assert at[0] <= KEYS * S
            return arena[:, at[0] - n:at[0]]

        def tiles(ap):
            return ap.rearrange("p (t n) -> p t n", t=TILES)

        mixer = {n: tiles(take(W * TILES)) for n in ("iq", "ck", "cq", "ag", "ai", "cv", "bu", "bv")}
        gates = take(BRANCHES * D * TILES).rearrange("p (t n) -> p t n", t=TILES)
        xn = tiles(take(D * TILES))
        mixsum = xn
        zT = take(HEADS * S)
        qs = take(HEADS * S)
        key = take(HEADS * S)
        logf = take(HEADS * S)
        bcum = take(HEADS * S)
        lev = [take(HEADS * S) for _ in range(3)]
        pairT = take(TILES * W).rearrange("p (t h n) -> p t h n", t=TILES, h=HEADS)
        crossT = take(W).rearrange("p (h n) -> p h n", h=HEADS)
        iqT = take(4 * S).rearrange("p (b t) -> p b t", b=4)
        tmp = take(2 * W)
        cqT = take(HEADS * S).rearrange("p (h t) -> p h t", h=HEADS)
        ckT = take(HEADS * S).rearrange("p (h t) -> p h t", h=HEADS)
        ikT = take(S)
        ikn = xn[:, :, 0:P]
        wi = tiles(take(TILES * IDX_HEADS))
        score = tiles(take(TILES * S))
        top8 = take(16)
        wsmall = take(KC * SMALL_COLS).rearrange("p (c n) -> p c n", c=KC)
        ws = take(HEADS * P).rearrange("p (g t) -> p g t", g=HEADS)
        bs = take(HEADS)
        hrow = take(P)
        grow = take(W)
        prob = arena[:, 0:2 * W * TILES].rearrange("p (t h n) -> p t h n", t=TILES, h=HEADS)
        pT0 = iqT.rearrange("p b t -> p (b t)")[:, 0:W].rearrange("p (h n) -> p h n", h=HEADS)
        pT1 = tmp.rearrange("p (h b n) -> p h b n", h=HEADS, b=2)
        yT = [bcum.rearrange("p (k t) -> p k t", k=HEADS), logf.rearrange("p (k t) -> p k t", k=HEADS),
              key.rearrange("p (k t) -> p k t", k=HEADS)]
        mT = [zT.rearrange("p (k t) -> p k t", k=4), qs.rearrange("p (k t) -> p k t", k=4)]
        oh = lev[0].rearrange("p (t n) -> p t n", t=TILES)
        osq = lev[1].rearrange("p (t n) -> p t n", t=TILES)
        yc = mixer["cq"]

        at[0] = 0
        qryT = take(HP * S).rearrange("p (n t) -> p n t", n=HP)
        sc = take(TILES * HP * KEYS).rearrange("p (t n k) -> p t n k", t=TILES, n=HP)
        topv = take(TILES * HP * TOPK).rearrange("p (t n k) -> p t n k", t=TILES, n=HP)
        topi = take(TILES * HP * TOPK).rearrange("p (t n k) -> p t n k", t=TILES, n=HP)
        topf = take(TILES * HP * TOPK).rearrange("p (t n k) -> p t n k", t=TILES, n=HP)
        cand = take(TILES * PEER_HEADS * CAND).rearrange("p (t h n) -> p t h n", t=TILES, h=PEER_HEADS)
        bestv = take(TILES * PICKS).rearrange("p (t h k) -> p t h k", t=TILES, h=PEER_HEADS)
        bestp = take(TILES * PICKS).rearrange("p (t h k) -> p t h k", t=TILES, h=PEER_HEADS)
        half_pos = take(2 * PICKS).rearrange("p (b n) -> p b n", b=2)
        half_f = take(2 * PICKS).rearrange("p (b n) -> p b n", b=2)
        onehot = take(PICKS * TOPK).rearrange("p (h k a) -> p h k a", h=PEER_HEADS, k=TOPK)
        pick_ij = take(TILES * 2 * PICKS).rearrange("p (t b n) -> p t b n", t=TILES, b=2)
        gate_k = take(TILES * PICKS).rearrange("p (t h k) -> p t h k", t=TILES, h=PEER_HEADS)
        frow = arena[:, D * TILES * 8:D * TILES * 8 + D]
        xfin = arena[:, 0:D * TILES].rearrange("p (t n) -> p t n", t=TILES)

        bank = [ctx.enter_context(nc.psum_tensor(f"bank{b}", [P, 512], F32)) for b in range(8)]

        const_in = sem("const_in")
        x_in = sem("x_in")
        layer_in = sem("layer_in")
        ws_causal = sem("ws_causal")
        arrived = [sem(f"arrived{s}") for s in range(SLOTS)]
        products_done = sem("products_done")
        read = {n: sem(n) for n in (
            "hT_ready", "roped", "blocks_out", "idxT_out", "relued", "attnT_out", "pairs_out", "cross_out", "masked",
            "yb_out", "pT_out", "o_out", "yc_out", "yT_out", "gated", "mT_out", "x_done", "qry_out", "sc_out",
            "picksT_out")}
        plan = Plan(read)
        squares = sem("squares")
        meansq = sem("meansq")
        roots = sem("roots")
        xn_ready = sem("xn_ready")
        trig_in = sem("trig_in")
        trig_out = sem("trig_out")
        lb_in = sem("lb_in")
        lb_out = sem("lb_out")
        relu_used = sem("relu_used")
        soft_in = sem("soft_in")
        soft_out = sem("soft_out")
        decay_arg = sem("decay_arg")
        decay_exp = sem("decay_exp")
        decayed = sem("decayed")
        vsq = sem("vsq")
        vms = sem("vms")
        vroot = sem("vroot")
        v_normed = sem("v_normed")
        neg_max = sem("neg_max")
        probs = sem("probs")
        oms = sem("oms")
        oroot = sem("oroot")
        ya_ready = sem("ya_ready")
        mix_done = sem("mix_done")
        best_diff = sem("best_diff")
        best_exp = sem("best_exp")
        picked = sem("picked")
        hot_ready = sem("hot_ready")
        gates_out = sem("gates_out")
        gelu_done = sem("gelu_done")
        w_ready = sem("w_ready")
        dve_chain = sem("dve_chain")
        act_chain = sem("act_chain")
        final_out = sem("final_out")
        stored = sem("stored")

        block = ctx.enter_context(nc.Block())

        def full(eng, l, name):
            eng.wait_ge(products_done, plan.index[l, name] + 1)
            return bank[plan.bank[l, name]]

        def done_reading(ins, l, name):
            ins.then_inc(plan.read[l, name][0], 1)

        def wait_read(eng, l, name):
            eng.wait_ge(*plan.read[l, name])

        @block.sync
        def _(sp):
            for t in range(TILES):
                sp.dma_start(xs[:, t, :], x[t * P:(t + 1) * P, :]).then_inc(x_in, 16)

            def load(n, slot):
                sp.dma_start(ring[:, slot, :], stream[n, :, :]).then_inc(arrived[slot], 16)

            for l in range(LAYERS):
                for item in range(UV_ITEM + 1):
                    n = l * ITEMS + item
                    if item >= SLOTS:
                        sp.wait_ge(products_done, plan.item_last(l, item - SLOTS) + 1)
                    elif l > 0:
                        j = KEYS - 1 - 2 * (SLOTS - 1 - item)
                        sp.wait_ge(products_done, plan.v_index(l - 1, j) + 1)
                    load(n, n % SLOTS)
                for m in range(1, SLOTS):
                    n = l * ITEMS + UV_ITEM + m
                    sp.wait_ge(products_done, plan.item_last(l, UV_ITEM + m - SLOTS) + 1)
                    load(n, n % SLOTS)
                first = UV_ITEM + SLOTS
                assert (UV_ITEMS - SLOTS - 1) % SLOTS == 0
                with sp.Fori(0, (UV_ITEMS - SLOTS - 1) // SLOTS) as i:
                    for m in range(SLOTS):
                        n = l * ITEMS + first + m
                        sp.wait_ge(products_done, i * (4 * SLOTS) + (plan.v_index(l, 2 * m + 1) + 1))
                        sp.dma_start(ring[:, n % SLOTS, :], stream[bass.ds(i * SLOTS + n, 1), :, :].rearrange("a p n -> p (a n)"))\
                          .then_inc(arrived[n % SLOTS], 16)
                n = l * ITEMS + ITEMS - 1
                sp.wait_ge(products_done, plan.v_index(l, 2 * (UV_ITEMS - 1 - SLOTS) + 1) + 1)
                load(n, n % SLOTS)
            for t in range(TILES):
                sp.wait_ge(final_out, t + 1)
                sp.dma_start(out[t * P:(t + 1) * P, :], xfin[:, t, :]).then_inc(stored, 16)
            sp.wait_ge(stored, 16 * TILES)

        @block.gpsimd
        def _(pool):
            pool.dma_start(const[:, :], consts).then_inc(const_in, 16)
            pool.dma_start(lev[0][:, 0:NLEV * P], masks).then_inc(const_in, 16)
            pool.dma_start(gcol[:, :, :].rearrange("p n c -> p (n c)"), cols).then_inc(const_in, 16)
            pool.dma_start(lb[:, 0:2, :].rearrange("p n h -> p (n h)"), lbl).then_inc(const_in, 16)
            pool.dma_start(stat[:, 92:94].bitcast(I32), pos).then_inc(const_in, 16)
            for l in range(LAYERS):
                if l > 0:
                    pool.wait_ge(read["x_done"], 8 * l)
                pool.dma_start(wsmall.rearrange("p c n -> p (c n)"), small[l]).then_inc(layer_in, 16)
                pool.dma_start(ws.rearrange("p g t -> p (g t)"), wsT[l]).then_inc(layer_in, 16)
                pool.dma_start(bs, bsT[l]).then_inc(layer_in, 16)
                pool.dma_start(hrow, hgain[l:l + 1, :].to_broadcast([P, P])).then_inc(layer_in, 16)
                pool.dma_start(grow, ggain[l:l + 1, :].to_broadcast([P, W])).then_inc(layer_in, 16)
                pool.wait_ge(layer_in, 80 * (l + 1))
                pool.affine_select(out=ws, in_=ws, pattern=[[0, HEADS], [1, P]], compare_op=ALU.is_ge,
                                   fill=0.0, base=0, channel_multiplier=-1).then_inc(ws_causal, 1)
            pool.wait_ge(read["x_done"], 8 * LAYERS)
            pool.dma_start(frow, fgain.to_broadcast([P, D])).then_inc(layer_in, 16)

        @block.tensor
        def _(pe):
            done = [0]

            def begin(l, name):
                assert plan.index[l, name] == done[0], (name, done[0])
                done[0] += 1
                if plan.before[l, name]:
                    wait_read(pe, *plan.before[l, name])
                return bank[plan.bank[l, name]]

            def item_in(l, item):
                n = l * ITEMS + item
                pe.wait_ge(arrived[n % SLOTS], 16 * (n // SLOTS + 1))
                return ring[:, n % SLOTS, :]

            def transposes(l, name, sources):
                b = begin(l, name)
                for n, src in enumerate(sources):
                    mm = pe.transpose(b[:, n * P:(n + 1) * P], src, ident)
                mm.then_inc(products_done, 1)

            def norm_transposes(l, which):
                for t in range(TILES):
                    pe.wait_ge(xn_ready, TILES * (2 * l + which) + t + 1)
                    for half in range(2):
                        transposes(l, f"n{which + 1}.{t}{half}",
                                   [xn[:, t, (4 * half + c) * P:(4 * half + c + 1) * P] for c in range(4)])

            def block_by_token(l, name, item, width=W, weights=None):
                w = weights if weights is not None else item_in(l, item).rearrange("p (c n) -> p c n", c=KC)
                for t in range(TILES):
                    b = begin(l, f"{name}{t}")
                    for c in range(KC):
                        mm = pe.matmul(b[:, 0:width], hT[:, c, t * P:(t + 1) * P], w[:, c, :],
                                       start=(c == 0), stop=(c == KC - 1))
                    mm.then_inc(products_done, 1)

            def block_by_column(l, name, item):
                w = item_in(l, item).rearrange("p (c n) -> p c n", c=KC)
                for pair in range(2):
                    b = begin(l, f"{name}{pair}")
                    for m in range(2):
                        col = (2 * pair + m) * P
                        for c in range(KC):
                            mm = pe.matmul(b[:, m * S:(m + 1) * S], w[:, c, col:col + P], hT[:, c, :],
                                           start=(c == 0), stop=(c == KC - 1))
                    mm.then_inc(products_done, 1)

            for l in range(LAYERS):
                blk = BLOCKS.index
                if l == 0:
                    pe.wait_ge(const_in, 16 * 5)
                norm_transposes(l, 0)
                wait_read(pe, l, "n1.11")
                block_by_token(l, "iq", blk("iq"))
                pe.wait_ge(layer_in, 80 * (l + 1))
                block_by_token(l, "small", None, SMALL_COLS, wsmall)
                block_by_token(l, "cq", blk("cq"))
                block_by_token(l, "ck", blk("ck"))
                block_by_column(l, "af", blk("af"))
                block_by_column(l, "aq", blk("aq"))
                for t in range(TILES):
                    wait_read(pe, l, f"iq{t}")
                    transposes(l, f"iqT{t}", [mixer["iq"][:, t, n * P:(n + 1) * P] for n in range(4)])
                wait_read(pe, l, "small1")
                transposes(l, "ikT", [ikn[:, t, :] for t in range(TILES)])
                block_by_token(l, "ag", blk("ag"))
                block_by_token(l, "ai", blk("ai"))
                wait_read(pe, l, "ikT")
                for t in range(TILES):
                    keys = (t + 1) * P
                    for n in range(4):
                        b = begin(l, f"logit{t}{n}")
                        odd, first = n % 2, 4 * (n // 2)
                        rows = slice(IDX_DIM * odd, IDX_DIM * (odd + 1))
                        for m in range(2):
                            head = first + 2 * m + odd
                            mm = pe.matmul(b[:, m * S:m * S + keys], iqT[rows, head // 2, t * P:(t + 1) * P],
                                           ikT[rows, 0:keys], start=True, stop=True)
                        mm.then_inc(products_done, 1)
                for name in ("cq", "ck"):
                    for t in range(TILES):
                        wait_read(pe, l, f"{name}{t}")
                        transposes(l, f"{name}T{t}", [mixer[name][:, t, h * P:(h + 1) * P] for h in range(HEADS)])
                block_by_token(l, "cv", blk("cv"))
                block_by_token(l, "bu", blk("bu"))
                block_by_token(l, "bv", blk("bv"))
                block_by_token(l, "gate0", blk("gate0"))
                head = lambda ap, h, t: ap[:, h * S + t * P:h * S + (t + 1) * P]
                pe.wait_ge(decayed, (NLEV + 2) * l + 1)
                for t in range(TILES):
                    b = begin(l, f"diag{t}")
                    for h in range(HEADS):
                        mm = pe.matmul(b[:, h * P:(h + 1) * P], head(key, h, t), head(qs, h, t), start=True, stop=True)
                    mm.then_inc(products_done, 1)
                pe.wait_ge(decayed, (NLEV + 2) * l + 2)
                b = begin(l, "cross")
                for h in range(HEADS):
                    mm = pe.matmul(b[:, h * P:(h + 1) * P], head(lev[0], h, 0), head(lev[0], h, 1), start=True, stop=True)
                mm.then_inc(products_done, 1)
                block_by_token(l, "gate1", blk("gate1"))
                for k in range(NLEV):
                    if k in (1, 3, 5):
                        block_by_token(l, f"gate{2 + k // 2}", blk(f"gate{2 + k // 2}"))
                    pe.wait_ge(decayed, (NLEV + 2) * l + 3 + k)
                    for t in range(TILES):
                        b = begin(l, f"lev{k}{t}")
                        for h in range(HEADS):
                            m = head(lev[(k + 1) % 3], h, t)
                            mm = pe.matmul(b[:, h * P:(h + 1) * P], m, m, start=True, stop=True)
                        mm.then_inc(products_done, 1)
                wait_read(pe, l, "ckT1")
                for t in range(TILES):
                    keys = (t + 1) * P
                    for pair in range(2):
                        b = begin(l, f"att{t}{pair}")
                        for m in range(2):
                            h = 2 * pair + m
                            mm = pe.matmul(b[:, m * S:m * S + keys], cqT[:, h, t * P:(t + 1) * P], ckT[:, h, 0:keys],
                                           start=True, stop=True)
                        mm.then_inc(products_done, 1)
                pe.wait_ge(ws_causal, l + 1)
                for t in range(TILES):
                    pe.wait_ge(v_normed, TILES * l + t + 1)
                    b = begin(l, f"mix{t}")
                    for g in range(HEADS):
                        mm = pe.matmul(b[:, g * P:(g + 1) * P], ws[:, g, :], mixer["bv"][:, t, g * P:(g + 1) * P],
                                       start=True, stop=True)
                    mm.then_inc(products_done, 1)
                block_by_token(l, "gate5", blk("gate5"))
                pe.wait_ge(probs, 8 * l + 4)
                transposes(l, "pT0", [prob[:, 0, h, 0:P] for h in range(HEADS)])
                pe.wait_ge(probs, 8 * l + 8)
                for pair in range(2):
                    transposes(l, f"pT1{pair}", [prob[:, 1, 2 * pair + m, s * P:(s + 1) * P]
                                                 for m in range(2) for s in range(2)])
                wait_read(pe, l, f"lev{NLEV - 1}1")
                wait_read(pe, l, "cross")
                wait_read(pe, l, "ai1")
                for t in range(TILES):
                    b = begin(l, f"hout{t}")
                    for h in range(HEADS):
                        cols_h = slice(h * P, (h + 1) * P)
                        mm = pe.matmul(b[:, cols_h], pairT[:, t, h, :], mixer["ai"][:, t, cols_h],
                                       start=True, stop=(t == 0))
                        if t == 1:
                            mm = pe.matmul(b[:, cols_h], crossT[:, h, :], mixer["ai"][:, 0, cols_h],
                                           start=False, stop=True)
                    mm.then_inc(products_done, 1)
                wait_read(pe, l, "cv1")
                wait_read(pe, l, "pT11")
                for t in range(TILES):
                    b = begin(l, f"aout{t}")
                    for h in range(HEADS):
                        cols_h = slice(h * P, (h + 1) * P)
                        for s in range(t + 1):
                            lhs = pT0[:, h, :] if t == 0 else pT1[:, h, s, :]
                            mm = pe.matmul(b[:, cols_h], lhs, mixer["cv"][:, s, cols_h], start=(s == 0), stop=(s == t))
                    mm.then_inc(products_done, 1)
                ys = (mixer["ag"], mixer["bu"], yc)
                pe.wait_ge(ya_ready, l + 1)
                wait_read(pe, l, "mix1")
                wait_read(pe, l, "aout1")
                for n in range(BRANCHES):
                    for t in range(TILES):
                        transposes(l, f"y{n}{t}", [ys[n][:, t, k * P:(k + 1) * P] for k in range(4)])
                for n in range(BRANCHES):
                    w = item_in(l, BRANCH_ITEM + n).rearrange("p (k n) -> p k n", k=4)
                    wait_read(pe, l, f"y{n}1")
                    for half in range(2):
                        for t in range(TILES):
                            b = begin(l, f"br{n}{half}{t}")
                            for k in range(4):
                                mm = pe.matmul(b[:, :], yT[n][:, k, t * P:(t + 1) * P], w[:, k, half * 512:(half + 1) * 512],
                                               start=(k == 0), stop=(k == 3))
                            mm.then_inc(products_done, 1)
                for half in range(2):
                    for t in range(TILES):
                        pe.wait_ge(mix_done, 4 * l + 2 * half + t + 1)
                        transposes(l, f"mT{half}{t}", [mixsum[:, t, (4 * half + c) * P:(4 * half + c + 1) * P] for c in range(4)])
                wait_read(pe, l, "mT11")
                for half in range(2):
                    w = item_in(l, OUT_ITEM + half).rearrange("p (c n) -> p c n", c=KC)
                    for t in range(TILES):
                        b = begin(l, f"out{half}{t}")
                        for c in range(KC):
                            mm = pe.matmul(b[:, :], mT[c // 4][:, c % 4, t * P:(t + 1) * P], w[:, c, :],
                                           start=(c == 0), stop=(c == KC - 1))
                        mm.then_inc(products_done, 1)
                norm_transposes(l, 1)
                wait_read(pe, l, "n2.11")
                for n in range(4):
                    block_by_column(l, f"qry{n}", QRY_ITEM + n)
                wait_read(pe, l, "qry31")
                subkeys = item_in(l, KEY_ITEM)[:, 0:HP * KEYS].rearrange("p (n k) -> p n k", n=HP)
                for t in range(TILES):
                    for n in range(4):
                        b = begin(l, f"sc{t}{n}")
                        for m in range(4):
                            hp = 4 * n + m
                            mm = pe.matmul(b[:, m * KEYS:(m + 1) * KEYS], qryT[:, hp, t * P:(t + 1) * P], subkeys[:, hp, :],
                                           start=True, stop=True)
                        mm.then_inc(products_done, 1)
                pe.wait_ge(picked, TILES * (l + 1))
                for n, name in enumerate(("IT", "JT", "gT")):
                    src = [pick_ij[:, t, n, :] if n < 2 else gate_k[:, t, :, :].rearrange("p h k -> p (h k)")
                           for t in range(TILES)]
                    transposes(l, name, src)
                for b in range(4, 8):
                    wait_read(pe, *plan.last_of(l, b))

                def gates16(i, first=False):
                    for m in range(16):
                        if m % 4 == 0 and not first:
                            pe.wait_ge(gates_out, i * 4 + (S // 4 * l + m // 4 - 3))
                        pe.wait_ge(hot_ready, i * 16 + (S * l + m + 1))
                        pe.matmul(bank[4 + m // 4][:, (m % 4) * P:(m % 4 + 1) * P], hot[:, m % 8, 0, :],
                                  hot[:, m % 8, 1, :], start=True, stop=True).then_inc(products_done, 1)

                gates16(0, first=True)
                with pe.Fori(1, S // 16) as i:
                    gates16(i)
                done[0] += S
                uv0 = l * ITEMS + UV_ITEM

                def u_group(slot, odd, e):
                    for c in range(KC):
                        mm = pe.matmul(bank[4 + e % 2][:, 0:S], ring[:, slot, odd * D + c * P:odd * D + (c + 1) * P],
                                       hT[:, c, :], start=(c == 0), stop=(c == KC - 1))
                    mm.then_inc(products_done, 1)

                def v_group(slot, odd, e, first=False, last=False):
                    for t in range(TILES):
                        for half in range(2):
                            at_v = 2 * D + odd * D + half * 512
                            mm = pe.matmul(bank[2 * half + t][:, :], w_ring[:, e % 2, t * P:(t + 1) * P],
                                           ring[:, slot, at_v:at_v + 512], start=first, stop=last, skip_group_check=True)
                    mm.then_inc(products_done, 1)

                pe.wait_ge(arrived[uv0 % SLOTS], 16 * (uv0 // SLOTS + 1))
                pe.wait_ge(gates_out, S // 4 * (l + 1))
                u_group(uv0 % SLOTS, 0, 0)
                u_group(uv0 % SLOTS, 1, 1)
                for b in range(4):
                    wait_read(pe, *plan.last_of(l, b))
                pe.wait_ge(w_ready, KEYS * l + 1)
                v_group(uv0 % SLOTS, 0, 0, first=True)
                with pe.Fori(0, (UV_ITEMS - 1) // SLOTS) as i:
                    for m in range(2 * SLOTS):
                        n = uv0 + 1 + m // 2
                        if m % 2 == 0:
                            pe.wait_ge(arrived[n % SLOTS], i * 16 + 16 * (n // SLOTS + 1))
                        pe.wait_ge(gelu_done, i * (2 * SLOTS) + (KEYS * l + m + 1))
                        u_group(n % SLOTS, m % 2, m)
                        pe.wait_ge(w_ready, i * (2 * SLOTS) + (KEYS * l + m + 2))
                        v_group((uv0 + (m + 1) // 2) % SLOTS, (m + 1) % 2, m + 1)
                pe.wait_ge(w_ready, KEYS * (l + 1))
                v_group((uv0 + UV_ITEMS - 1) % SLOTS, 1, 1, last=True)
                done[0] += 2 * KEYS

        @block.scalar
        def _(act):
            chain = [0]

            def link(ins):
                chain[0] += 1
                ins.then_inc(act_chain, 1)
                act.wait_ge(act_chain, chain[0])

            def norm(n):
                if n > 0:
                    act.wait_ge(read["x_done"], 4 * n)
                for t in range(TILES):
                    act.activation((xn if n < 2 * LAYERS else xfin)[:, t, :], xs[:, t, :], ACT.Square,
                                   accum_out=stat[:, t:t + 1]).then_inc(squares, 1)
                act.wait_ge(meansq, n + 1)
                act.activation(stat[:, 4:6], stat[:, 2:4], ACT.Sqrt).then_inc(roots, 1)

            act.wait_ge(const_in, 16 * 5)
            act.wait_ge(x_in, 16 * TILES)
            act.wait_ge(trig_in, 1)
            act.activation(trig[:, :, :, :], trig[:, :, :, :], ACT.Sin).then_inc(trig_out, 1)
            act.wait_ge(lb_in, 1)
            act.activation(lb[:, 2:4, :], lb[:, 0:2, :], ACT.Exp).then_inc(lb_out, 1)
            act.wait_ge(lb_in, 2)
            act.activation(lb[:, 5, :], lb[:, 4, :], ACT.Ln).then_inc(lb_out, 1)

            for l in range(LAYERS):
                def out_of(name, dst, func=ACT.Copy, cols=512):
                    b = full(act, l, name)
                    src = b[:, 0:cols]
                    if len(dst.shape) == 3:
                        src = src.rearrange("p (a n) -> p a n", a=dst.shape[1])
                    elif len(dst.shape) == 4:
                        src = src.rearrange("p (a b n) -> p a b n", a=dst.shape[1], b=dst.shape[2])
                    done_reading(act.activation(dst, src, func), l, name)

                def block_out(name, dst, func=ACT.Copy):
                    for t in range(TILES):
                        out_of(f"{name}{t}", dst[:, t, :], func)

                def gate_out(n):
                    block_out(f"gate{n}", gates[:, :, n * 512:(n + 1) * 512], ACT.Sigmoid)

                norm(2 * l)
                for pair in range(2):
                    b = full(act, l, f"af{pair}")
                    act.activation(zT[:, pair * 512:(pair + 1) * 512], b[:, :], ACT.Copy)
                    done_reading(act.activation(key[:, pair * 512:(pair + 1) * 512], b[:, :], ACT.Sigmoid, scale=-1.0),
                                 l, f"af{pair}")
                for pair in range(2):
                    out_of(f"aq{pair}", qs[:, pair * 512:(pair + 1) * 512], ACT.Silu)
                for t in range(TILES):
                    out_of(f"iqT{t}", iqT[:, :, t * P:(t + 1) * P])
                out_of("ikT", ikT, cols=S)
                block_out("ag", mixer["ag"], ACT.Silu)
                block_out("ai", mixer["ai"])
                wait_read(act, l, "ck1")
                for t in range(TILES):
                    keys = (t + 1) * P
                    for n in range(4):
                        use = 8 * l + 4 * t + n
                        if n + 4 * t >= 2:
                            act.wait_ge(relu_used, use - 1)
                        b = full(act, l, f"logit{t}{n}")
                        dst = tmp[:, (n % 2) * 512:(n % 2 + 1) * 512].rearrange("p (m k) -> p m k", m=2)[:, :, 0:keys]
                        src = b[:, :].rearrange("p (m k) -> p m k", m=2)[:, :, 0:keys]
                        done_reading(act.activation(dst, src, ACT.Relu, scale=IDX_DIM ** -0.5), l, f"logit{t}{n}")
                for t in range(TILES):
                    out_of(f"cqT{t}", cqT[:, :, t * P:(t + 1) * P])
                for t in range(TILES):
                    out_of(f"ckT{t}", ckT[:, :, t * P:(t + 1) * P])
                block_out("cv", mixer["cv"])
                block_out("bu", mixer["bu"], ACT.Gelu_apprx_tanh)
                block_out("bv", mixer["bv"], ACT.Gelu_apprx_tanh)
                wait_read(act, l, "bv1")
                for t in range(TILES):
                    link(act.activation(gates[:, t, 1024:1536], mixer["bv"][:, t, :], ACT.Square,
                                        accum_out=stat[:, 8 + t:9 + t]))
                act.sem_inc(vsq, 1)
                act.wait_ge(vms, l + 1)
                act.activation(stat[:, 12:14], stat[:, 10:12], ACT.Sqrt).then_inc(vroot, 1)
                gate_out(0)
                for n in range(1 if l == 0 else 2):
                    use = 1 if l == 0 else 2 * l + n
                    act.wait_ge(soft_in, use)
                    link(act.activation(logf, logf, ACT.Exp))
                    act.activation(logf, logf, ACT.Ln, bias=1.0).then_inc(soft_out, 1)

                def decay(q):
                    act.wait_ge(decay_arg, (NLEV + 1) * l + q + 1)
                    act.activation(lev[q % 3], lev[q % 3], ACT.Exp).then_inc(decay_exp, 1)

                decay(0)
                decay(1)
                b = full(act, l, "cross")
                done_reading(act.activation(crossT, b[:, :].rearrange("p (h n) -> p h n", h=HEADS), ACT.Copy), l, "cross")
                gate_out(1)
                for k in range(NLEV):
                    if k in (1, 3, 5):
                        gate_out(2 + k // 2)
                    if k + 2 <= NLEV:
                        decay(k + 2)
                for t in range(TILES):
                    keys = (t + 1) * P
                    act.wait_ge(neg_max, TILES * l + t + 1)
                    for h in range(HEADS):
                        c = HEADS * t + h
                        act.activation(prob[:, t, h, 0:keys], prob[:, t, h, 0:keys], ACT.Exp, scale=P ** -0.5,
                                       bias=stat[:, 24 + c:25 + c], accum_out=stat[:, 32 + c:33 + c]).then_inc(probs, 1)
                gate_out(5)
                out_of("pT0", pT0)
                for pair in range(2):
                    out_of(f"pT1{pair}", pT1[:, 2 * pair:2 * pair + 2, :, :])
                for t in range(TILES):
                    out_of(f"hout{t}", oh[:, t, :])
                act.wait_ge(oms, l + 1)
                act.activation(stat[:, 56:64], stat[:, 48:56], ACT.Sqrt).then_inc(oroot, 1)
                for n in range(BRANCHES):
                    for t in range(TILES):
                        out_of(f"y{n}{t}", yT[n][:, :, t * P:(t + 1) * P])
                for half in range(2):
                    for t in range(TILES):
                        out_of(f"mT{half}{t}", mT[half][:, :, t * P:(t + 1) * P])
                norm(2 * l + 1)
                for n in range(4):
                    for pair in range(2):
                        out_of(f"qry{n}{pair}", qryT[:, 4 * n + 2 * pair:4 * n + 2 * pair + 2, :])
                for t in range(TILES):
                    for n in range(4):
                        out_of(f"sc{t}{n}", sc[:, t, 4 * n:4 * n + 4, :])
                for t in range(TILES):
                    act.wait_ge(best_diff, TILES * l + t + 1)
                    act.activation(gate_k[:, t, :, :], gate_k[:, t, :, :], ACT.Exp).then_inc(best_exp, 1)
                for name, dst in (("IT", IT), ("JT", JT), ("gT", gT)):
                    out_of(name, dst, cols=S)

                def gates16(i):
                    for m in range(4):
                        act.wait_ge(products_done, i * 16 + (plan.base[l, "G"] + 4 * m + 4))
                        act.activation(G[:, :, bass.ds(i * 16 + 4 * m, 4)], bank[4 + m][:, :].rearrange("p (t j) -> p j t", t=4),
                                       ACT.Copy).then_inc(gates_out, 1)

                with act.Fori(0, S // 16) as i:
                    gates16(i)

                def gelu(i, j, first=False):
                    act.wait_ge(products_done, i * 12 + (plan.s_index(l, j) + 1))
                    if not first:
                        act.wait_ge(w_ready, i * 6 + (KEYS * l + j - 1))
                    act.activation(act_ring[:, j % 2, :], bank[4 + j % 2][:, 0:S], ACT.Gelu_apprx_tanh).then_inc(gelu_done, 1)

                gelu(0, 0, first=True)
                gelu(0, 1, first=True)
                with act.Fori(0, (UV_ITEMS - 1) // SLOTS) as i:
                    for m in range(2 * SLOTS):
                        gelu(i, 2 + m)
            norm(2 * LAYERS)

        @block.vector
        def _(dve):
            chain = [0]

            def link(ins):
                chain[0] += 1
                ins.then_inc(dve_chain, 1)
                dve.wait_ge(dve_chain, chain[0])

            def norm(n, dst):
                dve.wait_ge(squares, TILES * (n + 1))
                dve.tensor_scalar(stat[:, 2:4], stat[:, 0:2], 1.0 / D, EPS, ALU.mult, ALU.add).then_inc(meansq, 1)
                dve.wait_ge(roots, n + 1)
                link(dve.reciprocal(stat[:, 6:8], stat[:, 4:6]))
                for t in range(TILES):
                    ins = dve.tensor_scalar(dst[:, t, :], xs[:, t, :], stat[:, 6 + t:7 + t], None, ALU.mult)
                    if n < 2 * LAYERS:
                        ins.then_inc(xn_ready, 1)
                    else:
                        link(ins)

            def gained(l, which):
                for t in range(TILES):
                    for half in range(2):
                        name = f"n{which + 1}.{t}{half}"
                        b = full(dve, l, name)
                        gain = gcol[:, 2 * l + which, 4 * half:4 * half + 4].unsqueeze(2).to_broadcast([P, 4, P])
                        done_reading(dve.tensor_tensor(hT[:, 4 * half:4 * half + 4, t * P:(t + 1) * P],
                                                       b[:, :].rearrange("p (c t) -> p c t", c=4), gain, ALU.mult), l, name)

            def rope(l, name, t, src, dst, heads, half, extra=None):
                first = 0 if half == 64 else 64
                table = lambda f: trig[:, f, t, first:first + half].unsqueeze(1)
                n = heads * half
                both = tmp[:, 0:2 * n].rearrange("p (h s d) -> p h s d", h=heads, s=2)
                cross = tmp[:, 512:512 + 2 * n].rearrange("p (h s d) -> p h s d", h=heads, s=2)
                cos = table(0).unsqueeze(1).to_broadcast([P, heads, 2, half])
                sin = table(1).to_broadcast([P, heads, half])
                dve.tensor_tensor(both, src, cos, ALU.mult)
                dve.tensor_tensor(cross[:, :, 0, :], src[:, :, 1, :], sin, ALU.mult)
                link(dve.tensor_tensor(cross[:, :, 1, :], src[:, :, 0, :], sin, ALU.mult))
                dve.tensor_tensor(dst[:, :, 0, :], both[:, :, 0, :], cross[:, :, 0, :], ALU.subtract)
                ins = dve.tensor_tensor(dst[:, :, 1, :], both[:, :, 1, :], cross[:, :, 1, :], ALU.add)
                return ins

            dve.memset(zero64[:, :], 0.0)
            dve.wait_ge(const_in, 16 * 5)
            dve.tensor_copy(mask[:, :, :].rearrange("p k n -> p (k n)"), lev[0][:, 0:NLEV * P])
            dve.wait_ge(x_in, 16 * TILES)
            posf = stat[:, 94:96]
            link(dve.tensor_copy(posf, stat[:, 92:94].bitcast(I32)))
            two_pi = 2.0 * np.pi
            c1 = 6.28125
            c2 = float(np.uint32(int(np.float32(two_pi - c1).view(np.uint32)) & 0xFFFFE000).view(np.float32))
            c3 = float(two_pi - c1 - c2)
            magic = 1.5 * 2.0 ** 23
            turns = tmp[:, 0:192].rearrange("p (t n) -> p t n", t=TILES)
            for f in range(2):
                shift = 0.25 if f == 0 else 0.0
                for t in range(TILES):
                    link(dve.tensor_scalar(trig[:, f, t, :], freq, posf[:, t:t + 1], None, ALU.mult))
                link(dve.tensor_scalar(turns, trig[:, f, :, :], 1.0 / two_pi, shift, ALU.mult, ALU.add))
                link(dve.tensor_scalar(turns, turns, magic, None, ALU.add))
                link(dve.tensor_scalar(turns, turns, -magic, None, ALU.add))
                for c in (c1, c2, c3):
                    link(dve.scalar_tensor_tensor(out=trig[:, f, :, :], in0=turns, scalar=-c, in1=trig[:, f, :, :],
                                                  op0=ALU.mult, op1=ALU.add))
                if f == 0:
                    link(dve.tensor_scalar(trig[:, f, :, :], trig[:, f, :, :], np.pi / 2, None, ALU.add))
            dve.tensor_scalar(trig[:, :, :, :], trig[:, :, :, :], 3.1415925, -3.1415925, ALU.min, ALU.max).then_inc(trig_in, 1)

            scale_a = P ** -0.5
            link(dve.tensor_tensor(lb[:, 4, :], lb[:, 0, :], lb[:, 1, :], ALU.max))
            for l in range(LAYERS):
                ins = dve.tensor_tensor(lb[:, l, :], lb[:, l, :], lb[:, 4, :], ALU.subtract)
                link(ins)
            dve.sem_inc(lb_in, 1)
            dve.wait_ge(lb_out, 1)
            link(dve.tensor_tensor(lb[:, 4, :], lb[:, 2, :], lb[:, 3, :], ALU.add))
            dve.sem_inc(lb_in, 1)
            dve.wait_ge(lb_out, 2)
            log_lb, log_rest, rest = lb[:, 6, :], lb[:, 7, :], lb[:, 4, :]
            dve.tensor_tensor(log_lb, lb[:, 1, :], lb[:, 5, :], ALU.subtract)
            link(dve.tensor_tensor(log_rest, lb[:, 0, :], lb[:, 5, :], ALU.subtract))
            link(dve.reciprocal(lb[:, 5, :], lb[:, 4, :]))
            for n in (2, 3):
                link(dve.tensor_tensor(lb[:, n, :], lb[:, n, :], lb[:, 5, :], ALU.mult))
            link(dve.tensor_tensor(rest, lb[:, 2, :], lb[:, 3, :], ALU.add))
            link(dve.tensor_tensor(rest, rest, lb[:, 2, :], ALU.subtract))
            link(dve.tensor_scalar(rest, rest, -scale_a, scale_a, ALU.mult, ALU.add))
            dve.wait_ge(trig_out, 1)

            by_head = lambda c: c.unsqueeze(2).to_broadcast([P, HEADS, S])
            heads_of = lambda ap: ap.rearrange("p (h t) -> p h t", h=HEADS)

            for l in range(LAYERS):
                norm(2 * l, xn)
                gained(l, 0)
                for t in range(TILES):
                    b = full(dve, l, f"iq{t}")
                    view = lambda ap: ap.rearrange("p (h s d) -> p h s d", h=IDX_HEADS, s=2)
                    done_reading(rope(l, "iq", t, view(b[:, :]), view(mixer["iq"][:, t, :]), IDX_HEADS, 32), l, f"iq{t}")
                    wait_read(dve, l, f"iq{t}")
                for t in range(TILES):
                    b = full(dve, l, f"small{t}")
                    view = lambda ap: ap.rearrange("p (h s d) -> p h s d", h=1, s=2)
                    link(rope(l, "ik", t, view(b[:, 0:IDX_DIM]), view(ikn[:, t, 0:IDX_DIM]), 1, 32))
                    dve.tensor_copy(ikn[:, t, IDX_DIM:2 * IDX_DIM], ikn[:, t, 0:IDX_DIM])
                    done_reading(dve.tensor_scalar(wi[:, t, :], b[:, IDX_DIM:SMALL_COLS], IDX_HEADS ** -0.5, None, ALU.mult),
                                 l, f"small{t}")
                    wait_read(dve, l, f"small{t}")
                for name in ("cq", "ck"):
                    for t in range(TILES):
                        b = full(dve, l, f"{name}{t}")
                        view = lambda ap: ap.rearrange("p (h s d) -> p h s d", h=HEADS, s=2)
                        done_reading(rope(l, name, t, view(b[:, :]), view(mixer[name][:, t, :]), HEADS, 64), l, f"{name}{t}")
                        wait_read(dve, l, f"{name}{t}")
                for t in range(TILES):
                    keys = (t + 1) * P
                    for n in range(4):
                        wait_read(dve, l, f"logit{t}{n}")
                        for m in range(2):
                            head = 4 * (n // 2) + 2 * m + n % 2
                            src = tmp[:, (n % 2) * 512 + m * S:(n % 2) * 512 + m * S + keys]
                            if n == 0 and m == 0:
                                ins = dve.tensor_scalar(score[:, t, 0:keys], src, wi[:, t, head:head + 1], None, ALU.mult)
                            else:
                                ins = dve.scalar_tensor_tensor(out=score[:, t, 0:keys], in0=src, scalar=wi[:, t, head:head + 1],
                                                               in1=score[:, t, 0:keys], op0=ALU.mult, op1=ALU.add)
                            link(ins)
                        dve.sem_inc(relu_used, 1)
                for t in range(TILES):
                    keys = (t + 1) * P
                    link(dve.memset(score[0:CHUNK, t, keys - CHUNK:keys], NEG))
                for r in range(DSA_TOPK // 8):
                    for t in range(TILES):
                        keys = (t + 1) * P
                        ins = dve.max(out=top8[:, 8 * t:8 * t + 8], in_=score[:, t, 0:keys])
                    link(ins)
                    for t in range(TILES):
                        keys = (t + 1) * P
                        ins = dve.match_replace(out=score[:, t, 0:keys], in_to_replace=top8[:, 8 * t:8 * t + 8],
                                                in_values=score[:, t, 0:keys], imm_value=MARK)
                    link(ins)
                for t in range(TILES):
                    keys = (t + 1) * P
                    link(dve.tensor_scalar(score[:, t, 0:keys], score[:, t, 0:keys], MARK, MASKED, ALU.not_equal, ALU.mult))

                dve.wait_ge(vsq, l + 1)
                dve.tensor_scalar(stat[:, 10:12], stat[:, 8:10], 1.0 / W, EPS, ALU.mult, ALU.add).then_inc(vms, 1)
                dve.wait_ge(vroot, l + 1)
                link(dve.reciprocal(stat[:, 14:16], stat[:, 12:14]))
                dve.wait_ge(layer_in, 80 * (l + 1))
                for t in range(TILES):
                    v = mixer["bv"][:, t, :]
                    dve.scalar_tensor_tensor(out=v, in0=v, scalar=stat[:, 14 + t:15 + t], in1=grow, op0=ALU.mult,
                                             op1=ALU.mult).then_inc(v_normed, 1)

                wait_read(dve, l, "aq1")
                z = zT
                dve.scalar_tensor_tensor(out=logf, in0=z, scalar=-1.0, in1=z, op0=ALU.mult, op1=ALU.min)\
                   .then_inc(soft_in, 1)
                if l == 0:
                    dve.tensor_scalar(key, key, scale_a, None, ALU.mult).then_inc(decayed, 1)
                else:
                    dve.tensor_tensor(heads_of(key), heads_of(key), by_head(rest), ALU.mult).then_inc(decayed, 1)
                dve.wait_ge(soft_out, 1 if l == 0 else 2 * l)
                link(dve.scalar_tensor_tensor(out=z, in0=z, scalar=0.0, in1=logf, op0=ALU.min, op1=ALU.subtract))
                if l > 0:
                    link(dve.tensor_tensor(heads_of(z), heads_of(z), by_head(log_rest), ALU.add))
                    link(dve.tensor_tensor(heads_of(bcum), heads_of(z), by_head(log_lb), ALU.subtract))
                    dve.scalar_tensor_tensor(out=logf, in0=bcum, scalar=-1.0, in1=bcum, op0=ALU.mult, op1=ALU.min)\
                       .then_inc(soft_in, 1)
                    link(dve.tensor_tensor(heads_of(z), heads_of(z), by_head(log_lb), ALU.max))
                    dve.wait_ge(soft_out, 2 * l + 1)
                    link(dve.tensor_tensor(z, z, logf, ALU.add))
                for c in range(HEADS * S // CHUNK):
                    ins = dve.tensor_tensor_scan(bcum[:, c * CHUNK:(c + 1) * CHUNK], z[:, c * CHUNK:(c + 1) * CHUNK],
                                                 zero64[:, :], 0.0, ALU.add, ALU.add)
                link(ins)

                def exponents(q):
                    if q >= 3:
                        full(dve, l, "cross" if q == 3 else f"lev{q - 4}1")
                    e = lev[q % 3]
                    if q == 0:
                        eh = e.rearrange("p (h c n) -> p h c n", h=HEADS, c=4)
                        bh = bcum.rearrange("p (h c n) -> p h c n", h=HEADS, c=4)
                        end = lambda c: bh[:, :, c, CHUNK - 1:CHUNK].to_broadcast([P, HEADS, CHUNK])
                        dve.tensor_tensor(eh[:, :, 1, :], end(1), bh[:, :, 1, :], ALU.subtract)
                        dve.tensor_copy(eh[:, :, 2, :], bh[:, :, 2, :])
                        dve.tensor_tensor(eh[:, :, 3, :], bh[:, :, 3, :], end(2), ALU.add)
                        link(dve.tensor_tensor(eh[:, :, 0, :], end(0), bh[:, :, 0, :], ALU.subtract))
                        dve.tensor_tensor(eh[:, :, 0, :], eh[:, :, 0, :], end(1), ALU.add).then_inc(decay_arg, 1)
                        return
                    half = HALVES[q - 1]
                    n = HEADS * S // (2 * half)
                    eb = e.rearrange("p (n s i) -> p n s i", n=n, s=2)
                    bb = bcum.rearrange("p (n s i) -> p n s i", n=n, s=2)
                    last = bb[:, :, 0, half - 1:half].to_broadcast([P, n, half])
                    dve.tensor_tensor(eb[:, :, 0, :], last, bb[:, :, 0, :], ALU.subtract)
                    if half == CHUNK:
                        dve.tensor_copy(eb[:, :, 1, :], bb[:, :, 1, :]).then_inc(decay_arg, 1)
                    else:
                        dve.tensor_tensor(eb[:, :, 1, :], bb[:, :, 1, :], last, ALU.subtract).then_inc(decay_arg, 1)

                def decayed_rows(q):
                    dve.wait_ge(decay_exp, (NLEV + 1) * l + q + 1)
                    half = P if q == 0 else HALVES[q - 1]
                    n = HEADS * S // (2 * half)
                    view = lambda ap: ap.rearrange("p (n s i) -> p n s i", n=n, s=2)
                    e = view(lev[q % 3])
                    dve.tensor_tensor(e[:, :, 0, :], e[:, :, 0, :], view(key)[:, :, 0, :], ALU.mult)
                    dve.tensor_tensor(e[:, :, 1, :], e[:, :, 1, :], view(qs)[:, :, 1, :], ALU.mult).then_inc(decayed, 1)

                def into_pairs(k):
                    wait_read(dve, l, f"lev{k - 1}1" if k else "diag1")
                    for t in range(TILES):
                        b = full(dve, l, f"lev{k}{t}")
                        m = mask[:, k, :].unsqueeze(1).to_broadcast([P, HEADS, P])
                        done_reading(dve.copy_predicated(pairT[:, t, :, :], m, b[:, :].rearrange("p (h n) -> p h n", h=HEADS)),
                                     l, f"lev{k}{t}")

                dve.wait_ge(decayed, (NLEV + 2) * l + 1)
                exponents(0)
                exponents(1)
                decayed_rows(0)
                exponents(2)
                decayed_rows(1)
                for t in range(TILES):
                    b = full(dve, l, f"diag{t}")
                    ins = dve.tensor_tensor(pairT[:, t, :, :], b[:, :].rearrange("p (h n) -> p h n", h=HEADS),
                                            ident.unsqueeze(1).to_broadcast([P, HEADS, P]), ALU.mult)
                    done_reading(ins, l, f"diag{t}")
                for k in range(NLEV):
                    if k + 3 <= NLEV:
                        exponents(k + 3)
                    if k + 2 <= NLEV:
                        decayed_rows(k + 2)
                    into_pairs(k)

                for t in range(TILES):
                    keys = (t + 1) * P
                    for pair in range(2):
                        b = full(dve, l, f"att{t}{pair}")
                        bias = score[:, t, 0:keys].unsqueeze(1).to_broadcast([P, 2, keys])
                        ins = dve.tensor_tensor(prob[:, t, 2 * pair:2 * pair + 2, 0:keys],
                                                b[:, :].rearrange("p (m k) -> p m k", m=2)[:, :, 0:keys], bias, ALU.add)
                        done_reading(ins, l, f"att{t}{pair}")
                    wait_read(dve, l, f"att{t}1")
                    link(dve.tensor_reduce(stat[:, 16 + 4 * t:20 + 4 * t], prob[:, t, :, 0:keys], AX.X, ALU.max))
                    dve.tensor_scalar(stat[:, 24 + 4 * t:28 + 4 * t], stat[:, 16 + 4 * t:20 + 4 * t], -(P ** -0.5), None,
                                      ALU.mult).then_inc(neg_max, 1)
                for t in range(TILES):
                    b = full(dve, l, f"mix{t}")
                    for g in range(HEADS):
                        u = mixer["bu"][:, t, g * P:(g + 1) * P]
                        ins = dve.scalar_tensor_tensor(out=u, in0=b[:, g * P:(g + 1) * P], scalar=bs[:, g:g + 1], in1=u,
                                                       op0=ALU.add, op1=ALU.mult)
                    done_reading(ins, l, f"mix{t}")
                dve.wait_ge(probs, 8 * (l + 1))
                link(dve.reciprocal(stat[:, 40:48], stat[:, 32:40]))
                wait_read(dve, l, "hout1")
                per_head = lambda ap: ap.rearrange("p t (h n) -> p (t h) n", h=HEADS)
                link(dve.tensor_tensor(osq, oh, oh, ALU.mult))
                link(dve.tensor_reduce(stat[:, 48:56], per_head(osq), AX.X, ALU.add))
                dve.tensor_scalar(stat[:, 48:56], stat[:, 48:56], 1.0 / P, EPS, ALU.mult, ALU.add).then_inc(oms, 1)
                for t in range(TILES):
                    b = full(dve, l, f"aout{t}")
                    r = stat[:, 40 + 4 * t:44 + 4 * t].unsqueeze(2).to_broadcast([P, HEADS, P])
                    done_reading(dve.tensor_tensor(yc[:, t, :].rearrange("p (h n) -> p h n", h=HEADS),
                                                   b[:, :].rearrange("p (h n) -> p h n", h=HEADS), r, ALU.mult), l, f"aout{t}")
                dve.wait_ge(oroot, l + 1)
                link(dve.reciprocal(stat[:, 64:72], stat[:, 56:64]))
                link(dve.tensor_tensor(per_head(oh), per_head(oh), stat[:, 64:72].unsqueeze(2).to_broadcast([P, 8, P]), ALU.mult))
                link(dve.tensor_tensor(per_head(oh), per_head(oh), hrow.unsqueeze(1).to_broadcast([P, 8, P]), ALU.mult))
                dve.tensor_tensor(mixer["ag"], mixer["ag"], oh, ALU.mult).then_inc(ya_ready, 1)

                for n in range(BRANCHES):
                    for half in range(2):
                        for t in range(TILES):
                            name = f"br{n}{half}{t}"
                            b = full(dve, l, name)
                            gate = gates[:, t, n * D + half * 512:n * D + (half + 1) * 512]
                            part = mixsum[:, t, half * 512:(half + 1) * 512]
                            dst = part if n == 0 else gate
                            done_reading(dve.tensor_tensor(dst, b[:, :], gate, ALU.mult), l, name)
                            if n > 0:
                                wait_read(dve, l, name)
                                ins = dve.tensor_tensor(part, part, gate, ALU.add)
                                if n == BRANCHES - 1:
                                    ins.then_inc(mix_done, 1)
                                else:
                                    link(ins)
                for half in range(2):
                    for t in range(TILES):
                        name = f"out{half}{t}"
                        b = full(dve, l, name)
                        part = xs[:, t, half * 512:(half + 1) * 512]
                        done_reading(dve.tensor_tensor(part, part, b[:, :], ALU.add), l, name)

                norm(2 * l + 1, xn)
                gained(l, 1)

                for t in range(TILES):
                    wait_read(dve, l, f"sc{t}3")
                    for n in range(HP):
                        ins = dve.max(out=topv[:, t, n, 0:8], in_=sc[:, t, n, :])
                    link(ins)
                    for n in range(HP):
                        ins = dve.max_index(out=topi[:, t, n, 0:8].bitcast(U32), in_max=topv[:, t, n, 0:8], in_values=sc[:, t, n, :])
                    link(ins)
                    for n in range(HP):
                        ins = dve.match_replace(out=sc[:, t, n, :], in_to_replace=topv[:, t, n, 0:8], in_values=sc[:, t, n, :],
                                                imm_value=TINY)
                    link(ins)
                    for n in range(HP):
                        ins = dve.max(out=topv[:, t, n, 8:16], in_=sc[:, t, n, :])
                    link(ins)
                    for n in range(HP):
                        ins = dve.max_index(out=topi[:, t, n, 8:16].bitcast(U32), in_max=topv[:, t, n, 8:16], in_values=sc[:, t, n, :])
                    link(ins)
                    halves = topv[:, t, :, :].rearrange("p (h s) k -> p h s k", s=2)
                    for h in range(PEER_HEADS):
                        ins = dve.tensor_tensor(cand[:, t, h, :].rearrange("p (a b) -> p a b", a=TOPK),
                                                halves[:, h, 0, :].unsqueeze(2).to_broadcast([P, TOPK, TOPK]),
                                                halves[:, h, 1, :].unsqueeze(1).to_broadcast([P, TOPK, TOPK]), ALU.add)
                    link(ins)
                    for h in range(PEER_HEADS):
                        ins = dve.max(out=bestv[:, t, h, 0:8], in_=cand[:, t, h, :])
                    link(ins)
                    for h in range(PEER_HEADS):
                        ins = dve.max_index(out=bestp[:, t, h, 0:8].bitcast(U32), in_max=bestv[:, t, h, 0:8], in_values=cand[:, t, h, :])
                    link(ins)
                    for h in range(PEER_HEADS):
                        ins = dve.match_replace(out=cand[:, t, h, :], in_to_replace=bestv[:, t, h, 0:8], in_values=cand[:, t, h, :],
                                                imm_value=TINY)
                    link(ins)
                    for h in range(PEER_HEADS):
                        ins = dve.max(out=bestv[:, t, h, 8:16], in_=cand[:, t, h, :])
                    link(ins)
                    dve.tensor_tensor(gate_k[:, t, :, :], bestv[:, t, :, :], bestv[:, t, :, 0:1].to_broadcast([P, PEER_HEADS, TOPK]),
                                      ALU.subtract).then_inc(best_diff, 1)
                    for h in range(PEER_HEADS):
                        ins = dve.max_index(out=bestp[:, t, h, 8:16].bitcast(U32), in_max=bestv[:, t, h, 8:16], in_values=cand[:, t, h, :])
                    link(ins)
                    flat = bestp[:, t, :, :].rearrange("p h k -> p (h k)").bitcast(U32)
                    dve.tensor_scalar(half_pos[:, 0, :].bitcast(U32), flat, 4, None, ALU.logical_shift_right)
                    link(dve.tensor_scalar(half_pos[:, 1, :].bitcast(U32), flat, 15, None, ALU.bitwise_and))
                    dve.tensor_copy(half_f, half_pos.bitcast(U32))
                    link(dve.tensor_copy(topf[:, t, :, :], topi[:, t, :, :].bitcast(U32)))
                    numbers = topf[:, t, :, :].rearrange("p (h s) k -> p h s k", s=2)
                    for s in range(2):
                        place = half_f[:, s, :].rearrange("p (h k) -> p h k", h=PEER_HEADS).unsqueeze(3)\
                                               .to_broadcast([P, PEER_HEADS, TOPK, TOPK])
                        steps = iota[:, 0:TOPK].unsqueeze(1).unsqueeze(1).to_broadcast([P, PEER_HEADS, TOPK, TOPK])
                        number = numbers[:, :, s, :].unsqueeze(2).to_broadcast([P, PEER_HEADS, TOPK, TOPK])
                        link(dve.tensor_tensor(onehot, place, steps, ALU.is_equal))
                        link(dve.tensor_tensor(onehot, onehot, number, ALU.mult))
                        link(dve.tensor_reduce(pick_ij[:, t, s, :].rearrange("p (h k) -> p h k", h=PEER_HEADS), onehot, AX.X, ALU.add))
                    dve.wait_ge(best_exp, TILES * l + t + 1)
                    link(dve.tensor_reduce(stat[:, 72:80], gate_k[:, t, :, :], AX.X, ALU.add))
                    link(dve.reciprocal(stat[:, 80:88], stat[:, 72:80]))
                    dve.tensor_tensor(gate_k[:, t, :, :], gate_k[:, t, :, :],
                                      stat[:, 80:88].unsqueeze(2).to_broadcast([P, PEER_HEADS, TOPK]), ALU.mult).then_inc(picked, 1)

                wait_read(dve, l, "gT")

                def one_hots(i, m, first=False):
                    if not first:
                        dve.wait_ge(products_done, i * 8 + (plan.base[l, "G"] + m - 7))
                    tok = lambda ap: ap[:, bass.ds(i * 8 + m, 1)]
                    dve.tensor_scalar(hot[:, m, 0, :], iota, tok(IT), tok(gT), ALU.is_equal, ALU.mult)
                    dve.tensor_scalar(hot[:, m, 1, :], iota, tok(JT), None, ALU.is_equal).then_inc(hot_ready, 1)

                for m in range(8):
                    one_hots(0, m, first=True)
                with dve.Fori(1, S // 8) as i:
                    for m in range(8):
                        one_hots(i, m)

                dve.wait_ge(gates_out, S // 4 * (l + 1))

                def gated(i, j, first=False):
                    dve.wait_ge(gelu_done, i * 6 + (KEYS * l + j + 1))
                    if not first:
                        dve.wait_ge(products_done, i * 12 + (plan.v_index(l, j - 2) + 1))
                    dve.tensor_tensor(w_ring[:, j % 2, :], act_ring[:, j % 2, :],
                                      G[:, bass.ds(i * 6 + j, 1), :].rearrange("p a t -> p (a t)"), ALU.mult).then_inc(w_ready, 1)

                gated(0, 0, first=True)
                gated(0, 1, first=True)
                with dve.Fori(0, (UV_ITEMS - 1) // SLOTS) as i:
                    for m in range(2 * SLOTS):
                        gated(i, 2 + m)
                dve.wait_ge(products_done, plan.v_index(l, KEYS - 1) + 1)
                for half in range(2):
                    for t in range(TILES):
                        part = xs[:, t, half * 512:(half + 1) * 512]
                        dve.tensor_tensor(part, part, bank[2 * half + t][:, :], ALU.add).then_inc(read["x_done"], 1)

            norm(2 * LAYERS, xfin)
            dve.wait_ge(layer_in, 80 * LAYERS + 16)
            for t in range(TILES):
                dve.tensor_tensor(xfin[:, t, :], xfin[:, t, :], frow, ALU.mult).then_inc(final_out, 1)


def _blocks_of_w_in(w_in):
    names = ["aq", "af", "ai", "ag", "bu", "bv", "cq", "ck", "cv", "iq"]
    blocks = {n: w_in[:, :, k * W:(k + 1) * W] for k, n in enumerate(names)}
    at = len(names) * W
    blocks["small"] = w_in[:, :, at:at + SMALL_COLS]
    for n in range(6):
        blocks[f"gate{n}"] = w_in[:, :, at + SMALL_COLS + n * W:at + SMALL_COLS + (n + 1) * W]
    return blocks


def _rows_to_partitions(w):
    layers, rows, columns = w.shape
    return w.reshape(layers, rows // P, P, columns).transpose(0, 2, 1, 3).reshape(layers, P, -1)


def kernel(**inputs):
    import numpy as _np
    import concourse.bacc as _bacc
    from concourse import mybir as _mybir
    from concourse.bass_utils import run_bass_kernel_spmd as _run

    a = {n: _np.asarray(v) for n, v in inputs.items()}
    blocks = _blocks_of_w_in(a["w_in"])
    stream = _np.zeros((LAYERS, ITEMS, P, ITEM), _np.float32)
    for n, name in enumerate(BLOCKS):
        stream[:, n] = _rows_to_partitions(blocks[name])
    for n in range(BRANCHES):
        stream[:, BRANCH_ITEM + n] = _rows_to_partitions(a["w_branch"][:, n])
    for n in range(2):
        stream[:, OUT_ITEM + n] = _rows_to_partitions(a["w_out"][:, :, n * W:(n + 1) * W])
    for n in range(4):
        stream[:, QRY_ITEM + n] = _rows_to_partitions(a["peer_w_q"][:, :, n * W:(n + 1) * W])
    stream[:, KEY_ITEM, :, 0:HP * KEYS] = a["peer_sub_keys"].transpose(0, 4, 1, 2, 3).reshape(LAYERS, P, HP * KEYS)
    uv = stream[:, UV_ITEM:].reshape(LAYERS, UV_ITEMS, P, 4, D)
    for l in range(LAYERS):
        u = a["peer_u"][l].reshape(KEYS, UV_ITEMS, 2, KC, P).transpose(1, 4, 2, 3, 0)
        uv[l, :, :, 0:2] = u.reshape(UV_ITEMS, P, 2, D)
        uv[l, :, :, 2:4] = a["peer_v"][l].reshape(KEYS, UV_ITEMS, 2, D).transpose(1, 0, 2, 3)

    half_c, half_i = P // 2, IDX_DIM // 2
    inv = lambda half: (10000.0 ** (-_np.arange(half, dtype=_np.float32) / _np.float32(half)).astype(_np.float64))\
        .astype(_np.float32)
    consts = _np.zeros((P, 2 * P + 96), _np.float32)
    consts[:, 0:P] = _np.eye(P)
    consts[:, P:2 * P] = _np.arange(P)
    consts[:, 2 * P:] = _np.concatenate([inv(half_c), inv(half_i)])
    s, t = _np.meshgrid(_np.arange(P), _np.arange(P), indexing="ij")
    masks = _np.stack([(s // (2 * h) == t // (2 * h)) & (s % (2 * h) < h) & (t % (2 * h) >= h) for h in HALVES], 1)

    gains = _np.stack([a["norm1_gain"], a["norm2_gain"]], 1)
    arrays = {
        "x": a["x"].reshape(S, D),
        "pos": a["positions"].reshape(TILES, P).T,
        "stream": stream.reshape(LAYERS * ITEMS, P, ITEM),
        "small": _rows_to_partitions(blocks["small"]),
        "wsT": a["gmlp_w_s"].transpose(0, 3, 1, 2).reshape(LAYERS, P, HEADS * P),
        "bsT": a["gmlp_b_s"].transpose(0, 2, 1),
        "cols": gains.reshape(2 * LAYERS, KC, P).transpose(2, 0, 1).reshape(P, 2 * LAYERS * KC),
        "lbl": a["hgrn_lb_logits"].reshape(LAYERS, HEADS, P).transpose(2, 0, 1).reshape(P, LAYERS * HEADS),
        "hgain": a["hgrn_norm_gain"],
        "ggain": a["gmlp_norm_gain"],
        "fgain": a["final_gain"].reshape(1, D),
        "consts": consts,
        "masks": masks.astype(_np.float32).reshape(P, NLEV * P),
    }
    nc = _bacc.Bacc("TRN2", target_bir_lowering=False, num_devices=1)
    args = []
    for name, v in arrays.items():
        arrays[name] = v = _np.ascontiguousarray(v)
        args.append(nc.dram_tensor(f"{name}_dram", v.shape, _mybir.dt.from_np(v.dtype), kind="ExternalInput").ap())
    args.append(nc.dram_tensor("out_dram", (S, D), F32, kind="ExternalOutput").ap())
    trunk_kernel(nc, *args)
    r = _run(nc, [{f"{n}_dram": v for n, v in arrays.items()}], core_ids=[0])
    return r.results[0]["out_dram"].reshape(1, S, D)
```

```python
import numpy as np
import concourse.bass as bass
from concourse import mybir
from contextlib import ExitStack

F32 = mybir.dt.float32
F32R = mybir.dt.float32r
I32 = mybir.dt.int32
U32 = mybir.dt.uint32
U8 = mybir.dt.uint8
ALU = mybir.AluOpType
ACT = mybir.ActivationFunctionType
AX = mybir.AxisListType

P = 128
LAYERS = 2
D = 1024
S = 256
TILES = S // P
KC = D // P
HEADS = 4
W = HEADS * P
IDX_HEADS, IDX_DIM = 8, 64
BRANCHES = 3
CHUNK = 64
EPS = 1e-6
DSA_TOPK = min(256, S // 4)
PEER_HEADS, KEYS, TOPK = 8, 128, 16
HP = PEER_HEADS * 2
CAND = TOPK * TOPK
PICKS = PEER_HEADS * TOPK

BLOCKS = ["iq", "cq", "ck", "af", "aq", "ag", "ai", "cv", "bu", "bv"] + [f"gate{n}" for n in range(6)]
BY_COLUMN = ("af", "aq", "qry0", "qry1", "qry2", "qry3")
HEAD = BLOCKS + [f"br{n}" for n in range(BRANCHES)] + ["out0", "out1"] + [f"qry{n}" for n in range(4)]
FIRST = {name: 2 * n for n, name in enumerate(HEAD)}
KEY_ITEM = 2 * len(HEAD)
U_ITEM = KEY_ITEM + 1
V_ITEM = U_ITEM + KEYS // 2
ITEMS = V_ITEM + KEYS // 2
SLOTS = 3
ITEM = 2048

SPLIT = BLOCKS + [f"qry{n}" for n in range(4)]
UNIT = {name: 4 * n for n, name in enumerate(SPLIT)}
U_UNIT = 4 * len(SPLIT)
V_UNIT = U_UNIT + KEYS
UNITS = V_UNIT + KEYS
PARTS = 3
assert UNITS % PARTS == 0

TURN = 6
AHEAD = 54
GROUPS = S // 4
GATED = KEYS - AHEAD
assert AHEAD % TURN == 0 and GATED > GROUPS

HALVES = [64, 32, 16, 8, 4, 2, 1]
NLEV = len(HALVES)

NEG = -1.0e38
MARK = -3.0e38
MASKED = -1.0e30
TINY = -3.0e38

SMALL_COLS = IDX_DIM + IDX_HEADS


class Plan:

    def __init__(self, sems):
        self.sems = sems
        self.n = 0
        self.turn = {"wide": 0, "side": 0, "gates": 0}
        self.last = [None] * 8
        self.reads = {}
        self.index, self.bank, self.read, self.before, self.base = {}, {}, {}, {}, {}
        for l in range(LAYERS):
            self.layer(l)

    def add(self, banks, l, signal, *names):
        for name in names:
            those = {"wide": (0, 1, 2, 3), "side": (4, 5, 6, 7), "gates": (4, 5)}[banks]
            b = those[self.turn[banks] % len(those)]
            self.turn[banks] += 1
            self.reads[signal] = self.reads.get(signal, 0) + 1
            self.index[l, name], self.bank[l, name] = self.n, b
            self.read[l, name] = (self.sems[signal], self.reads[signal])
            self.before[l, name] = self.last[b]
            self.last[b] = (l, name)
            self.n += 1

    def block(self, l, signal, *names):
        for name in names:
            split, by_column = name in SPLIT, name in BY_COLUMN
            steps = range(3) if split else range(1)
            if by_column:
                for q in range(2):
                    self.index[l, f"{name}.{2 * q}"] = self.n
                    self.n += 1
                    self.add("wide", l, signal, f"{name}{q}")
            else:
                for step in steps:
                    self.index[l, f"{name}.{step}"] = self.n
                    self.n += 1
                self.add("wide", l, signal, f"{name}0", f"{name}1")

    def layer(self, l):
        side = lambda signal, *names: self.add("side", l, signal, *names)
        wide = lambda signal, *names: self.add("wide", l, signal, *names)
        side("hT_ready", "n1.00", "n1.01", "n1.10", "n1.11")
        self.block(l, "roped", "iq")
        side("roped", "small0", "small1")
        self.block(l, "roped", "cq", "ck")
        self.block(l, "blocks_out", "af", "aq")
        side("idxT_out", "iqT0", "iqT1", "ikT")
        self.block(l, "blocks_out", "ag", "ai")
        side("relued", *[f"logit{t}{n}" for t in range(TILES) for n in range(4)])
        side("attnT_out", "cqT0", "cqT1", "ckT0", "ckT1")
        self.block(l, "blocks_out", "cv", "bu", "bv", "gate0", "gate1")
        side("pairs_out", "diag0", "diag1")
        side("cross_out", "cross")
        for k in range(NLEV):
            if k in (1, 3, 5):
                self.block(l, "blocks_out", f"gate{2 + k // 2}")
            side("pairs_out", f"lev{k}0", f"lev{k}1")
        side("masked", "att00", "att01", "att10", "att11")
        side("yb_out", "mix0", "mix1")
        side("o_out", "hout0", "hout1")
        self.block(l, "blocks_out", "gate5")
        side("pT_out", "pT0", "pT10", "pT11")
        side("yc_out", "aout0", "aout1")
        side("yT_out", *[f"y{n}{t}" for n in range(BRANCHES) for t in range(TILES)])
        for n in range(BRANCHES):
            wide("gated", *[f"br{n}{half}{t}" for half in range(2) for t in range(TILES)])
        side("mT_out", "mT00", "mT01", "mT10", "mT11")
        self.block(l, "x_done", "out0", "out1")
        side("hT_ready", "n2.00", "n2.01", "n2.10", "n2.11")
        self.block(l, "qry_out", *[f"qry{n}" for n in range(4)])
        self.base[l, "seed"] = self.n
        self.n += 4
        side("sc_out", *[f"sc{t}{n}" for t in range(TILES) for n in range(4)])
        self.base[l, "U"] = self.n
        self.n += AHEAD
        self.add("gates", l, "picksT_out", "IT", "JT", "gT")
        self.base[l, "G"] = self.n
        self.n += 5 * GROUPS
        self.base[l, "T"] = self.n
        self.n += GATED - GROUPS
        self.base[l, "V"] = self.n
        self.n += KEYS
        self.reads["x_done"] += 4

    def last_of(self, l, b):
        return max((index, n) for n, index in self.index.items() if n[0] == l and self.bank.get(n) == b)[1]

    def token_index(self, l, g, m):
        return self.base[l, "G"] + 5 * g + m

    def u_index(self, l, j):
        if j < AHEAD:
            return self.base[l, "U"] + j
        if j < AHEAD + GROUPS:
            return self.base[l, "G"] + 5 * (j - AHEAD) + 4
        return self.base[l, "T"] + j - AHEAD - GROUPS

    def v_index(self, l, j):
        return self.base[l, "V"] + j

    def item_last(self, l, item):
        if item == KEY_ITEM:
            return self.index[l, f"sc{TILES - 1}3"]
        name, q = HEAD[item // 2], item % 2
        if name[:2] == "br":
            return self.index[l, f"{name}{q}1"]
        return self.index[l, f"{name}1" if q else f"{name}.0"]

    def unit_step(self, l, k):
        if k >= V_UNIT:
            return self.v_index(l, k - V_UNIT)
        if k >= U_UNIT:
            return self.u_index(l, k - U_UNIT)
        name, u = SPLIT[k // 4], k % 4
        if name in BY_COLUMN:
            return self.index[l, f"{name}{u // 2}" if u % 2 else f"{name}.{u}"]
        return self.index[l, f"{name}1" if u == 3 else f"{name}.{u}"]


def trunk_kernel(nc, x, pos, stream, small, wsT, bsT, cols, lbl, hgain, ggain, fgain, consts, masks, out):
    ctx = ExitStack()
    with ctx:
        def sb(name, shape, dt=F32):
            return ctx.enter_context(nc.sbuf_tensor(name, shape, dt))

        def sem(name):
            return ctx.enter_context(nc.semaphore(name))

        ring = sb("ring", [P, SLOTS, ITEM])
        upper = sb("upper", [P, PARTS, D], F32R)
        lower = sb("lower", [P, PARTS, D], F32R)
        hT_upper = sb("hT_upper", [P, KC * S], F32R)
        hT_lower = sb("hT_lower", [P, KC * S], F32R)
        w_upper = sb("w_upper", [P, 2, S], F32R)
        w_lower = sb("w_lower", [P, 2, S], F32R)
        const = sb("const", [P, 2 * P + 96])
        ident, iota, freq = const[:, 0:P], const[:, P:2 * P], const[:, 2 * P:]
        mask = sb("mask", [P, NLEV, P], U8)
        zero64 = sb("zero64", [P, CHUNK])
        trig = sb("trig", [P, 2, TILES, 96])
        gcol = sb("gcol", [P, 2 * LAYERS, KC])
        lb = sb("lb", [P, 8, HEADS])
        stat = sb("stat", [P, 96])
        picks = sb("picks", [P, 3, S])
        hot = sb("hot", [P, 2, 4, P])
        IT, JT, gT = picks[:, 0, :], picks[:, 1, :], picks[:, 2, :]

        arena = sb("arena", [P, KEYS * S])
        G = arena[:, :].rearrange("p (j t) -> p j t", j=KEYS)
        at = [0]

        def take(n):
            at[0] += n
            assert at[0] <= KEYS * S
            return arena[:, at[0] - n:at[0]]

        def tiles(ap):
            return ap.rearrange("p (t n) -> p t n", t=TILES)

        mixer = {n: tiles(take(W * TILES)) for n in ("iq", "ck", "cq", "ag", "ai", "cv", "bu", "bv")}
        gates = take(BRANCHES * D * TILES).rearrange("p (t n) -> p t n", t=TILES)
        xn = tiles(take(D * TILES))
        mixsum = xn
        zT = take(HEADS * S)
        qs = take(HEADS * S)
        key = take(HEADS * S)
        logf = take(HEADS * S)
        bcum = take(HEADS * S)
        lev = [take(HEADS * S), zT, logf]
        pairs = take(TILES * W)
        pairT = pairs.rearrange("p (t h n) -> p t h n", t=TILES, h=HEADS)
        iqT = pairs.rearrange("p (b t) -> p b t", b=4)
        crossT = take(W).rearrange("p (h n) -> p h n", h=HEADS)
        tmp = take(2 * W)
        cqT = take(HEADS * S).rearrange("p (h t) -> p h t", h=HEADS)
        ckT = take(HEADS * S).rearrange("p (h t) -> p h t", h=HEADS)
        ikT = take(S)
        ikn = xn[:, :, 0:P]
        wi = tiles(take(TILES * IDX_HEADS))
        score = tiles(take(TILES * S))
        top8 = take(16)
        wsmall = hot[:, :, :, :].rearrange("p a b c -> p (a b c)")[:, 0:KC * SMALL_COLS].rearrange("p (c n) -> p c n", c=KC)
        ws = picks[:, :, :].rearrange("p a t -> p (a t)")[:, 0:HEADS * P].rearrange("p (g t) -> p g t", g=HEADS)
        bs = take(HEADS)
        hrow = take(P)
        grow = take(W)
        xs = tiles(take(TILES * D))
        hT = take(KC * S).rearrange("p (c t) -> p c t", c=KC)
        prob = arena[:, 0:2 * W * TILES].rearrange("p (t h n) -> p t h n", t=TILES, h=HEADS)
        pT0 = cqT.rearrange("p h t -> p (h t)")[:, 0:W].rearrange("p (h n) -> p h n", h=HEADS)
        pT1 = tmp.rearrange("p (h b n) -> p h b n", h=HEADS, b=2)
        yT = [bcum.rearrange("p (k t) -> p k t", k=HEADS), logf.rearrange("p (k t) -> p k t", k=HEADS),
              key.rearrange("p (k t) -> p k t", k=HEADS)]
        mT = [zT.rearrange("p (k t) -> p k t", k=4), qs.rearrange("p (k t) -> p k t", k=4)]
        oh = lev[0].rearrange("p (t n) -> p t n", t=TILES)
        osq = lev[1].rearrange("p (t n) -> p t n", t=TILES)
        yc = mixer["cq"]

        at[0] = AHEAD * S
        qryT = take(HP * S).rearrange("p (n t) -> p n t", n=HP)
        sc = take(TILES * HP * KEYS).rearrange("p (t n k) -> p t n k", t=TILES, n=HP)
        topv = take(TILES * HP * TOPK).rearrange("p (t n k) -> p t n k", t=TILES, n=HP)
        topi = take(TILES * HP * TOPK).rearrange("p (t n k) -> p t n k", t=TILES, n=HP)
        topf = take(TILES * HP * TOPK).rearrange("p (t n k) -> p t n k", t=TILES, n=HP)
        cand = take(TILES * PEER_HEADS * CAND).rearrange("p (t h n) -> p t h n", t=TILES, h=PEER_HEADS)
        bestv = take(TILES * PICKS).rearrange("p (t h k) -> p t h k", t=TILES, h=PEER_HEADS)
        bestp = take(TILES * PICKS).rearrange("p (t h k) -> p t h k", t=TILES, h=PEER_HEADS)
        half_pos = take(2 * PICKS).rearrange("p (b n) -> p b n", b=2)
        half_f = take(2 * PICKS).rearrange("p (b n) -> p b n", b=2)
        assert AHEAD * S + 2 * HP * S <= KEYS * S - TILES * D - KC * S
        flat_hot = hot[:, :, :, :].rearrange("p a b c -> p (a b c)")
        pick_ij = flat_hot[:, 0:TILES * 2 * PICKS].rearrange("p (t b n) -> p t b n", t=TILES, b=2)
        gate_k = flat_hot[:, TILES * 2 * PICKS:TILES * 3 * PICKS].rearrange("p (t h k) -> p t h k", t=TILES, h=PEER_HEADS)
        frow = tmp[:, 0:D]
        xfin = xn

        bank = [ctx.enter_context(nc.psum_tensor(f"bank{b}", [P, 512], F32)) for b in range(8)]

        const_in = sem("const_in")
        x_in = sem("x_in")
        layer_in = sem("layer_in")
        ws_causal = sem("ws_causal")
        arrived = [sem(f"arrived{s}") for s in range(SLOTS)]
        products_done = sem("products_done")
        read = {n: sem(n) for n in (
            "hT_ready", "roped", "blocks_out", "idxT_out", "relued", "attnT_out", "pairs_out", "cross_out", "masked",
            "yb_out", "pT_out", "o_out", "yc_out", "yT_out", "gated", "mT_out", "x_done", "qry_out", "sc_out",
            "picksT_out")}
        plan = Plan(read)
        squares = sem("squares")
        meansq = sem("meansq")
        roots = sem("roots")
        xn_ready = sem("xn_ready")
        trig_in = sem("trig_in")
        trig_out = sem("trig_out")
        lb_in = sem("lb_in")
        lb_out = sem("lb_out")
        relu_used = sem("relu_used")
        soft_in = sem("soft_in")
        soft_out = sem("soft_out")
        decay_arg = sem("decay_arg")
        decay_exp = sem("decay_exp")
        decayed = sem("decayed")
        vsq = sem("vsq")
        vms = sem("vms")
        vroot = sem("vroot")
        v_normed = sem("v_normed")
        neg_max = sem("neg_max")
        probs = sem("probs")
        oms = sem("oms")
        oroot = sem("oroot")
        ya_ready = sem("ya_ready")
        mix_done = sem("mix_done")
        best_diff = sem("best_diff")
        best_exp = sem("best_exp")
        hT_split = sem("hT_split")
        picked = sem("picked")
        hot_ready = sem("hot_ready")
        gates_in = sem("gates_in")
        upper_ready = sem("upper_ready")
        lower_ready = sem("lower_ready")
        v_ready = sem("v_ready")
        gelu_done = sem("gelu_done")
        gelu_in = sem("gelu_in")
        w_upper_ready = sem("w_upper_ready")
        w_ready = sem("w_ready")
        dve_chain = sem("dve_chain")
        act_chain = sem("act_chain")
        final_out = sem("final_out")
        stored = sem("stored")

        block = ctx.enter_context(nc.Block())

        def full(eng, l, name):
            eng.wait_ge(products_done, plan.index[l, name] + 1)
            return bank[plan.bank[l, name]]

        def columns(eng, start, end, body, straight=0, tail=0):
            for n in range(start, start + straight):
                body(0, n)
            first = start + straight
            turns = (end - tail - first) // TURN
            with eng.Fori(0, turns) as i:
                for n in range(first, first + TURN):
                    body(i, n)
            for n in range(first + TURN * turns, end):
                body(0, n)

        def done_reading(ins, l, name):
            ins.then_inc(plan.read[l, name][0], 1)

        def wait_read(eng, l, name):
            eng.wait_ge(*plan.read[l, name])

        @block.sync
        def _(sp):
            for t in range(TILES):
                sp.dma_start(xs[:, t, :], x[t * P:(t + 1) * P, :]).then_inc(x_in, 16)

            def load(l, item, wait, i=None):
                if wait:
                    sp.wait_ge(*wait)
                n = l * ITEMS + item
                src = stream[n, :, :] if i is None else \
                    stream[bass.ds(i * SLOTS + n, 1), :, :].rearrange("a p n -> p (a n)")
                sp.dma_start(ring[:, n % SLOTS, :], src).then_inc(arrived[n % SLOTS], 16)

            def split_done(l, item, i=None):
                if item >= V_ITEM:
                    ready, value = v_ready, KEYS * l + 2 * (item - V_ITEM) + 2
                elif item >= U_ITEM:
                    ready, value = lower_ready, V_UNIT * l + U_UNIT + 2 * (item - U_ITEM) + 2
                else:
                    ready, value = lower_ready, V_UNIT * l + UNIT[HEAD[item // 2]] + 2 * (item % 2) + 2
                return ready, value if i is None else i * (2 * SLOTS) + value

            for l in range(LAYERS):
                for item in range(U_ITEM + SLOTS):
                    if item >= SLOTS and item - SLOTS < KEY_ITEM and HEAD[(item - SLOTS) // 2] in SPLIT:
                        wait = split_done(l, item - SLOTS)
                    elif item >= SLOTS:
                        wait = (products_done, plan.item_last(l, item - SLOTS) + 1)
                    elif l > 0:
                        wait = split_done(l - 1, ITEMS - SLOTS + item)
                    else:
                        wait = None
                    load(l, item, wait)
                for first in (U_ITEM, V_ITEM):
                    last = min(first + KEYS // 2, ITEMS - SLOTS)
                    turns = (last - first) // SLOTS
                    with sp.Fori(0, turns) as i:
                        for m in range(SLOTS):
                            load(l, first + SLOTS + m, split_done(l, first + m, i), i)
                    for item in range(first + SLOTS * turns, last):
                        load(l, item + SLOTS, split_done(l, item))
            for t in range(TILES):
                sp.wait_ge(final_out, t + 1)
                sp.dma_start(out[t * P:(t + 1) * P, :], xfin[:, t, :]).then_inc(stored, 16)
            sp.wait_ge(stored, 16 * TILES)

        @block.gpsimd
        def _(pool):
            pool.dma_start(const[:, :], consts).then_inc(const_in, 16)
            pool.dma_start(lev[0][:, 0:NLEV * P], masks).then_inc(const_in, 16)
            pool.dma_start(gcol[:, :, :].rearrange("p n c -> p (n c)"), cols).then_inc(const_in, 16)
            pool.dma_start(lb[:, 0:2, :].rearrange("p n h -> p (n h)"), lbl).then_inc(const_in, 16)
            pool.dma_start(stat[:, 92:94].bitcast(I32), pos).then_inc(const_in, 16)
            for l in range(LAYERS):
                if l > 0:
                    pool.wait_ge(read["x_done"], 8 * l)
                pool.dma_start(wsmall.rearrange("p c n -> p (c n)"), small[l]).then_inc(layer_in, 16)
                pool.dma_start(ws.rearrange("p g t -> p (g t)"), wsT[l]).then_inc(layer_in, 16)
                pool.dma_start(bs, bsT[l]).then_inc(layer_in, 16)
                pool.dma_start(hrow, hgain[l:l + 1, :].to_broadcast([P, P])).then_inc(layer_in, 16)
                pool.dma_start(grow, ggain[l:l + 1, :].to_broadcast([P, W])).then_inc(layer_in, 16)

                def lower_part(i, k, item, half):
                    n = l * ITEMS + item
                    pool.wait_ge(upper_ready, i * TURN + (UNITS * l + k + 1))
                    pool.tensor_tensor(lower[:, k % PARTS, :], ring[:, n % SLOTS, half * D:(half + 1) * D],
                                       upper[:, k % PARTS, :].bitcast(F32), ALU.subtract).then_inc(lower_ready, 1)

                for name in SPLIT:
                    for u in range(4):
                        lower_part(0, UNIT[name] + u, FIRST[name] + u // 2, u % 2)
                    if name == "ck":
                        pool.wait_ge(layer_in, 80 * (l + 1))
                        pool.affine_select(out=ws, in_=ws, pattern=[[0, HEADS], [1, P]], compare_op=ALU.is_ge,
                                           fill=0.0, base=0, channel_multiplier=-1).then_inc(ws_causal, 1)
                columns(pool, 0, KEYS, lambda i, j: lower_part(i, U_UNIT + j, U_ITEM + j // 2, j % 2))
            pool.wait_ge(read["x_done"], 8 * LAYERS)
            pool.dma_start(frow, fgain.to_broadcast([P, D])).then_inc(layer_in, 16)

        @block.tensor
        def _(pe):
            done = [0]

            def begin(l, name):
                assert plan.index[l, name] == done[0], (name, done[0])
                done[0] += 1
                if plan.before[l, name]:
                    wait_read(pe, *plan.before[l, name])
                return bank[plan.bank[l, name]]

            def item_in(l, item):
                n = l * ITEMS + item
                pe.wait_ge(arrived[n % SLOTS], 16 * (n // SLOTS + 1))
                return ring[:, n % SLOTS, :]

            def begin_at(l, name):
                if plan.before[l, name]:
                    wait_read(pe, *plan.before[l, name])
                return bank[plan.bank[l, name]]

            def finish(l, name, mm):
                assert plan.index[l, name] == done[0], (name, done[0])
                done[0] += 1
                mm.then_inc(products_done, 1)

            def step_done(l, name, step, mm):
                assert plan.index[l, f"{name}.{step}"] == done[0]
                done[0] += 1
                mm.then_inc(products_done, 1)

            WEIGHT_BY_H = ((upper, hT_upper), (upper, hT_lower), (lower, hT_upper))
            H_BY_WEIGHT = ((hT_upper, upper), (hT_upper, lower), (hT_lower, upper))

            def unit_in(l, k):
                pe.wait_ge(lower_ready, V_UNIT * l + k + 1)
                return k % PARTS

            def transposes(l, name, sources):
                b = begin(l, name)
                for n, src in enumerate(sources):
                    mm = pe.transpose(b[:, n * P:(n + 1) * P], src, ident)
                mm.then_inc(products_done, 1)

            def norm_transposes(l, which):
                for t in range(TILES):
                    pe.wait_ge(xn_ready, TILES * (2 * l + which) + t + 1)
                    for half in range(2):
                        transposes(l, f"n{which + 1}.{t}{half}",
                                   [xn[:, t, (4 * half + c) * P:(4 * half + c + 1) * P] for c in range(4)])

            def split_block_by_token(l, name):
                opened = [begin_at(l, f"{name}{t}") for t in range(TILES)]
                for u in range(4):
                    k = unit_in(l, UNIT[name] + u)
                    for t in range(TILES):
                        for c in range(2):
                            at_h = (2 * u + c) * S + t * P
                            for n, (h, w) in enumerate(H_BY_WEIGHT):
                                mm = pe.matmul(opened[t][:, :], h[:, at_h:at_h + P], w[:, k, c * W:(c + 1) * W],
                                               start=(u == 0 and c == 0 and n == 0), stop=(u == 3 and c == 1 and n == 2))
                        if u == 3:
                            finish(l, f"{name}{t}", mm)
                    if u < 3:
                        step_done(l, name, u, mm)

            def block_by_token(l, name, chunks):
                opened = [begin_at(l, f"{name}{t}") for t in range(TILES)]
                for q in range(2):
                    w = item_in(l, FIRST[name] + q).rearrange("p (c n) -> p c n", c=KC // 2)
                    for t in range(TILES):
                        for c in range(KC // 2):
                            mm = pe.matmul(opened[t][:, :], chunks(4 * q + c)[:, t * P:(t + 1) * P], w[:, c, :],
                                           start=(q == 0 and c == 0), stop=(q == 1 and c == KC // 2 - 1))
                        if q == 1:
                            finish(l, f"{name}{t}", mm)
                    if q == 0:
                        step_done(l, name, 0, mm)

            def split_block_by_column(l, name):
                for pair in range(2):
                    b = begin_at(l, f"{name}{pair}")
                    for m in range(2):
                        k = unit_in(l, UNIT[name] + 2 * pair + m)
                        for c in range(KC):
                            for n, (w, h) in enumerate(WEIGHT_BY_H):
                                mm = pe.matmul(b[:, m * S:(m + 1) * S], w[:, k, c * P:(c + 1) * P], h[:, c * S:(c + 1) * S],
                                               start=(c == 0 and n == 0), stop=(c == KC - 1 and n == 2))
                        if m == 0:
                            step_done(l, name, 2 * pair, mm)
                    finish(l, f"{name}{pair}", mm)

            for l in range(LAYERS):
                if l == 0:
                    pe.wait_ge(const_in, 16 * 5)
                norm_transposes(l, 0)
                pe.wait_ge(hT_split, 2 * l + 1)
                split_block_by_token(l, "iq")
                pe.wait_ge(layer_in, 80 * (l + 1))
                for t in range(TILES):
                    b = begin(l, f"small{t}")
                    for c in range(KC):
                        mm = pe.matmul(b[:, 0:SMALL_COLS], hT[:, c, t * P:(t + 1) * P], wsmall[:, c, :],
                                       start=(c == 0), stop=(c == KC - 1))
                    mm.then_inc(products_done, 1)
                split_block_by_token(l, "cq")
                split_block_by_token(l, "ck")
                split_block_by_column(l, "af")
                split_block_by_column(l, "aq")
                for t in range(TILES):
                    wait_read(pe, l, f"iq{t}")
                    transposes(l, f"iqT{t}", [mixer["iq"][:, t, n * P:(n + 1) * P] for n in range(4)])
                wait_read(pe, l, "small1")
                transposes(l, "ikT", [ikn[:, t, :] for t in range(TILES)])
                split_block_by_token(l, "ag")
                split_block_by_token(l, "ai")
                wait_read(pe, l, "ikT")
                for t in range(TILES):
                    keys = (t + 1) * P
                    for n in range(4):
                        b = begin(l, f"logit{t}{n}")
                        odd, first = n % 2, 4 * (n // 2)
                        rows = slice(IDX_DIM * odd, IDX_DIM * (odd + 1))
                        for m in range(2):
                            head = first + 2 * m + odd
                            mm = pe.matmul(b[:, m * S:m * S + keys], iqT[rows, head // 2, t * P:(t + 1) * P],
                                           ikT[rows, 0:keys], start=True, stop=True)
                        mm.then_inc(products_done, 1)
                for name in ("cq", "ck"):
                    for t in range(TILES):
                        wait_read(pe, l, f"{name}{t}")
                        transposes(l, f"{name}T{t}", [mixer[name][:, t, h * P:(h + 1) * P] for h in range(HEADS)])
                split_block_by_token(l, "cv")
                split_block_by_token(l, "bu")
                split_block_by_token(l, "bv")
                split_block_by_token(l, "gate0")
                split_block_by_token(l, "gate1")
                head = lambda ap, h, t: ap[:, h * S + t * P:h * S + (t + 1) * P]
                pe.wait_ge(decayed, (NLEV + 2) * l + 1)
                for t in range(TILES):
                    b = begin(l, f"diag{t}")
                    for h in range(HEADS):
                        mm = pe.matmul(b[:, h * P:(h + 1) * P], head(key, h, t), head(qs, h, t), start=True, stop=True)
                    mm.then_inc(products_done, 1)
                pe.wait_ge(decayed, (NLEV + 2) * l + 2)
                b = begin(l, "cross")
                for h in range(HEADS):
                    mm = pe.matmul(b[:, h * P:(h + 1) * P], head(lev[0], h, 0), head(lev[0], h, 1), start=True, stop=True)
                mm.then_inc(products_done, 1)
                for k in range(NLEV):
                    if k in (1, 3, 5):
                        split_block_by_token(l, f"gate{2 + k // 2}")
                    pe.wait_ge(decayed, (NLEV + 2) * l + 3 + k)
                    for t in range(TILES):
                        b = begin(l, f"lev{k}{t}")
                        for h in range(HEADS):
                            m = head(lev[(k + 1) % 3], h, t)
                            mm = pe.matmul(b[:, h * P:(h + 1) * P], m, m, start=True, stop=True)
                        mm.then_inc(products_done, 1)
                wait_read(pe, l, "ckT1")
                for t in range(TILES):
                    keys = (t + 1) * P
                    for pair in range(2):
                        b = begin(l, f"att{t}{pair}")
                        for m in range(2):
                            h = 2 * pair + m
                            mm = pe.matmul(b[:, m * S:m * S + keys], cqT[:, h, t * P:(t + 1) * P], ckT[:, h, 0:keys],
                                           start=True, stop=True)
                        mm.then_inc(products_done, 1)
                pe.wait_ge(ws_causal, l + 1)
                for t in range(TILES):
                    pe.wait_ge(v_normed, TILES * l + t + 1)
                    b = begin(l, f"mix{t}")
                    for g in range(HEADS):
                        mm = pe.matmul(b[:, g * P:(g + 1) * P], ws[:, g, :], mixer["bv"][:, t, g * P:(g + 1) * P],
                                       start=True, stop=True)
                    mm.then_inc(products_done, 1)
                wait_read(pe, l, f"lev{NLEV - 1}1")
                wait_read(pe, l, "cross")
                wait_read(pe, l, "ai1")
                for t in range(TILES):
                    b = begin(l, f"hout{t}")
                    for h in range(HEADS):
                        cols_h = slice(h * P, (h + 1) * P)
                        mm = pe.matmul(b[:, cols_h], pairT[:, t, h, :], mixer["ai"][:, t, cols_h],
                                       start=True, stop=(t == 0))
                        if t == 1:
                            mm = pe.matmul(b[:, cols_h], crossT[:, h, :], mixer["ai"][:, 0, cols_h],
                                           start=False, stop=True)
                    mm.then_inc(products_done, 1)
                split_block_by_token(l, "gate5")
                pe.wait_ge(probs, 8 * l + 4)
                transposes(l, "pT0", [prob[:, 0, h, 0:P] for h in range(HEADS)])
                pe.wait_ge(probs, 8 * l + 8)
                for pair in range(2):
                    transposes(l, f"pT1{pair}", [prob[:, 1, 2 * pair + m, s * P:(s + 1) * P]
                                                 for m in range(2) for s in range(2)])
                wait_read(pe, l, "cv1")
                wait_read(pe, l, "pT11")
                for t in range(TILES):
                    b = begin(l, f"aout{t}")
                    for h in range(HEADS):
                        cols_h = slice(h * P, (h + 1) * P)
                        for s in range(t + 1):
                            lhs = pT0[:, h, :] if t == 0 else pT1[:, h, s, :]
                            mm = pe.matmul(b[:, cols_h], lhs, mixer["cv"][:, s, cols_h], start=(s == 0), stop=(s == t))
                    mm.then_inc(products_done, 1)
                ys = (mixer["ag"], mixer["bu"], yc)
                pe.wait_ge(ya_ready, l + 1)
                wait_read(pe, l, "mix1")
                wait_read(pe, l, "aout1")
                for n in range(BRANCHES):
                    for t in range(TILES):
                        transposes(l, f"y{n}{t}", [ys[n][:, t, k * P:(k + 1) * P] for k in range(4)])
                for n in range(BRANCHES):
                    wait_read(pe, l, f"y{n}1")
                    for half in range(2):
                        w = item_in(l, FIRST[f"br{n}"] + half).rearrange("p (k n) -> p k n", k=4)
                        for t in range(TILES):
                            b = begin(l, f"br{n}{half}{t}")
                            for k in range(4):
                                mm = pe.matmul(b[:, :], yT[n][:, k, t * P:(t + 1) * P], w[:, k, :],
                                               start=(k == 0), stop=(k == 3))
                            mm.then_inc(products_done, 1)
                for half in range(2):
                    for t in range(TILES):
                        pe.wait_ge(mix_done, 4 * l + 2 * half + t + 1)
                        transposes(l, f"mT{half}{t}", [mixsum[:, t, (4 * half + c) * P:(4 * half + c + 1) * P] for c in range(4)])
                wait_read(pe, l, "mT11")
                for half in range(2):
                    block_by_token(l, f"out{half}", lambda c: mT[c // 4][:, c % 4, :])
                norm_transposes(l, 1)
                pe.wait_ge(hT_split, 2 * l + 2)
                for n in range(4):
                    split_block_by_column(l, f"qry{n}")
                wait_read(pe, l, "qry31")
                for b in range(4):
                    wait_read(pe, *plan.last_of(l, b))
                assert done[0] == plan.base[l, "seed"]
                for half in range(2):
                    for t in range(TILES):
                        pe.matmul(bank[2 * half + t][:, :], ident, xs[:, t, half * 512:(half + 1) * 512], start=True,
                                  stop=False, skip_group_check=True).then_inc(products_done, 1)
                        done[0] += 1
                subkeys = item_in(l, KEY_ITEM)[:, 0:HP * KEYS].rearrange("p (n k) -> p n k", n=HP)
                for t in range(TILES):
                    for n in range(4):
                        b = begin(l, f"sc{t}{n}")
                        for m in range(4):
                            hp = 4 * n + m
                            mm = pe.matmul(b[:, m * KEYS:(m + 1) * KEYS], qryT[:, hp, t * P:(t + 1) * P], subkeys[:, hp, :],
                                           start=True, stop=True)
                        mm.then_inc(products_done, 1)
                for b in (6, 7):
                    wait_read(pe, *plan.last_of(l, b))

                def u_column(i, j):
                    if 2 <= j < AHEAD + 2:
                        pe.wait_ge(gelu_done, i * TURN + (KEYS * l + j - 1))
                    elif j >= AHEAD + 2:
                        pe.wait_ge(gelu_in, i * TURN + (GATED * l + j - AHEAD - 1))
                    k = U_UNIT + j
                    pe.wait_ge(lower_ready, i * TURN + (V_UNIT * l + k + 1))
                    for c in range(KC):
                        at_h = slice(c * S, (c + 1) * S)
                        for n, (u, h) in enumerate(WEIGHT_BY_H):
                            mm = pe.matmul(bank[6 + j % 2][:, 0:S], u[:, k % PARTS, c * P:(c + 1) * P], h[:, at_h],
                                           start=(c == 0 and n == 0), stop=(c == KC - 1 and n == 2))
                    mm.then_inc(products_done, 1)

                columns(pe, 0, AHEAD, u_column, straight=TURN)
                done[0] += AHEAD

                pe.wait_ge(picked, TILES * (l + 1))
                for n, name in enumerate(("IT", "JT", "gT")):
                    src = [pick_ij[:, t, n, :] if n < 2 else gate_k[:, t, :, :].rearrange("p h k -> p (h k)")
                           for t in range(TILES)]
                    transposes(l, name, src)
                for b in (4, 5):
                    wait_read(pe, *plan.last_of(l, b))

                def gates_and_u(i, g):
                    if g >= 2:
                        pe.wait_ge(gates_in, i * TURN + (GROUPS * l + g - 1))
                    pe.wait_ge(hot_ready, i * TURN + (GROUPS * l + g + 1))
                    for m in range(4):
                        mm = pe.matmul(bank[4 + g % 2][:, m * P:(m + 1) * P], hot[:, 0, m, :], hot[:, 1, m, :],
                                       start=True, stop=True)
                        mm.then_inc(products_done, 1)
                    u_column(i, AHEAD + g)

                columns(pe, 0, GROUPS, gates_and_u, straight=TURN)
                columns(pe, AHEAD + GROUPS, KEYS, u_column)

                def v_column(i, j):
                    pe.wait_ge(w_ready, i * TURN + (KEYS * l + j + 1))
                    pe.wait_ge(v_ready, i * TURN + (KEYS * l + j + 1))
                    k = (V_UNIT + j) % PARTS
                    for t in range(TILES):
                        for n, (w, v) in enumerate(((w_upper, upper), (w_upper, lower), (w_lower, upper))):
                            for half in range(2):
                                mm = pe.matmul(bank[2 * half + t][:, :], w[:, j % 2, t * P:(t + 1) * P],
                                               v[:, k, half * 512:(half + 1) * 512], start=False,
                                               stop=(j == KEYS - 1 and n == 2), skip_group_check=True)
                    mm.then_inc(products_done, 1)

                columns(pe, 0, KEYS, v_column)
                done[0] += 5 * GROUPS + GATED - GROUPS + KEYS

        @block.scalar
        def _(act):
            chain = [0]

            def link(ins):
                chain[0] += 1
                ins.then_inc(act_chain, 1)
                act.wait_ge(act_chain, chain[0])

            def norm(n):
                if n > 0:
                    act.wait_ge(read["x_done"], 4 * n)
                for t in range(TILES):
                    act.activation(xn[:, t, :], xs[:, t, :], ACT.Square,
                                   accum_out=stat[:, t:t + 1]).then_inc(squares, 1)
                act.wait_ge(meansq, n + 1)
                act.activation(stat[:, 4:6], stat[:, 2:4], ACT.Sqrt).then_inc(roots, 1)

            act.wait_ge(const_in, 16 * 5)
            act.wait_ge(x_in, 16 * TILES)
            act.wait_ge(trig_in, 1)
            act.activation(trig[:, :, :, :], trig[:, :, :, :], ACT.Sin).then_inc(trig_out, 1)
            act.wait_ge(lb_in, 1)
            act.activation(lb[:, 2:4, :], lb[:, 0:2, :], ACT.Exp).then_inc(lb_out, 1)
            act.wait_ge(lb_in, 2)
            act.activation(lb[:, 5, :], lb[:, 4, :], ACT.Ln).then_inc(lb_out, 1)

            unit = [0]

            def to_upper(l, i, k):
                item = FIRST[SPLIT[k // 4]] + k % 4 // 2 if k < U_UNIT else \
                    U_ITEM + (k - U_UNIT) // 2 if k < V_UNIT else V_ITEM + (k - V_UNIT) // 2
                n = l * ITEMS + item
                if k % 2 == 0:
                    act.wait_ge(arrived[n % SLOTS], i * 16 + 16 * (n // SLOTS + 1))
                act.activation(upper[:, k % PARTS, :], ring[:, n % SLOTS, (k % 2) * D:(k % 2 + 1) * D], ACT.Copy)\
                   .then_inc(upper_ready, 1)

            def uppers_to(l, name):
                end = U_UNIT if plan.index[l, name] >= plan.index[l, "out11"] else UNIT["qry0"]
                while unit[0] < end and (unit[0] < PARTS or plan.unit_step(l, unit[0] - PARTS) <= plan.index[l, name]):
                    if unit[0] >= PARTS:
                        act.wait_ge(products_done, plan.unit_step(l, unit[0] - PARTS) + 1)
                    elif l > 0:
                        act.wait_ge(products_done, plan.v_index(l - 1, KEYS - PARTS + unit[0]) + 1)
                    to_upper(l, 0, unit[0])
                    unit[0] += 1

            for l in range(LAYERS):
                def out_of(name, dst, func=ACT.Copy, cols=512):
                    uppers_to(l, name)
                    b = full(act, l, name)
                    src = b[:, 0:cols]
                    if len(dst.shape) == 3:
                        src = src.rearrange("p (a n) -> p a n", a=dst.shape[1])
                    elif len(dst.shape) == 4:
                        src = src.rearrange("p (a b n) -> p a b n", a=dst.shape[1], b=dst.shape[2])
                    done_reading(act.activation(dst, src, func), l, name)

                def block_out(name, dst, func=ACT.Copy):
                    for t in range(TILES):
                        out_of(f"{name}{t}", dst[:, t, :], func)

                def gate_out(n):
                    block_out(f"gate{n}", gates[:, :, n * 512:(n + 1) * 512], ACT.Sigmoid)

                unit[0] = 0
                uppers_to(l, "n1.00")
                norm(2 * l)
                for pair in range(2):
                    uppers_to(l, f"af{pair}")
                    b = full(act, l, f"af{pair}")
                    act.activation(zT[:, pair * 512:(pair + 1) * 512], b[:, :], ACT.Copy)
                    done_reading(act.activation(key[:, pair * 512:(pair + 1) * 512], b[:, :], ACT.Sigmoid, scale=-1.0),
                                 l, f"af{pair}")
                for pair in range(2):
                    out_of(f"aq{pair}", qs[:, pair * 512:(pair + 1) * 512], ACT.Silu)
                for t in range(TILES):
                    out_of(f"iqT{t}", iqT[:, :, t * P:(t + 1) * P])
                out_of("ikT", ikT, cols=S)
                block_out("ag", mixer["ag"], ACT.Silu)
                block_out("ai", mixer["ai"])
                wait_read(act, l, "ck1")
                for t in range(TILES):
                    keys = (t + 1) * P
                    for n in range(4):
                        use = 8 * l + 4 * t + n
                        if n + 4 * t >= 2:
                            act.wait_ge(relu_used, use - 1)
                        uppers_to(l, f"logit{t}{n}")
                        b = full(act, l, f"logit{t}{n}")
                        dst = tmp[:, (n % 2) * 512:(n % 2 + 1) * 512].rearrange("p (m k) -> p m k", m=2)[:, :, 0:keys]
                        src = b[:, :].rearrange("p (m k) -> p m k", m=2)[:, :, 0:keys]
                        done_reading(act.activation(dst, src, ACT.Relu, scale=IDX_DIM ** -0.5), l, f"logit{t}{n}")
                for t in range(TILES):
                    out_of(f"cqT{t}", cqT[:, :, t * P:(t + 1) * P])
                for t in range(TILES):
                    out_of(f"ckT{t}", ckT[:, :, t * P:(t + 1) * P])
                block_out("cv", mixer["cv"])
                block_out("bu", mixer["bu"], ACT.Gelu_apprx_tanh)
                block_out("bv", mixer["bv"], ACT.Gelu_apprx_tanh)
                wait_read(act, l, "bv1")
                for t in range(TILES):
                    link(act.activation(gates[:, t, 1024:1536], mixer["bv"][:, t, :], ACT.Square,
                                        accum_out=stat[:, 8 + t:9 + t]))
                act.sem_inc(vsq, 1)
                act.wait_ge(vms, l + 1)
                act.activation(stat[:, 12:14], stat[:, 10:12], ACT.Sqrt).then_inc(vroot, 1)

                def softplus(use):
                    act.wait_ge(soft_in, use)
                    link(act.activation(logf, logf, ACT.Exp))
                    act.activation(logf, logf, ACT.Ln, bias=1.0).then_inc(soft_out, 1)

                def decay(q):
                    act.wait_ge(decay_arg, (NLEV + 1) * l + q + 1)
                    act.activation(lev[q % 3], lev[q % 3], ACT.Exp).then_inc(decay_exp, 1)

                uppers_to(l, "gate0.0")
                softplus(1 if l == 0 else 2 * l)
                gate_out(0)
                uppers_to(l, "gate1.0")
                if l > 0:
                    softplus(2 * l + 1)
                decay(0)
                decay(1)
                gate_out(1)
                b = full(act, l, "cross")
                done_reading(act.activation(crossT, b[:, :].rearrange("p (h n) -> p h n", h=HEADS), ACT.Copy), l, "cross")
                for n in (2, 3, 4):
                    uppers_to(l, f"gate{n}.0")
                    decay(2 * n - 2)
                    decay(2 * n - 1)
                    gate_out(n)
                for t in range(TILES):
                    keys = (t + 1) * P
                    act.wait_ge(neg_max, TILES * l + t + 1)
                    for h in range(HEADS):
                        c = HEADS * t + h
                        act.activation(prob[:, t, h, 0:keys], prob[:, t, h, 0:keys], ACT.Exp, scale=P ** -0.5,
                                       bias=stat[:, 24 + c:25 + c], accum_out=stat[:, 32 + c:33 + c]).then_inc(probs, 1)
                for t in range(TILES):
                    out_of(f"hout{t}", oh[:, t, :])
                uppers_to(l, "gate5.0")
                act.wait_ge(oms, l + 1)
                act.activation(stat[:, 56:64], stat[:, 48:56], ACT.Sqrt).then_inc(oroot, 1)
                gate_out(5)
                out_of("pT0", pT0)
                for pair in range(2):
                    out_of(f"pT1{pair}", pT1[:, 2 * pair:2 * pair + 2, :, :])
                for n in range(BRANCHES):
                    for t in range(TILES):
                        out_of(f"y{n}{t}", yT[n][:, :, t * P:(t + 1) * P])
                for half in range(2):
                    for t in range(TILES):
                        out_of(f"mT{half}{t}", mT[half][:, :, t * P:(t + 1) * P])
                uppers_to(l, "out11")
                norm(2 * l + 1)
                for n in range(4):
                    for pair in range(2):
                        out_of(f"qry{n}{pair}", qryT[:, 4 * n + 2 * pair:4 * n + 2 * pair + 2, :])
                assert unit[0] == U_UNIT
                for k in range(PARTS):
                    act.wait_ge(products_done, plan.unit_step(l, U_UNIT + k - PARTS) + 1)
                    to_upper(l, 0, U_UNIT + k)
                for t in range(TILES):
                    for n in range(4):
                        out_of(f"sc{t}{n}", sc[:, t, 4 * n:4 * n + 4, :])
                def u_column(i, j):
                    steps = 5 if AHEAD <= j < AHEAD + GROUPS else 1
                    act.wait_ge(products_done, i * (steps * TURN) + (plan.u_index(l, j) + 1))
                    b = bank[6 + j % 2]
                    dst = G[:, bass.ds(i * TURN + j, 1), :].rearrange("p a t -> p (a t)") if j < AHEAD else b[:, S:2 * S]
                    act.activation(dst, b[:, 0:S], ACT.Gelu_apprx_tanh).then_inc(gelu_done, 1)
                    to_upper(l, i, U_UNIT + j + PARTS)

                for t, (first, last) in enumerate(((0, AHEAD // 2), (AHEAD // 2, AHEAD * 3 // 4), (AHEAD * 3 // 4, AHEAD))):
                    columns(act, first, last, u_column)
                    if t < TILES:
                        act.wait_ge(best_diff, TILES * l + t + 1)
                        act.activation(gate_k[:, t, :, :], gate_k[:, t, :, :], ACT.Exp).then_inc(best_exp, 1)
                for name, dst in (("IT", IT), ("JT", JT), ("gT", gT)):
                    out_of(name, dst, cols=S)
                columns(act, AHEAD, AHEAD + GROUPS, u_column)
                columns(act, AHEAD + GROUPS, KEYS, u_column)

                def v_column(i, j):
                    if j >= 2:
                        act.wait_ge(products_done, i * TURN + (plan.v_index(l, j - 2) + 1))
                    act.activation(w_upper[:, j % 2, :], G[:, bass.ds(i * TURN + j, 1), :].rearrange("p a t -> p (a t)"),
                                   ACT.Copy).then_inc(w_upper_ready, 1)
                    if 2 <= j < KEYS - 1:
                        to_upper(l, i, V_UNIT + j + 1)

                act.wait_ge(gelu_in, GATED * (l + 1))
                act.wait_ge(gates_in, GROUPS * (l + 1))
                columns(act, 0, KEYS, v_column, straight=2, tail=1)
            norm(2 * LAYERS)

        @block.vector
        def _(dve):
            chain = [0]

            def link(ins):
                chain[0] += 1
                ins.then_inc(dve_chain, 1)
                dve.wait_ge(dve_chain, chain[0])

            def norm(n, dst):
                dve.wait_ge(squares, TILES * (n + 1))
                dve.tensor_scalar(stat[:, 2:4], stat[:, 0:2], 1.0 / D, EPS, ALU.mult, ALU.add).then_inc(meansq, 1)
                dve.wait_ge(roots, n + 1)
                link(dve.reciprocal(stat[:, 6:8], stat[:, 4:6]))
                for t in range(TILES):
                    ins = dve.tensor_scalar(dst[:, t, :], xs[:, t, :], stat[:, 6 + t:7 + t], None, ALU.mult)
                    if n < 2 * LAYERS:
                        ins.then_inc(xn_ready, 1)
                    else:
                        link(ins)

            def gained(l, which):
                for t in range(TILES):
                    for half in range(2):
                        name = f"n{which + 1}.{t}{half}"
                        b = full(dve, l, name)
                        gain = gcol[:, 2 * l + which, 4 * half:4 * half + 4].unsqueeze(2).to_broadcast([P, 4, P])
                        done_reading(dve.tensor_tensor(hT[:, 4 * half:4 * half + 4, t * P:(t + 1) * P],
                                                       b[:, :].rearrange("p (c t) -> p c t", c=4), gain, ALU.mult), l, name)
                wait_read(dve, l, name)
                flat = hT.rearrange("p c t -> p (c t)")
                link(dve.tensor_copy(hT_upper[:, :], flat))
                dve.tensor_tensor(hT_lower[:, :], flat, hT_upper[:, :].bitcast(F32), ALU.subtract).then_inc(hT_split, 1)

            def rope(l, name, t, src, dst, heads, half, extra=None):
                first = 0 if half == 64 else 64
                table = lambda f: trig[:, f, t, first:first + half].unsqueeze(1)
                n = heads * half
                both = tmp[:, 0:2 * n].rearrange("p (h s d) -> p h s d", h=heads, s=2)
                cross = tmp[:, 512:512 + 2 * n].rearrange("p (h s d) -> p h s d", h=heads, s=2)
                cos = table(0).unsqueeze(1).to_broadcast([P, heads, 2, half])
                sin = table(1).to_broadcast([P, heads, half])
                dve.tensor_tensor(both, src, cos, ALU.mult)
                dve.tensor_tensor(cross[:, :, 0, :], src[:, :, 1, :], sin, ALU.mult)
                link(dve.tensor_tensor(cross[:, :, 1, :], src[:, :, 0, :], sin, ALU.mult))
                dve.tensor_tensor(dst[:, :, 0, :], both[:, :, 0, :], cross[:, :, 0, :], ALU.subtract)
                ins = dve.tensor_tensor(dst[:, :, 1, :], both[:, :, 1, :], cross[:, :, 1, :], ALU.add)
                return ins

            dve.memset(zero64[:, :], 0.0)
            dve.wait_ge(const_in, 16 * 5)
            dve.tensor_copy(mask[:, :, :].rearrange("p k n -> p (k n)"), lev[0][:, 0:NLEV * P])
            dve.wait_ge(x_in, 16 * TILES)
            posf = stat[:, 94:96]
            link(dve.tensor_copy(posf, stat[:, 92:94].bitcast(I32)))
            two_pi = 2.0 * np.pi
            c1 = 6.28125
            c2 = float(np.uint32(int(np.float32(two_pi - c1).view(np.uint32)) & 0xFFFFE000).view(np.float32))
            c3 = float(two_pi - c1 - c2)
            magic = 1.5 * 2.0 ** 23
            turns = tmp[:, 0:192].rearrange("p (t n) -> p t n", t=TILES)
            for f in range(2):
                shift = 0.25 if f == 0 else 0.0
                for t in range(TILES):
                    link(dve.tensor_scalar(trig[:, f, t, :], freq, posf[:, t:t + 1], None, ALU.mult))
                link(dve.tensor_scalar(turns, trig[:, f, :, :], 1.0 / two_pi, shift, ALU.mult, ALU.add))
                link(dve.tensor_scalar(turns, turns, magic, None, ALU.add))
                link(dve.tensor_scalar(turns, turns, -magic, None, ALU.add))
                for c in (c1, c2, c3):
                    link(dve.scalar_tensor_tensor(out=trig[:, f, :, :], in0=turns, scalar=-c, in1=trig[:, f, :, :],
                                                  op0=ALU.mult, op1=ALU.add))
                if f == 0:
                    link(dve.tensor_scalar(trig[:, f, :, :], trig[:, f, :, :], np.pi / 2, None, ALU.add))
            dve.tensor_scalar(trig[:, :, :, :], trig[:, :, :, :], 3.1415925, -3.1415925, ALU.min, ALU.max).then_inc(trig_in, 1)

            scale_a = P ** -0.5
            link(dve.tensor_tensor(lb[:, 4, :], lb[:, 0, :], lb[:, 1, :], ALU.max))
            for l in range(LAYERS):
                ins = dve.tensor_tensor(lb[:, l, :], lb[:, l, :], lb[:, 4, :], ALU.subtract)
                link(ins)
            dve.sem_inc(lb_in, 1)
            dve.wait_ge(lb_out, 1)
            link(dve.tensor_tensor(lb[:, 4, :], lb[:, 2, :], lb[:, 3, :], ALU.add))
            dve.sem_inc(lb_in, 1)
            dve.wait_ge(lb_out, 2)
            log_lb, log_rest, rest = lb[:, 6, :], lb[:, 7, :], lb[:, 4, :]
            dve.tensor_tensor(log_lb, lb[:, 1, :], lb[:, 5, :], ALU.subtract)
            link(dve.tensor_tensor(log_rest, lb[:, 0, :], lb[:, 5, :], ALU.subtract))
            link(dve.reciprocal(lb[:, 5, :], lb[:, 4, :]))
            for n in (2, 3):
                link(dve.tensor_tensor(lb[:, n, :], lb[:, n, :], lb[:, 5, :], ALU.mult))
            link(dve.tensor_tensor(rest, lb[:, 2, :], lb[:, 3, :], ALU.add))
            link(dve.tensor_tensor(rest, rest, lb[:, 2, :], ALU.subtract))
            link(dve.tensor_scalar(rest, rest, -scale_a, scale_a, ALU.mult, ALU.add))
            dve.wait_ge(trig_out, 1)

            by_head = lambda c: c.unsqueeze(2).to_broadcast([P, HEADS, S])
            heads_of = lambda ap: ap.rearrange("p (h t) -> p h t", h=HEADS)

            for l in range(LAYERS):
                norm(2 * l, xn)
                gained(l, 0)
                for t in range(TILES):
                    b = full(dve, l, f"iq{t}")
                    view = lambda ap: ap.rearrange("p (h s d) -> p h s d", h=IDX_HEADS, s=2)
                    done_reading(rope(l, "iq", t, view(b[:, :]), view(mixer["iq"][:, t, :]), IDX_HEADS, 32), l, f"iq{t}")
                    wait_read(dve, l, f"iq{t}")
                for t in range(TILES):
                    b = full(dve, l, f"small{t}")
                    view = lambda ap: ap.rearrange("p (h s d) -> p h s d", h=1, s=2)
                    link(rope(l, "ik", t, view(b[:, 0:IDX_DIM]), view(ikn[:, t, 0:IDX_DIM]), 1, 32))
                    dve.tensor_copy(ikn[:, t, IDX_DIM:2 * IDX_DIM], ikn[:, t, 0:IDX_DIM])
                    done_reading(dve.tensor_scalar(wi[:, t, :], b[:, IDX_DIM:SMALL_COLS], IDX_HEADS ** -0.5, None, ALU.mult),
                                 l, f"small{t}")
                    wait_read(dve, l, f"small{t}")
                for name in ("cq", "ck"):
                    for t in range(TILES):
                        b = full(dve, l, f"{name}{t}")
                        view = lambda ap: ap.rearrange("p (h s d) -> p h s d", h=HEADS, s=2)
                        done_reading(rope(l, name, t, view(b[:, :]), view(mixer[name][:, t, :]), HEADS, 64), l, f"{name}{t}")
                        wait_read(dve, l, f"{name}{t}")
                for t in range(TILES):
                    keys = (t + 1) * P
                    for n in range(4):
                        wait_read(dve, l, f"logit{t}{n}")
                        for m in range(2):
                            head = 4 * (n // 2) + 2 * m + n % 2
                            src = tmp[:, (n % 2) * 512 + m * S:(n % 2) * 512 + m * S + keys]
                            if n == 0 and m == 0:
                                ins = dve.tensor_scalar(score[:, t, 0:keys], src, wi[:, t, head:head + 1], None, ALU.mult)
                            else:
                                ins = dve.scalar_tensor_tensor(out=score[:, t, 0:keys], in0=src, scalar=wi[:, t, head:head + 1],
                                                               in1=score[:, t, 0:keys], op0=ALU.mult, op1=ALU.add)
                            link(ins)
                        dve.sem_inc(relu_used, 1)
                for t in range(TILES):
                    keys = (t + 1) * P
                    link(dve.memset(score[0:CHUNK, t, keys - CHUNK:keys], NEG))
                for r in range(DSA_TOPK // 8):
                    for t in range(TILES):
                        keys = (t + 1) * P
                        ins = dve.max(out=top8[:, 8 * t:8 * t + 8], in_=score[:, t, 0:keys])
                    link(ins)
                    for t in range(TILES):
                        keys = (t + 1) * P
                        ins = dve.match_replace(out=score[:, t, 0:keys], in_to_replace=top8[:, 8 * t:8 * t + 8],
                                                in_values=score[:, t, 0:keys], imm_value=MARK)
                    link(ins)
                for t in range(TILES):
                    keys = (t + 1) * P
                    link(dve.tensor_scalar(score[:, t, 0:keys], score[:, t, 0:keys], MARK, MASKED, ALU.not_equal, ALU.mult))

                dve.wait_ge(vsq, l + 1)
                dve.tensor_scalar(stat[:, 10:12], stat[:, 8:10], 1.0 / W, EPS, ALU.mult, ALU.add).then_inc(vms, 1)
                dve.wait_ge(vroot, l + 1)
                link(dve.reciprocal(stat[:, 14:16], stat[:, 12:14]))
                dve.wait_ge(layer_in, 80 * (l + 1))
                for t in range(TILES):
                    v = mixer["bv"][:, t, :]
                    dve.scalar_tensor_tensor(out=v, in0=v, scalar=stat[:, 14 + t:15 + t], in1=grow, op0=ALU.mult,
                                             op1=ALU.mult).then_inc(v_normed, 1)

                wait_read(dve, l, "aq1")
                z = zT
                dve.scalar_tensor_tensor(out=logf, in0=z, scalar=-1.0, in1=z, op0=ALU.mult, op1=ALU.min)\
                   .then_inc(soft_in, 1)
                if l == 0:
                    dve.tensor_scalar(key, key, scale_a, None, ALU.mult).then_inc(decayed, 1)
                else:
                    dve.tensor_tensor(heads_of(key), heads_of(key), by_head(rest), ALU.mult).then_inc(decayed, 1)
                dve.wait_ge(soft_out, 1 if l == 0 else 2 * l)
                link(dve.scalar_tensor_tensor(out=z, in0=z, scalar=0.0, in1=logf, op0=ALU.min, op1=ALU.subtract))
                if l > 0:
                    link(dve.tensor_tensor(heads_of(z), heads_of(z), by_head(log_rest), ALU.add))
                    link(dve.tensor_tensor(heads_of(bcum), heads_of(z), by_head(log_lb), ALU.subtract))
                    dve.scalar_tensor_tensor(out=logf, in0=bcum, scalar=-1.0, in1=bcum, op0=ALU.mult, op1=ALU.min)\
                       .then_inc(soft_in, 1)
                    link(dve.tensor_tensor(heads_of(z), heads_of(z), by_head(log_lb), ALU.max))
                    dve.wait_ge(soft_out, 2 * l + 1)
                    link(dve.tensor_tensor(z, z, logf, ALU.add))
                for c in range(HEADS * S // CHUNK):
                    ins = dve.tensor_tensor_scan(bcum[:, c * CHUNK:(c + 1) * CHUNK], z[:, c * CHUNK:(c + 1) * CHUNK],
                                                 zero64[:, :], 0.0, ALU.add, ALU.add)
                link(ins)

                def exponents(q):
                    if q >= 3:
                        full(dve, l, "cross" if q == 3 else f"lev{q - 4}1")
                    e = lev[q % 3]
                    if q == 0:
                        eh = e.rearrange("p (h c n) -> p h c n", h=HEADS, c=4)
                        bh = bcum.rearrange("p (h c n) -> p h c n", h=HEADS, c=4)
                        end = lambda c: bh[:, :, c, CHUNK - 1:CHUNK].to_broadcast([P, HEADS, CHUNK])
                        dve.tensor_tensor(eh[:, :, 1, :], end(1), bh[:, :, 1, :], ALU.subtract)
                        dve.tensor_copy(eh[:, :, 2, :], bh[:, :, 2, :])
                        dve.tensor_tensor(eh[:, :, 3, :], bh[:, :, 3, :], end(2), ALU.add)
                        link(dve.tensor_tensor(eh[:, :, 0, :], end(0), bh[:, :, 0, :], ALU.subtract))
                        dve.tensor_tensor(eh[:, :, 0, :], eh[:, :, 0, :], end(1), ALU.add).then_inc(decay_arg, 1)
                        return
                    half = HALVES[q - 1]
                    n = HEADS * S // (2 * half)
                    eb = e.rearrange("p (n s i) -> p n s i", n=n, s=2)
                    bb = bcum.rearrange("p (n s i) -> p n s i", n=n, s=2)
                    last = bb[:, :, 0, half - 1:half].to_broadcast([P, n, half])
                    dve.tensor_tensor(eb[:, :, 0, :], last, bb[:, :, 0, :], ALU.subtract)
                    if half == CHUNK:
                        dve.tensor_copy(eb[:, :, 1, :], bb[:, :, 1, :]).then_inc(decay_arg, 1)
                    else:
                        dve.tensor_tensor(eb[:, :, 1, :], bb[:, :, 1, :], last, ALU.subtract).then_inc(decay_arg, 1)

                def decayed_rows(q):
                    dve.wait_ge(decay_exp, (NLEV + 1) * l + q + 1)
                    half = P if q == 0 else HALVES[q - 1]
                    n = HEADS * S // (2 * half)
                    view = lambda ap: ap.rearrange("p (n s i) -> p n s i", n=n, s=2)
                    e = view(lev[q % 3])
                    dve.tensor_tensor(e[:, :, 0, :], e[:, :, 0, :], view(key)[:, :, 0, :], ALU.mult)
                    dve.tensor_tensor(e[:, :, 1, :], e[:, :, 1, :], view(qs)[:, :, 1, :], ALU.mult).then_inc(decayed, 1)

                def into_pairs(k):
                    wait_read(dve, l, f"lev{k - 1}1" if k else "diag1")
                    for t in range(TILES):
                        b = full(dve, l, f"lev{k}{t}")
                        m = mask[:, k, :].unsqueeze(1).to_broadcast([P, HEADS, P])
                        done_reading(dve.copy_predicated(pairT[:, t, :, :], m, b[:, :].rearrange("p (h n) -> p h n", h=HEADS)),
                                     l, f"lev{k}{t}")

                dve.wait_ge(decayed, (NLEV + 2) * l + 1)
                exponents(0)
                exponents(1)
                decayed_rows(0)
                exponents(2)
                decayed_rows(1)
                for t in range(TILES):
                    b = full(dve, l, f"diag{t}")
                    ins = dve.tensor_tensor(pairT[:, t, :, :], b[:, :].rearrange("p (h n) -> p h n", h=HEADS),
                                            ident.unsqueeze(1).to_broadcast([P, HEADS, P]), ALU.mult)
                    done_reading(ins, l, f"diag{t}")
                for k in range(NLEV):
                    if k + 3 <= NLEV:
                        exponents(k + 3)
                    if k + 2 <= NLEV:
                        decayed_rows(k + 2)
                    into_pairs(k)

                for t in range(TILES):
                    keys = (t + 1) * P
                    for pair in range(2):
                        b = full(dve, l, f"att{t}{pair}")
                        bias = score[:, t, 0:keys].unsqueeze(1).to_broadcast([P, 2, keys])
                        ins = dve.tensor_tensor(prob[:, t, 2 * pair:2 * pair + 2, 0:keys],
                                                b[:, :].rearrange("p (m k) -> p m k", m=2)[:, :, 0:keys], bias, ALU.add)
                        done_reading(ins, l, f"att{t}{pair}")
                    wait_read(dve, l, f"att{t}1")
                    link(dve.tensor_reduce(stat[:, 16 + 4 * t:20 + 4 * t], prob[:, t, :, 0:keys], AX.X, ALU.max))
                    dve.tensor_scalar(stat[:, 24 + 4 * t:28 + 4 * t], stat[:, 16 + 4 * t:20 + 4 * t], -(P ** -0.5), None,
                                      ALU.mult).then_inc(neg_max, 1)
                for t in range(TILES):
                    b = full(dve, l, f"mix{t}")
                    for g in range(HEADS):
                        u = mixer["bu"][:, t, g * P:(g + 1) * P]
                        ins = dve.scalar_tensor_tensor(out=u, in0=b[:, g * P:(g + 1) * P], scalar=bs[:, g:g + 1], in1=u,
                                                       op0=ALU.add, op1=ALU.mult)
                    done_reading(ins, l, f"mix{t}")
                wait_read(dve, l, "hout1")
                per_head = lambda ap: ap.rearrange("p t (h n) -> p (t h) n", h=HEADS)
                link(dve.tensor_tensor(osq, oh, oh, ALU.mult))
                link(dve.tensor_reduce(stat[:, 48:56], per_head(osq), AX.X, ALU.add))
                dve.tensor_scalar(stat[:, 48:56], stat[:, 48:56], 1.0 / P, EPS, ALU.mult, ALU.add).then_inc(oms, 1)
                dve.wait_ge(oroot, l + 1)
                link(dve.reciprocal(stat[:, 64:72], stat[:, 56:64]))
                link(dve.tensor_tensor(per_head(oh), per_head(oh), stat[:, 64:72].unsqueeze(2).to_broadcast([P, 8, P]), ALU.mult))
                link(dve.tensor_tensor(per_head(oh), per_head(oh), hrow.unsqueeze(1).to_broadcast([P, 8, P]), ALU.mult))
                dve.tensor_tensor(mixer["ag"], mixer["ag"], oh, ALU.mult).then_inc(ya_ready, 1)
                dve.wait_ge(probs, 8 * (l + 1))
                link(dve.reciprocal(stat[:, 40:48], stat[:, 32:40]))
                for t in range(TILES):
                    b = full(dve, l, f"aout{t}")
                    r = stat[:, 40 + 4 * t:44 + 4 * t].unsqueeze(2).to_broadcast([P, HEADS, P])
                    done_reading(dve.tensor_tensor(yc[:, t, :].rearrange("p (h n) -> p h n", h=HEADS),
                                                   b[:, :].rearrange("p (h n) -> p h n", h=HEADS), r, ALU.mult), l, f"aout{t}")

                for n in range(BRANCHES):
                    for half in range(2):
                        for t in range(TILES):
                            name = f"br{n}{half}{t}"
                            b = full(dve, l, name)
                            gate = gates[:, t, n * D + half * 512:n * D + (half + 1) * 512]
                            part = mixsum[:, t, half * 512:(half + 1) * 512]
                            dst = part if n == 0 else gate
                            done_reading(dve.tensor_tensor(dst, b[:, :], gate, ALU.mult), l, name)
                            if n > 0:
                                wait_read(dve, l, name)
                                ins = dve.tensor_tensor(part, part, gate, ALU.add)
                                if n == BRANCHES - 1:
                                    ins.then_inc(mix_done, 1)
                                else:
                                    link(ins)
                for half in range(2):
                    for t in range(TILES):
                        name = f"out{half}{t}"
                        b = full(dve, l, name)
                        part = xs[:, t, half * 512:(half + 1) * 512]
                        done_reading(dve.tensor_tensor(part, part, b[:, :], ALU.add), l, name)

                norm(2 * l + 1, xn)
                gained(l, 1)

                for t in range(TILES):
                    wait_read(dve, l, f"sc{t}3")
                    for n in range(HP):
                        ins = dve.max(out=topv[:, t, n, 0:8], in_=sc[:, t, n, :])
                    link(ins)
                    for n in range(HP):
                        ins = dve.max_index(out=topi[:, t, n, 0:8].bitcast(U32), in_max=topv[:, t, n, 0:8], in_values=sc[:, t, n, :])
                    link(ins)
                    for n in range(HP):
                        ins = dve.match_replace(out=sc[:, t, n, :], in_to_replace=topv[:, t, n, 0:8], in_values=sc[:, t, n, :],
                                                imm_value=TINY)
                    link(ins)
                    for n in range(HP):
                        ins = dve.max(out=topv[:, t, n, 8:16], in_=sc[:, t, n, :])
                    link(ins)
                    for n in range(HP):
                        ins = dve.max_index(out=topi[:, t, n, 8:16].bitcast(U32), in_max=topv[:, t, n, 8:16], in_values=sc[:, t, n, :])
                    link(ins)
                    halves = topv[:, t, :, :].rearrange("p (h s) k -> p h s k", s=2)
                    for h in range(PEER_HEADS):
                        ins = dve.tensor_tensor(cand[:, t, h, :].rearrange("p (a b) -> p a b", a=TOPK),
                                                halves[:, h, 0, :].unsqueeze(2).to_broadcast([P, TOPK, TOPK]),
                                                halves[:, h, 1, :].unsqueeze(1).to_broadcast([P, TOPK, TOPK]), ALU.add)
                    link(ins)
                    for h in range(PEER_HEADS):
                        ins = dve.max(out=bestv[:, t, h, 0:8], in_=cand[:, t, h, :])
                    link(ins)
                    for h in range(PEER_HEADS):
                        ins = dve.max_index(out=bestp[:, t, h, 0:8].bitcast(U32), in_max=bestv[:, t, h, 0:8], in_values=cand[:, t, h, :])
                    link(ins)
                    for h in range(PEER_HEADS):
                        ins = dve.match_replace(out=cand[:, t, h, :], in_to_replace=bestv[:, t, h, 0:8], in_values=cand[:, t, h, :],
                                                imm_value=TINY)
                    link(ins)
                    for h in range(PEER_HEADS):
                        ins = dve.max(out=bestv[:, t, h, 8:16], in_=cand[:, t, h, :])
                    link(ins)
                    dve.tensor_tensor(gate_k[:, t, :, :], bestv[:, t, :, :], bestv[:, t, :, 0:1].to_broadcast([P, PEER_HEADS, TOPK]),
                                      ALU.subtract).then_inc(best_diff, 1)
                    for h in range(PEER_HEADS):
                        ins = dve.max_index(out=bestp[:, t, h, 8:16].bitcast(U32), in_max=bestv[:, t, h, 8:16], in_values=cand[:, t, h, :])
                    link(ins)
                    flat = bestp[:, t, :, :].rearrange("p h k -> p (h k)").bitcast(U32)
                    dve.tensor_scalar(half_pos[:, 0, :].bitcast(U32), flat, 4, None, ALU.logical_shift_right)
                    link(dve.tensor_scalar(half_pos[:, 1, :].bitcast(U32), flat, 15, None, ALU.bitwise_and))
                    dve.tensor_copy(half_f, half_pos.bitcast(U32))
                    link(dve.tensor_copy(topf[:, t, :, :], topi[:, t, :, :].bitcast(U32)))
                    onehot = cand[:, t, :, :].rearrange("p h (k a) -> p h k a", k=TOPK)
                    numbers = topf[:, t, :, :].rearrange("p (h s) k -> p h s k", s=2)
                    for s in range(2):
                        place = half_f[:, s, :].rearrange("p (h k) -> p h k", h=PEER_HEADS).unsqueeze(3)\
                                               .to_broadcast([P, PEER_HEADS, TOPK, TOPK])
                        steps = iota[:, 0:TOPK].unsqueeze(1).unsqueeze(1).to_broadcast([P, PEER_HEADS, TOPK, TOPK])
                        number = numbers[:, :, s, :].unsqueeze(2).to_broadcast([P, PEER_HEADS, TOPK, TOPK])
                        link(dve.tensor_tensor(onehot, place, steps, ALU.is_equal))
                        link(dve.tensor_tensor(onehot, onehot, number, ALU.mult))
                        link(dve.tensor_reduce(pick_ij[:, t, s, :].rearrange("p (h k) -> p h k", h=PEER_HEADS), onehot, AX.X, ALU.add))
                    dve.wait_ge(best_exp, TILES * l + t + 1)
                    link(dve.tensor_reduce(stat[:, 72:80], gate_k[:, t, :, :], AX.X, ALU.add))
                    link(dve.reciprocal(stat[:, 80:88], stat[:, 72:80]))
                    dve.tensor_tensor(gate_k[:, t, :, :], gate_k[:, t, :, :],
                                      stat[:, 80:88].unsqueeze(2).to_broadcast([P, PEER_HEADS, TOPK]), ALU.mult).then_inc(picked, 1)

                dve.wait_ge(picked, TILES * (l + 1))
                dve.wait_ge(products_done, plan.base[l, "seed"] + 4)
                link(dve.memset(arena[:, AHEAD * S:KEYS * S], 1.0))
                wait_read(dve, l, "gT")

                def one_hots(i, g):
                    for m in range(4):
                        if g > 0:
                            dve.wait_ge(products_done, i * (5 * TURN) + (plan.token_index(l, g - 1, m) + 1))
                        tok = lambda ap: ap[:, bass.ds(i * (4 * TURN) + 4 * g + m, 1)]
                        dve.tensor_scalar(hot[:, 0, m, :], iota, tok(IT), tok(gT), ALU.is_equal, ALU.mult)
                    dve.tensor_tensor(hot[:, 1, :, :], iota.unsqueeze(1).to_broadcast([P, 4, P]),
                                      JT[:, bass.ds(i * (4 * TURN) + 4 * g, 4)].unsqueeze(2).to_broadcast([P, 4, P]),
                                      ALU.is_equal).then_inc(hot_ready, 1)

                def gates_into(i, g):
                    dve.wait_ge(products_done, i * (5 * TURN) + (plan.token_index(l, g, 3) + 1))
                    if g > 0:
                        dve.wait_ge(gates_in, i * TURN + (GROUPS * l + g))
                    part = G[:, :, bass.ds(i * (4 * TURN) + 4 * g, 4)]
                    dve.tensor_tensor(part, part, bank[4 + g % 2][:, :].rearrange("p (t j) -> p j t", t=4),
                                      ALU.mult).then_inc(gates_in, 1)

                def gelu_column(i, j):
                    dve.wait_ge(gelu_done, i * TURN + (KEYS * l + j + 1))
                    part = G[:, bass.ds(i * TURN + j, 1), :].rearrange("p a t -> p (a t)")
                    dve.tensor_tensor(part, part, bank[6 + j % 2][:, S:2 * S], ALU.mult).then_inc(gelu_in, 1)

                def group(i, g):
                    one_hots(i, g)
                    if g > 0:
                        gates_into(i, g - 1)
                        dve.wait_ge(gates_in, i * TURN + (GROUPS * l + g))
                        gelu_column(i, AHEAD + g - 1)
                        dve.wait_ge(gelu_in, i * TURN + (GATED * l + g))

                dve.wait_ge(gelu_done, KEYS * l + AHEAD)
                columns(dve, 0, GROUPS, group, straight=TURN)
                gates_into(0, GROUPS - 1)
                dve.wait_ge(gates_in, GROUPS * (l + 1))
                columns(dve, AHEAD + GROUPS - 1, KEYS, gelu_column)

                def lower_v(i, j):
                    n = l * ITEMS + V_ITEM + j // 2
                    k = (V_UNIT + j) % PARTS
                    dve.wait_ge(upper_ready, i * TURN + (UNITS * l + V_UNIT + j + 1))
                    dve.tensor_tensor(lower[:, k, :], ring[:, n % SLOTS, (j % 2) * D:(j % 2 + 1) * D],
                                      upper[:, k, :].bitcast(F32), ALU.subtract).then_inc(v_ready, 1)

                def v_column(i, j):
                    dve.wait_ge(w_upper_ready, i * TURN + (KEYS * l + j + 1))
                    dve.tensor_tensor(w_lower[:, j % 2, :], G[:, bass.ds(i * TURN + j, 1), :].rearrange("p a t -> p (a t)"),
                                      w_upper[:, j % 2, :].bitcast(F32), ALU.subtract).then_inc(w_ready, 1)
                    if 2 <= j < KEYS - 1:
                        lower_v(i, j + 1)

                for j in range(PARTS):
                    lower_v(0, j)
                columns(dve, 0, KEYS, v_column, straight=2, tail=1)
                dve.wait_ge(products_done, plan.v_index(l, KEYS - 1) + 1)
                for half in range(2):
                    for t in range(TILES):
                        dve.tensor_copy(xs[:, t, half * 512:(half + 1) * 512], bank[2 * half + t][:, :])\
                           .then_inc(read["x_done"], 1)

            norm(2 * LAYERS, xfin)
            dve.wait_ge(layer_in, 80 * LAYERS + 16)
            for t in range(TILES):
                dve.tensor_tensor(xfin[:, t, :], xfin[:, t, :], frow, ALU.mult).then_inc(final_out, 1)


def _blocks_of_w_in(w_in):
    names = ["aq", "af", "ai", "ag", "bu", "bv", "cq", "ck", "cv", "iq"]
    blocks = {n: w_in[:, :, k * W:(k + 1) * W] for k, n in enumerate(names)}
    at = len(names) * W
    blocks["small"] = w_in[:, :, at:at + SMALL_COLS]
    for n in range(6):
        blocks[f"gate{n}"] = w_in[:, :, at + SMALL_COLS + n * W:at + SMALL_COLS + (n + 1) * W]
    return blocks


def _rows_to_partitions(w):
    layers, rows, columns = w.shape
    return w.reshape(layers, rows // P, P, columns).transpose(0, 2, 1, 3).reshape(layers, P, -1)


def kernel(**inputs):
    import numpy as _np
    import concourse.bacc as _bacc
    from concourse import mybir as _mybir
    from concourse.bass_utils import run_bass_kernel_spmd as _run

    a = {n: _np.asarray(v) for n, v in inputs.items()}
    blocks = _blocks_of_w_in(a["w_in"])
    stream = _np.empty((LAYERS, ITEMS, P, ITEM), _np.float32)

    def put(name, w):
        columns = w.shape[2]
        if name in BY_COLUMN:
            parts = [_np.concatenate([_rows_to_partitions(w[:, :, m * P:(m + 1) * P]) for m in (2 * q, 2 * q + 1)], 2)
                     for q in range(2)]
        elif name[:2] == "br":
            parts = [_rows_to_partitions(w[:, :, q * columns // 2:(q + 1) * columns // 2]) for q in range(2)]
        else:
            parts = [_rows_to_partitions(w[:, q * D // 2:(q + 1) * D // 2]) for q in range(2)]
        for q in range(2):
            stream[:, FIRST[name] + q] = parts[q]

    for name in BLOCKS:
        put(name, blocks[name])
    for n in range(BRANCHES):
        put(f"br{n}", a["w_branch"][:, n])
    for n in range(2):
        put(f"out{n}", a["w_out"][:, :, n * W:(n + 1) * W])
    for n in range(4):
        put(f"qry{n}", a["peer_w_q"][:, :, n * W:(n + 1) * W])
    stream[:, KEY_ITEM] = a["peer_sub_keys"].transpose(0, 4, 1, 2, 3).reshape(LAYERS, P, HP * KEYS)
    u = a["peer_u"].reshape(LAYERS, KEYS, KEYS // 2, 2, KC, P).transpose(0, 2, 5, 3, 4, 1)
    stream[:, U_ITEM:V_ITEM] = u.reshape(LAYERS, KEYS // 2, P, ITEM)
    v = a["peer_v"].reshape(LAYERS, KEYS, KEYS // 2, 2 * D).transpose(0, 2, 1, 3)
    stream[:, V_ITEM:] = v

    half_c, half_i = P // 2, IDX_DIM // 2
    inv = lambda half: (10000.0 ** (-_np.arange(half, dtype=_np.float32) / _np.float32(half)).astype(_np.float64))\
        .astype(_np.float32)
    consts = _np.zeros((P, 2 * P + 96), _np.float32)
    consts[:, 0:P] = _np.eye(P)
    consts[:, P:2 * P] = _np.arange(P)
    consts[:, 2 * P:] = _np.concatenate([inv(half_c), inv(half_i)])
    s, t = _np.meshgrid(_np.arange(P), _np.arange(P), indexing="ij")
    masks = _np.stack([(s // (2 * h) == t // (2 * h)) & (s % (2 * h) < h) & (t % (2 * h) >= h) for h in HALVES], 1)

    gains = _np.stack([a["norm1_gain"], a["norm2_gain"]], 1)
    arrays = {
        "x": a["x"].reshape(S, D),
        "pos": a["positions"].reshape(TILES, P).T,
        "stream": stream.reshape(LAYERS * ITEMS, P, ITEM),
        "small": _rows_to_partitions(blocks["small"]),
        "wsT": a["gmlp_w_s"].transpose(0, 3, 1, 2).reshape(LAYERS, P, HEADS * P),
        "bsT": a["gmlp_b_s"].transpose(0, 2, 1),
        "cols": gains.reshape(2 * LAYERS, KC, P).transpose(2, 0, 1).reshape(P, 2 * LAYERS * KC),
        "lbl": a["hgrn_lb_logits"].reshape(LAYERS, HEADS, P).transpose(2, 0, 1).reshape(P, LAYERS * HEADS),
        "hgain": a["hgrn_norm_gain"],
        "ggain": a["gmlp_norm_gain"],
        "fgain": a["final_gain"].reshape(1, D),
        "consts": consts,
        "masks": masks.astype(_np.float32).reshape(P, NLEV * P),
    }
    nc = _bacc.Bacc("TRN2", target_bir_lowering=False, num_devices=1)
    args = []
    for name, v in arrays.items():
        arrays[name] = v = _np.ascontiguousarray(v)
        args.append(nc.dram_tensor(f"{name}_dram", v.shape, _mybir.dt.from_np(v.dtype), kind="ExternalInput").ap())
    args.append(nc.dram_tensor("out_dram", (S, D), F32, kind="ExternalOutput").ap())
    trunk_kernel(nc, *args)
    r = _run(nc, [{f"{n}_dram": v for n, v in arrays.items()}], core_ids=[0])
    return r.results[0]["out_dram"].reshape(1, S, D)
```

```python
import numpy as np
import concourse.bass as bass
from concourse import mybir
from contextlib import ExitStack

F32 = mybir.dt.float32
F32R = mybir.dt.float32r
I32 = mybir.dt.int32
U32 = mybir.dt.uint32
U8 = mybir.dt.uint8
ALU = mybir.AluOpType
ACT = mybir.ActivationFunctionType
AX = mybir.AxisListType

P = 128
LAYERS = 2
D = 1024
S = 256
TILES = S // P
KC = D // P
HEADS = 4
W = HEADS * P
IDX_HEADS, IDX_DIM = 8, 64
BRANCHES = 3
CHUNK = 64
EPS = 1e-6
DSA_TOPK = min(256, S // 4)
PEER_HEADS, KEYS, TOPK = 8, 128, 16
HP = PEER_HEADS * 2
CAND = TOPK * TOPK
PICKS = PEER_HEADS * TOPK

BLOCKS = ["iq", "cq", "ck", "af", "aq", "ag", "ai", "cv", "bu", "bv"] + [f"gate{n}" for n in range(6)]
BY_COLUMN = ("af", "aq", "qry0", "qry1", "qry2", "qry3")
HEAD = BLOCKS + [f"br{n}" for n in range(BRANCHES)] + ["out0", "out1"] + [f"qry{n}" for n in range(4)]
FIRST = {name: 2 * n for n, name in enumerate(HEAD)}
KEY_ITEM = 2 * len(HEAD)
U_ITEM = KEY_ITEM + 1
V_ITEM = U_ITEM + KEYS // 2
ITEMS = V_ITEM + KEYS // 2
SLOTS = 3
ITEM = 2048

U_UNIT = 2 * KEY_ITEM
V_UNIT = U_UNIT + KEYS
UNITS = V_UNIT + KEYS
PARTS = 3


def item_of(k):
    return k // 2 + (k >= U_UNIT)


def slot_of(l, k):
    return (l * UNITS + k) % PARTS


TURN = 12
AHEAD = 60
GROUPS = S // 4
GATED = KEYS - AHEAD
PICKED = AHEAD - TURN
EXPS = (TURN, 3 * TURN)
assert TURN % (2 * SLOTS) == 0 and TURN % PARTS == 0
assert AHEAD % TURN == 0 and EXPS[1] <= PICKED and GATED > GROUPS

HALVES = [64, 32, 16, 8, 4, 2, 1]
NLEV = len(HALVES)

NEG = -1.0e38
MARK = -3.0e38
MASKED = -1.0e30
TINY = -3.0e38

SMALL_COLS = IDX_DIM + IDX_HEADS


class Plan:

    def __init__(self, sems):
        self.sems = sems
        self.n = 0
        self.turn = {"wide": 0, "side": 0, "gates": 0}
        self.last = [None] * 8
        self.reads = {}
        self.index, self.bank, self.read, self.before, self.base = {}, {}, {}, {}, {}
        for l in range(LAYERS):
            self.layer(l)

    def add(self, banks, l, signal, *names):
        for name in names:
            those = {"wide": (0, 1, 2, 3), "side": (4, 5, 6, 7), "gates": (4, 5)}[banks]
            b = those[self.turn[banks] % len(those)]
            self.turn[banks] += 1
            self.reads[signal] = self.reads.get(signal, 0) + 1
            self.index[l, name], self.bank[l, name] = self.n, b
            self.read[l, name] = (self.sems[signal], self.reads[signal])
            self.before[l, name] = self.last[b]
            self.last[b] = (l, name)
            self.n += 1

    def block(self, l, signal, *names):
        for name in names:
            by_column = name in BY_COLUMN
            if by_column:
                for q in range(2):
                    self.index[l, f"{name}.{2 * q}"] = self.n
                    self.n += 1
                    self.add("wide", l, signal, f"{name}{q}")
            elif name == "out1":
                self.index[l, f"{name}.0"] = self.n
                self.n += 1
                self.add("wide", l, signal, f"{name}0")
                for step in (1, 2):
                    self.index[l, f"{name}.{step}"] = self.n
                    self.n += 1
                self.add("wide", l, signal, f"{name}1")
            else:
                for step in range(3):
                    self.index[l, f"{name}.{step}"] = self.n
                    self.n += 1
                self.add("wide", l, signal, f"{name}0", f"{name}1")

    def layer(self, l):
        side = lambda signal, *names: self.add("side", l, signal, *names)
        wide = lambda signal, *names: self.add("wide", l, signal, *names)
        side("hT_ready", "n1.00", "n1.01", "n1.10", "n1.11")
        self.block(l, "roped", "iq")
        side("roped", "small0", "small1")
        self.block(l, "roped", "cq", "ck")
        self.block(l, "blocks_out", "af", "aq")
        side("idxT_out", "iqT0", "iqT1", "ikT")
        self.block(l, "blocks_out", "ag", "ai")
        side("relued", *[f"logit{t}{n}" for t in range(TILES) for n in range(4)])
        side("attnT_out", "cqT0", "cqT1", "ckT0", "ckT1")
        self.block(l, "blocks_out", "cv", "bu", "bv", "gate0", "gate1")
        side("pairs_out", "diag0", "diag1")
        side("cross_out", "cross")
        for k in range(NLEV):
            if k in (1, 3, 5):
                self.block(l, "blocks_out", f"gate{2 + k // 2}")
            side("pairs_out", f"lev{k}0", f"lev{k}1")
        side("masked", "att00", "att01", "att10", "att11")
        side("yb_out", "mix0", "mix1")
        side("o_out", "hout0", "hout1")
        self.block(l, "blocks_out", "gate5")
        side("pT_out", "pT0", "pT10", "pT11")
        side("yT_out", *[f"y{n}{t}" for n in range(BRANCHES - 1) for t in range(TILES)])
        side("yc_out", "aout0", "aout1")
        for n in range(BRANCHES):
            for half in range(2):
                self.index[l, f"br{n}{half}.0"] = self.n
                self.n += 1
                wide("gated", *[f"br{n}{half}{t}" for t in range(TILES)])
            if n == 0:
                side("yT_out", *[f"y{BRANCHES - 1}{t}" for t in range(TILES)])
        side("mT_out", "mT00", "mT01", "mT10", "mT11")
        self.block(l, "x_done", "out0", "out1")
        side("hT_ready", "n2.00", "n2.01", "n2.10", "n2.11")
        self.block(l, "qry_out", *[f"qry{n}" for n in range(4)])
        self.base[l, "seed"] = self.n
        self.n += 4
        side("sc_out", *[f"sc{t}{n}" for t in range(TILES) for n in range(4)])
        self.base[l, "U"] = self.n
        self.n += PICKED
        self.add("gates", l, "picksT_out", "IJT", "gT")
        self.n += AHEAD - PICKED
        self.base[l, "G"] = self.n
        self.n += 5 * GROUPS
        self.base[l, "T"] = self.n
        self.n += GATED - GROUPS
        self.base[l, "V"] = self.n
        self.n += KEYS
        self.reads["x_done"] += 4

    def last_of(self, l, b):
        return max((index, n) for n, index in self.index.items() if n[0] == l and self.bank.get(n) == b)[1]

    def token_index(self, l, g, m):
        return self.base[l, "G"] + 5 * g + m

    def u_index(self, l, j):
        if j < AHEAD:
            return self.base[l, "U"] + j + (2 if j >= PICKED else 0)
        if j < AHEAD + GROUPS:
            return self.base[l, "G"] + 5 * (j - AHEAD) + 4
        return self.base[l, "T"] + j - AHEAD - GROUPS

    def v_index(self, l, j):
        return self.base[l, "V"] + j

    def unit_step(self, l, k):
        if k >= V_UNIT:
            return self.v_index(l, k - V_UNIT)
        if k >= U_UNIT:
            return self.u_index(l, k - U_UNIT)
        name, u = HEAD[k // 4], k % 4
        if name[:2] == "br":
            return self.index[l, f"{name}{u // 2}" + ("1" if u % 2 else ".0")]
        if name in BY_COLUMN:
            return self.index[l, f"{name}{u // 2}" if u % 2 else f"{name}.{u}"]
        return self.index[l, f"{name}1" if u == 3 else f"{name}.{u}"]


def trunk_kernel(nc, x, pos, stream, small, wsT, bsT, cols, lbl, hgain, ggain, fgain, consts, masks, out):
    ctx = ExitStack()
    with ctx:
        def sb(name, shape, dt=F32):
            return ctx.enter_context(nc.sbuf_tensor(name, shape, dt))

        def sem(name):
            return ctx.enter_context(nc.semaphore(name))

        ring = sb("ring", [P, SLOTS, ITEM])
        upper = sb("upper", [P, PARTS, D], F32R)
        lower = sb("lower", [P, PARTS, D], F32R)
        hT_upper = sb("hT_upper", [P, KC * S], F32R)
        hT_lower = sb("hT_lower", [P, KC * S], F32R)
        w_upper = sb("w_upper", [P, 2, S], F32R)
        w_lower = sb("w_lower", [P, 2, S], F32R)
        const = sb("const", [P, 2 * P + 96])
        ident, iota, freq = const[:, 0:P], const[:, P:2 * P], const[:, 2 * P:]
        mask = sb("mask", [P, NLEV, P], U8)
        zero64 = sb("zero64", [P, CHUNK])
        trig = sb("trig", [P, 2, TILES, 96])
        gcol = sb("gcol", [P, 2 * LAYERS, KC])
        lb = sb("lb", [P, 8, HEADS])
        stat = sb("stat", [P, 96])
        picks = sb("picks", [P, 3, S])
        hot = sb("hot", [P, 2, 4, P])
        IT, JT, gT = picks[:, 0, :], picks[:, 1, :], picks[:, 2, :]

        arena = sb("arena", [P, KEYS * S])
        G = arena[:, :].rearrange("p (j t) -> p j t", j=KEYS)
        at = [0]

        def take(n):
            at[0] += n
            assert at[0] <= KEYS * S
            return arena[:, at[0] - n:at[0]]

        def tiles(ap):
            return ap.rearrange("p (t n) -> p t n", t=TILES)

        mixer = {n: tiles(take(W * TILES)) for n in ("iq", "ck", "cq", "ag", "ai", "cv", "bu", "bv")}
        gates = take(BRANCHES * D * TILES).rearrange("p (t n) -> p t n", t=TILES)
        xn = tiles(take(D * TILES))
        mixsum = xn
        zT = take(HEADS * S)
        qs = take(HEADS * S)
        key = take(HEADS * S)
        logf = take(HEADS * S)
        bcum = take(HEADS * S)
        lev = [take(HEADS * S), zT, logf]
        pairs = take(TILES * W)
        pairT = pairs.rearrange("p (t h n) -> p t h n", t=TILES, h=HEADS)
        iqT = pairs.rearrange("p (b t) -> p b t", b=4)
        crossT = take(W).rearrange("p (h n) -> p h n", h=HEADS)
        tmp = take(2 * W)
        cqT = take(HEADS * S).rearrange("p (h t) -> p h t", h=HEADS)
        ckT = take(HEADS * S).rearrange("p (h t) -> p h t", h=HEADS)
        ikT = take(S)
        ikn = xn[:, :, 0:P]
        wi = tiles(take(TILES * IDX_HEADS))
        score = tiles(take(TILES * S))
        top8 = take(16)
        wsmall = hot[:, :, :, :].rearrange("p a b c -> p (a b c)")[:, 0:KC * SMALL_COLS].rearrange("p (c n) -> p c n", c=KC)
        ws = picks[:, :, :].rearrange("p a t -> p (a t)")[:, 0:HEADS * P].rearrange("p (g t) -> p g t", g=HEADS)
        bs = take(HEADS)
        hrow = take(P)
        grow = take(W)
        xs = tiles(take(TILES * D))
        hT = take(KC * S).rearrange("p (c t) -> p c t", c=KC)
        prob = arena[:, 0:2 * W * TILES].rearrange("p (t h n) -> p t h n", t=TILES, h=HEADS)
        pT0 = cqT.rearrange("p h t -> p (h t)")[:, 0:W].rearrange("p (h n) -> p h n", h=HEADS)
        pT1 = tmp.rearrange("p (h b n) -> p h b n", h=HEADS, b=2)
        AT_YT = [0, HEADS * S, 0]
        AT_MT = [HEADS * S, 0]
        oh = lev[0].rearrange("p (t n) -> p t n", t=TILES)
        osq = lev[1].rearrange("p (t n) -> p t n", t=TILES)
        yc = mixer["cq"]

        at[0] = AHEAD * S
        qryT = take(HP * S).rearrange("p (n t) -> p n t", n=HP)
        sc = take(TILES * HP * KEYS).rearrange("p (t n k) -> p t n k", t=TILES, n=HP)
        topv = take(TILES * HP * TOPK).rearrange("p (t n k) -> p t n k", t=TILES, n=HP)
        topi = take(TILES * HP * TOPK).rearrange("p (t n k) -> p t n k", t=TILES, n=HP)
        topf = take(TILES * HP * TOPK).rearrange("p (t n k) -> p t n k", t=TILES, n=HP)
        cand = take(TILES * PEER_HEADS * CAND).rearrange("p (t h n) -> p t h n", t=TILES, h=PEER_HEADS)
        bestv = take(TILES * PICKS).rearrange("p (t h k) -> p t h k", t=TILES, h=PEER_HEADS)
        bestp = take(TILES * PICKS).rearrange("p (t h k) -> p t h k", t=TILES, h=PEER_HEADS)
        half_pos = take(2 * PICKS).rearrange("p (b n) -> p b n", b=2)
        half_f = take(2 * PICKS).rearrange("p (b n) -> p b n", b=2)
        assert AHEAD * S + 2 * HP * S <= KEYS * S - TILES * D - KC * S
        flat_hot = hot[:, :, :, :].rearrange("p a b c -> p (a b c)")
        pick_ij = flat_hot[:, 0:TILES * 2 * PICKS].rearrange("p (t b n) -> p t b n", t=TILES, b=2)
        gate_k = flat_hot[:, TILES * 2 * PICKS:TILES * 3 * PICKS].rearrange("p (t h k) -> p t h k", t=TILES, h=PEER_HEADS)
        frow = flat_hot[:, 0:D]
        xfin = xn

        bank = [ctx.enter_context(nc.psum_tensor(f"bank{b}", [P, 512], F32)) for b in range(8)]

        const_in = sem("const_in")
        table_in = sem("table_in")
        x_in = sem("x_in")
        layer_in = sem("layer_in")
        ws_causal = sem("ws_causal")
        arrived = [sem(f"arrived{s}") for s in range(SLOTS)]
        products_done = sem("products_done")
        read = {n: sem(n) for n in (
            "hT_ready", "roped", "blocks_out", "idxT_out", "relued", "attnT_out", "pairs_out", "cross_out", "masked",
            "yb_out", "pT_out", "o_out", "yc_out", "yT_out", "gated", "mT_out", "x_done", "qry_out", "sc_out",
            "picksT_out")}
        plan = Plan(read)
        squares = sem("squares")
        meansq = sem("meansq")
        roots = sem("roots")
        xn_ready = sem("xn_ready")
        trig_in = sem("trig_in")
        trig_out = sem("trig_out")
        lb_in = sem("lb_in")
        lb_out = sem("lb_out")
        relu_used = sem("relu_used")
        soft_in = sem("soft_in")
        soft_out = sem("soft_out")
        decay_arg = sem("decay_arg")
        decay_exp = sem("decay_exp")
        decayed = sem("decayed")
        vsq = sem("vsq")
        vms = sem("vms")
        vroot = sem("vroot")
        v_normed = sem("v_normed")
        neg_max = sem("neg_max")
        probs = sem("probs")
        oms = sem("oms")
        oroot = sem("oroot")
        ya_ready = sem("ya_ready")
        mix_done = sem("mix_done")
        best_diff = sem("best_diff")
        best_exp = sem("best_exp")
        hT_upper_ready = sem("hT_upper_ready")
        hT_split = sem("hT_split")
        T_upper_ready = sem("T_upper_ready")
        picked = sem("picked")
        hot_ready = sem("hot_ready")
        gates_in = sem("gates_in")
        upper_ready = sem("upper_ready")
        lower_ready = sem("lower_ready")
        v_ready = sem("v_ready")
        gelu_done = sem("gelu_done")
        gelu_in = sem("gelu_in")
        w_upper_ready = sem("w_upper_ready")
        w_ready = sem("w_ready")
        dve_chain = sem("dve_chain")
        act_chain = sem("act_chain")
        final_out = sem("final_out")
        stored = sem("stored")

        block = ctx.enter_context(nc.Block())

        def full(eng, l, name):
            eng.wait_ge(products_done, plan.index[l, name] + 1)
            return bank[plan.bank[l, name]]

        def columns(eng, start, end, body, straight=0, tail=0):
            for n in range(start, start + straight):
                body(0, n)
            first = start + straight
            turns = (end - tail - first) // TURN
            if turns:
                with eng.Fori(0, turns) as i:
                    for n in range(first, first + TURN):
                        body(i, n)
            for n in range(first + TURN * turns, end):
                body(0, n)

        def tile_of(parts, at, t):
            return parts[:, at:at + 4 * S].rearrange("p (c t) -> p c t", c=4)[:, :, t * P:(t + 1) * P]

        def quarter(parts, t, half):
            return tile_of(parts, half * 4 * S, t)

        def done_reading(ins, l, name):
            ins.then_inc(plan.read[l, name][0], 1)

        def wait_read(eng, l, name):
            eng.wait_ge(*plan.read[l, name])

        @block.sync
        def _(sp):
            for t in range(TILES):
                sp.dma_start(xs[:, t, :], x[t * P:(t + 1) * P, :]).then_inc(x_in, 16)
            sp.dma_start(const[:, :], consts).then_inc(const_in, 16)
            sp.dma_start(gcol[:, :, :].rearrange("p n c -> p (n c)"), cols).then_inc(const_in, 16)

            def load(l, item, wait, i=None):
                if wait:
                    sp.wait_ge(*wait)
                n = l * ITEMS + item
                src = stream[n, :, :] if i is None else \
                    stream[bass.ds(i * SLOTS + n, 1), :, :].rearrange("a p n -> p (a n)")
                sp.dma_start(ring[:, n % SLOTS, :], src).then_inc(arrived[n % SLOTS], 16)

            def split_done(l, item, i=None):
                if item >= V_ITEM:
                    ready, value = v_ready, KEYS * l + 2 * (item - V_ITEM) + 2
                elif item >= U_ITEM:
                    ready, value = lower_ready, V_UNIT * l + U_UNIT + 2 * (item - U_ITEM) + 2
                else:
                    ready, value = lower_ready, V_UNIT * l + 2 * item + 2
                return ready, value if i is None else i * (2 * SLOTS) + value

            for l in range(LAYERS):
                for item in range(U_ITEM + SLOTS):
                    if item - SLOTS == KEY_ITEM:
                        wait = (products_done, plan.index[l, f"sc{TILES - 1}3"] + 1)
                    elif item >= SLOTS:
                        wait = split_done(l, item - SLOTS)
                    elif l > 0:
                        wait = split_done(l - 1, ITEMS - SLOTS + item)
                    else:
                        wait = None
                    load(l, item, wait)
                for first in (U_ITEM, V_ITEM):
                    last = min(first + KEYS // 2, ITEMS - SLOTS)
                    turns = (last - first) // SLOTS
                    with sp.Fori(0, turns) as i:
                        for m in range(SLOTS):
                            load(l, first + SLOTS + m, split_done(l, first + m, i), i)
                    for item in range(first + SLOTS * turns, last):
                        load(l, item + SLOTS, split_done(l, item))
            for t in range(TILES):
                sp.wait_ge(final_out, t + 1)
                sp.dma_start(out[t * P:(t + 1) * P, :], xfin[:, t, :]).then_inc(stored, 16)
            sp.wait_ge(stored, 16 * TILES)

        @block.gpsimd
        def _(pool):
            pool.dma_start(stat[:, 92:94].bitcast(I32), pos).then_inc(table_in, 16)
            pool.dma_start(lb[:, 0:2, :].rearrange("p n h -> p (n h)"), lbl).then_inc(table_in, 16)
            pool.dma_start(lev[0][:, 0:NLEV * P], masks).then_inc(table_in, 16)
            for l in range(LAYERS):
                if l > 0:
                    pool.wait_ge(read["x_done"], 8 * l)
                pool.dma_start(wsmall.rearrange("p c n -> p (c n)"), small[l]).then_inc(layer_in, 16)
                pool.dma_start(ws.rearrange("p g t -> p (g t)"), wsT[l]).then_inc(layer_in, 16)
                pool.dma_start(bs, bsT[l]).then_inc(layer_in, 16)
                pool.dma_start(hrow, hgain[l:l + 1, :].to_broadcast([P, P])).then_inc(layer_in, 16)
                pool.dma_start(grow, ggain[l:l + 1, :].to_broadcast([P, W])).then_inc(layer_in, 16)

                def lower_part(i, k):
                    n = l * ITEMS + item_of(k)
                    pool.wait_ge(upper_ready, i * TURN + (UNITS * l + k + 1))
                    pool.tensor_tensor(lower[:, slot_of(l, k), :], ring[:, n % SLOTS, (k % 2) * D:(k % 2 + 1) * D],
                                       upper[:, slot_of(l, k), :].bitcast(F32), ALU.subtract).then_inc(lower_ready, 1)

                for k in range(U_UNIT):
                    lower_part(0, k)
                    if k == 2 * FIRST["af"] - 1:
                        pool.wait_ge(layer_in, 80 * (l + 1))
                        pool.affine_select(out=ws, in_=ws, pattern=[[0, HEADS], [1, P]], compare_op=ALU.is_ge,
                                           fill=0.0, base=0, channel_multiplier=-1).then_inc(ws_causal, 1)
                columns(pool, 0, KEYS, lambda i, j: lower_part(i, U_UNIT + j))
            pool.wait_ge(products_done, plan.token_index(LAYERS - 1, GROUPS - 1, 3) + 1)
            pool.dma_start(frow, fgain.to_broadcast([P, D])).then_inc(layer_in, 16)

        @block.tensor
        def _(pe):
            done = [0]

            def begin(l, name):
                assert plan.index[l, name] == done[0], (name, done[0])
                done[0] += 1
                if plan.before[l, name]:
                    wait_read(pe, *plan.before[l, name])
                return bank[plan.bank[l, name]]

            def item_in(l, item):
                n = l * ITEMS + item
                pe.wait_ge(arrived[n % SLOTS], 16 * (n // SLOTS + 1))
                return ring[:, n % SLOTS, :]

            def begin_at(l, name):
                if plan.before[l, name]:
                    wait_read(pe, *plan.before[l, name])
                return bank[plan.bank[l, name]]

            def finish(l, name, mm):
                assert plan.index[l, name] == done[0], (name, done[0])
                done[0] += 1
                mm.then_inc(products_done, 1)

            def step_done(l, name, step, mm):
                assert plan.index[l, f"{name}.{step}"] == done[0]
                done[0] += 1
                mm.then_inc(products_done, 1)

            WEIGHT_BY_H = ((upper, hT_upper), (upper, hT_lower), (lower, hT_upper))
            H_BY_WEIGHT = ((hT_upper, upper), (hT_upper, lower), (hT_lower, upper))

            def unit_in(l, k):
                pe.wait_ge(lower_ready, V_UNIT * l + k + 1)
                return slot_of(l, k)

            def transposes(l, name, sources):
                b = begin(l, name)
                for n, src in enumerate(sources):
                    mm = pe.transpose(b[:, n * P:(n + 1) * P], src, ident)
                mm.then_inc(products_done, 1)

            def norm_transposes(l, which):
                for t in range(TILES):
                    pe.wait_ge(xn_ready, TILES * (2 * l + which) + t + 1)
                    for half in range(2):
                        transposes(l, f"n{which + 1}.{t}{half}",
                                   [xn[:, t, (4 * half + c) * P:(4 * half + c + 1) * P] for c in range(4)])

            def split_by_token(l, name, first, units, source, tile_in=None, before_unit=lambda u: None):
                opened = [begin_at(l, f"{name}{t}") for t in range(TILES)]
                for u in range(units):
                    k = unit_in(l, first + u)
                    before_unit(u)
                    for t in range(TILES):
                        if u == 0 and tile_in:
                            pe.wait_ge(hT_split, tile_in + t)
                        mm = unit_products(opened[t], k, u, units, t, source)
                        if u == units - 1:
                            finish(l, f"{name}{t}", mm)
                    if u < units - 1:
                        step_done(l, name, u, mm)

            def unit_products(b, k, u, units, t, source):
                for c in range(2):
                    at_h = source(2 * u + c) + t * P
                    for n, (h, w) in enumerate(H_BY_WEIGHT):
                        mm = pe.matmul(b[:, :], h[:, at_h:at_h + P], w[:, k, c * W:(c + 1) * W],
                                       start=(u == 0 and c == 0 and n == 0), stop=(u == units - 1 and c == 1 and n == 2))
                return mm

            def split_last_block(l, name, source):
                opened = [begin_at(l, f"{name}{t}") for t in range(TILES)]
                for t in range(TILES):
                    mm = unit_products(opened[t], unit_in(l, 2 * FIRST[name]), 0, 4, t, source)
                step_done(l, name, 0, mm)
                for t in range(TILES):
                    for u in range(1, 4):
                        mm = unit_products(opened[t], unit_in(l, 2 * FIRST[name] + u), u, 4, t, source)
                        if t > 0 and u < 3:
                            step_done(l, name, u, mm)
                    finish(l, f"{name}{t}", mm)

            def split_block_by_token(l, name, tile_in=None):
                split_by_token(l, name, 2 * FIRST[name], 4, lambda c: c * S, tile_in)

            def split_block_by_column(l, name):
                for pair in range(2):
                    b = begin_at(l, f"{name}{pair}")
                    for m in range(2):
                        k = unit_in(l, 2 * FIRST[name] + 2 * pair + m)
                        for c in range(KC):
                            for n, (w, h) in enumerate(WEIGHT_BY_H):
                                mm = pe.matmul(b[:, m * S:(m + 1) * S], w[:, k, c * P:(c + 1) * P], h[:, c * S:(c + 1) * S],
                                               start=(c == 0 and n == 0), stop=(c == KC - 1 and n == 2))
                        if m == 0:
                            step_done(l, name, 2 * pair, mm)
                    finish(l, f"{name}{pair}", mm)

            for l in range(LAYERS):
                if l == 0:
                    pe.wait_ge(const_in, 16 * 2)
                norm_transposes(l, 0)
                split_block_by_token(l, "iq", tile_in=2 * TILES * l + 1)
                pe.wait_ge(layer_in, 80 * (l + 1))
                for t in range(TILES):
                    b = begin(l, f"small{t}")
                    for c in range(KC):
                        mm = pe.matmul(b[:, 0:SMALL_COLS], hT[:, c, t * P:(t + 1) * P], wsmall[:, c, :],
                                       start=(c == 0), stop=(c == KC - 1))
                    mm.then_inc(products_done, 1)
                split_block_by_token(l, "cq")
                split_block_by_token(l, "ck")
                split_block_by_column(l, "af")
                split_block_by_column(l, "aq")
                for t in range(TILES):
                    wait_read(pe, l, f"iq{t}")
                    transposes(l, f"iqT{t}", [mixer["iq"][:, t, n * P:(n + 1) * P] for n in range(4)])
                wait_read(pe, l, "small1")
                transposes(l, "ikT", [ikn[:, t, :] for t in range(TILES)])
                split_block_by_token(l, "ag")
                split_block_by_token(l, "ai")
                wait_read(pe, l, "ikT")
                for t in range(TILES):
                    keys = (t + 1) * P
                    for n in range(4):
                        b = begin(l, f"logit{t}{n}")
                        odd, first = n % 2, 4 * (n // 2)
                        rows = slice(IDX_DIM * odd, IDX_DIM * (odd + 1))
                        for m in range(2):
                            head = first + 2 * m + odd
                            mm = pe.matmul(b[:, m * S:m * S + keys], iqT[rows, head // 2, t * P:(t + 1) * P],
                                           ikT[rows, 0:keys], start=True, stop=True)
                        mm.then_inc(products_done, 1)
                for name in ("cq", "ck"):
                    for t in range(TILES):
                        wait_read(pe, l, f"{name}{t}")
                        transposes(l, f"{name}T{t}", [mixer[name][:, t, h * P:(h + 1) * P] for h in range(HEADS)])
                split_block_by_token(l, "cv")
                split_block_by_token(l, "bu")
                split_block_by_token(l, "bv")
                split_block_by_token(l, "gate0")
                split_block_by_token(l, "gate1")
                head = lambda ap, h, t: ap[:, h * S + t * P:h * S + (t + 1) * P]
                pe.wait_ge(decayed, (NLEV + 2) * l + 1)
                for t in range(TILES):
                    b = begin(l, f"diag{t}")
                    for h in range(HEADS):
                        mm = pe.matmul(b[:, h * P:(h + 1) * P], head(key, h, t), head(qs, h, t), start=True, stop=True)
                    mm.then_inc(products_done, 1)
                pe.wait_ge(decayed, (NLEV + 2) * l + 2)
                b = begin(l, "cross")
                for h in range(HEADS):
                    mm = pe.matmul(b[:, h * P:(h + 1) * P], head(lev[0], h, 0), head(lev[0], h, 1), start=True, stop=True)
                mm.then_inc(products_done, 1)
                for k in range(NLEV):
                    if k in (1, 3, 5):
                        split_block_by_token(l, f"gate{2 + k // 2}")
                    pe.wait_ge(decayed, (NLEV + 2) * l + 3 + k)
                    for t in range(TILES):
                        b = begin(l, f"lev{k}{t}")
                        for h in range(HEADS):
                            m = head(lev[(k + 1) % 3], h, t)
                            mm = pe.matmul(b[:, h * P:(h + 1) * P], m, m, start=True, stop=True)
                        mm.then_inc(products_done, 1)
                wait_read(pe, l, "ckT1")
                for t in range(TILES):
                    keys = (t + 1) * P
                    for pair in range(2):
                        b = begin(l, f"att{t}{pair}")
                        for m in range(2):
                            h = 2 * pair + m
                            mm = pe.matmul(b[:, m * S:m * S + keys], cqT[:, h, t * P:(t + 1) * P], ckT[:, h, 0:keys],
                                           start=True, stop=True)
                        mm.then_inc(products_done, 1)
                pe.wait_ge(ws_causal, l + 1)
                for t in range(TILES):
                    pe.wait_ge(v_normed, TILES * l + t + 1)
                    b = begin(l, f"mix{t}")
                    for g in range(HEADS):
                        mm = pe.matmul(b[:, g * P:(g + 1) * P], ws[:, g, :], mixer["bv"][:, t, g * P:(g + 1) * P],
                                       start=True, stop=True)
                    mm.then_inc(products_done, 1)
                wait_read(pe, l, f"lev{NLEV - 1}1")
                wait_read(pe, l, "cross")
                wait_read(pe, l, "ai1")
                for t in range(TILES):
                    b = begin(l, f"hout{t}")
                    for h in range(HEADS):
                        cols_h = slice(h * P, (h + 1) * P)
                        mm = pe.matmul(b[:, cols_h], pairT[:, t, h, :], mixer["ai"][:, t, cols_h],
                                       start=True, stop=(t == 0))
                        if t == 1:
                            mm = pe.matmul(b[:, cols_h], crossT[:, h, :], mixer["ai"][:, 0, cols_h],
                                           start=False, stop=True)
                    mm.then_inc(products_done, 1)
                split_block_by_token(l, "gate5")
                pe.wait_ge(probs, 8 * l + 4)
                transposes(l, "pT0", [prob[:, 0, h, 0:P] for h in range(HEADS)])
                pe.wait_ge(probs, 8 * l + 8)
                for pair in range(2):
                    transposes(l, f"pT1{pair}", [prob[:, 1, 2 * pair + m, s * P:(s + 1) * P]
                                                 for m in range(2) for s in range(2)])
                ys = (mixer["ag"], mixer["bu"], yc)

                def y_transposes(n):
                    for t in range(TILES):
                        transposes(l, f"y{n}{t}", [ys[n][:, t, k * P:(k + 1) * P] for k in range(4)])

                pe.wait_ge(ya_ready, l + 1)
                y_transposes(0)
                wait_read(pe, l, "mix1")
                y_transposes(1)
                wait_read(pe, l, "cv1")
                wait_read(pe, l, "pT11")
                for t in range(TILES):
                    b = begin(l, f"aout{t}")
                    for h in range(HEADS):
                        cols_h = slice(h * P, (h + 1) * P)
                        for s in range(t + 1):
                            lhs = pT0[:, h, :] if t == 0 else pT1[:, h, s, :]
                            mm = pe.matmul(b[:, cols_h], lhs, mixer["cv"][:, s, cols_h], start=(s == 0), stop=(s == t))
                    mm.then_inc(products_done, 1)
                for n in range(BRANCHES):
                    wait_read(pe, l, f"y{n}1")
                    for half in range(2):
                        split_by_token(l, f"br{n}{half}", 2 * FIRST[f"br{n}"] + 2 * half, 2,
                                       lambda c: AT_YT[n] + c * S)
                    if n == 0:
                        wait_read(pe, l, "aout1")
                        y_transposes(2)
                for half in range(2):
                    for t in range(TILES):
                        pe.wait_ge(mix_done, 4 * l + 2 * half + t + 1)
                        transposes(l, f"mT{half}{t}", [mixsum[:, t, (4 * half + c) * P:(4 * half + c + 1) * P] for c in range(4)])
                for half in range(2):
                    source = lambda c: AT_MT[c // 4] + c % 4 * S
                    if half == 0:
                        split_by_token(l, "out0", 2 * FIRST["out0"], 4, source,
                                       before_unit=lambda u: wait_read(pe, l, f"mT{u // 2}1"))
                    else:
                        split_last_block(l, "out1", source)
                norm_transposes(l, 1)
                pe.wait_ge(hT_split, 2 * TILES * (l + 1))
                for n in range(4):
                    split_block_by_column(l, f"qry{n}")
                wait_read(pe, l, "qry31")
                for b in range(4):
                    wait_read(pe, *plan.last_of(l, b))
                assert done[0] == plan.base[l, "seed"]
                for half in range(2):
                    for t in range(TILES):
                        pe.matmul(bank[2 * half + t][:, :], ident, xs[:, t, half * 512:(half + 1) * 512], start=True,
                                  stop=False, skip_group_check=True).then_inc(products_done, 1)
                        done[0] += 1
                subkeys = item_in(l, KEY_ITEM)[:, 0:HP * KEYS].rearrange("p (n k) -> p n k", n=HP)
                for t in range(TILES):
                    for n in range(4):
                        b = begin(l, f"sc{t}{n}")
                        for m in range(4):
                            hp = 4 * n + m
                            mm = pe.matmul(b[:, m * KEYS:(m + 1) * KEYS], qryT[:, hp, t * P:(t + 1) * P], subkeys[:, hp, :],
                                           start=True, stop=True)
                        mm.then_inc(products_done, 1)
                for b in (6, 7):
                    wait_read(pe, *plan.last_of(l, b))

                def u_column(i, j):
                    if 2 <= j < AHEAD + 2:
                        pe.wait_ge(gelu_done, i * TURN + (KEYS * l + j - 1))
                    elif j >= AHEAD + 2:
                        pe.wait_ge(gelu_in, i * TURN + (GATED * l + j - AHEAD - 1))
                    pe.wait_ge(lower_ready, i * TURN + (V_UNIT * l + U_UNIT + j + 1))
                    k = slot_of(l, U_UNIT + j)
                    for c in range(KC):
                        at_h = slice(c * S, (c + 1) * S)
                        for n, (u, h) in enumerate(WEIGHT_BY_H):
                            mm = pe.matmul(bank[6 + j % 2][:, 0:S], u[:, k, c * P:(c + 1) * P], h[:, at_h],
                                           start=(c == 0 and n == 0), stop=(c == KC - 1 and n == 2))
                    mm.then_inc(products_done, 1)

                columns(pe, 0, PICKED, u_column, straight=TURN)
                done[0] += PICKED

                pe.wait_ge(picked, TILES * (l + 1))
                transposes(l, "IJT", [pick_ij[:, t, n, :] for n in range(2) for t in range(TILES)])
                transposes(l, "gT", [gate_k[:, t, :, :].rearrange("p h k -> p (h k)") for t in range(TILES)])
                columns(pe, PICKED, AHEAD, u_column)
                done[0] += AHEAD - PICKED
                for b in (4, 5):
                    wait_read(pe, *plan.last_of(l, b))

                def gates_and_u(i, g):
                    if g >= 2:
                        pe.wait_ge(gates_in, i * TURN + (GROUPS * l + g - 1))
                    pe.wait_ge(hot_ready, i * TURN + (GROUPS * l + g + 1))
                    for m in range(4):
                        mm = pe.matmul(bank[4 + g % 2][:, m * P:(m + 1) * P], hot[:, 0, m, :], hot[:, 1, m, :],
                                       start=True, stop=True)
                        mm.then_inc(products_done, 1)
                    u_column(i, AHEAD + g)

                columns(pe, 0, GROUPS, gates_and_u, straight=TURN)
                columns(pe, AHEAD + GROUPS, KEYS, u_column)

                def v_in(i, j):
                    pe.wait_ge(w_ready, i * TURN + (KEYS * l + j + 1))
                    pe.wait_ge(v_ready, i * TURN + (KEYS * l + j + 1))

                def v_tile(j, t):
                    k = slot_of(l, V_UNIT + j)
                    for n, (w, v) in enumerate(((w_upper, upper), (w_upper, lower), (w_lower, upper))):
                        for half in range(2):
                            mm = pe.matmul(bank[2 * half + t][:, :], w[:, j % 2, t * P:(t + 1) * P],
                                           v[:, k, half * 512:(half + 1) * 512], start=False,
                                           stop=(j == KEYS - 1 and n == 2), skip_group_check=True)
                    return mm

                def v_column(i, j):
                    v_in(i, j)
                    for t in range(TILES):
                        mm = v_tile(j, t)
                    mm.then_inc(products_done, 1)

                columns(pe, 0, KEYS - 2, v_column)
                for t in range(TILES):
                    for j in (KEYS - 2, KEYS - 1):
                        if t == 0:
                            v_in(0, j)
                        mm = v_tile(j, t)
                    mm.then_inc(products_done, 1)
                done[0] += 5 * GROUPS + GATED - GROUPS + KEYS

        @block.scalar
        def _(act):
            chain = [0]

            def link(ins):
                chain[0] += 1
                ins.then_inc(act_chain, 1)
                act.wait_ge(act_chain, chain[0])

            def roots_next():
                act.activation(stat[:, 88:89], ident[:, 0:1], ACT.Sqrt)

            def norm(n):
                for t in range(TILES):
                    if n == 0:
                        if t == 0:
                            act.wait_ge(const_in, 16 * 2)
                            roots_next()
                        act.wait_ge(x_in, 16 * TILES)
                    elif n % 2:
                        wait_read(act, n // 2, f"out1{t}")
                    else:
                        act.wait_ge(read["x_done"], 4 * (n - 1) + 2 * (t + 1))
                    act.activation(xn[:, t, :], xs[:, t, :], ACT.Square,
                                   accum_out=stat[:, t:t + 1]).then_inc(squares, 1)
                    act.wait_ge(meansq, TILES * n + t + 1)
                    act.activation(stat[:, 4 + t:5 + t], stat[:, 2 + t:3 + t], ACT.Sqrt).then_inc(roots, 1)

            def upper_hT(l, which, t):
                for half in range(2):
                    wait_read(act, l, f"n{which + 1}.{t}{half}")
                    part = hT[:, 4 * half:4 * half + 4, t * P:(t + 1) * P]
                    act.activation(quarter(hT_upper, t, half), part, ACT.Copy).then_inc(hT_upper_ready, 1)

            def tables():
                act.wait_ge(trig_in, 1)
                act.activation(trig[:, :, :, :], trig[:, :, :, :], ACT.Sin).then_inc(trig_out, 1)
                act.wait_ge(lb_in, 1)
                act.activation(lb[:, 2:4, :], lb[:, 0:2, :], ACT.Exp).then_inc(lb_out, 1)
                act.wait_ge(lb_in, 2)
                act.activation(lb[:, 5, :], lb[:, 4, :], ACT.Ln).then_inc(lb_out, 1)

            unit = [0]

            def to_upper(l, i, k):
                n = l * ITEMS + item_of(k)
                if k % 2 == 0:
                    act.wait_ge(arrived[n % SLOTS], i * (16 * TURN // (2 * SLOTS)) + 16 * (n // SLOTS + 1))
                act.activation(upper[:, slot_of(l, k), :], ring[:, n % SLOTS, (k % 2) * D:(k % 2 + 1) * D], ACT.Copy)\
                   .then_inc(upper_ready, 1)

            def uppers_to(l, name, most=UNITS):
                most += unit[0]
                while unit[0] < min(U_UNIT, most) and (unit[0] < PARTS or plan.unit_step(l, unit[0] - PARTS) <= plan.index[l, name]):
                    if unit[0] >= PARTS:
                        act.wait_ge(products_done, plan.unit_step(l, unit[0] - PARTS) + 1)
                    elif l > 0:
                        act.wait_ge(products_done, plan.v_index(l - 1, KEYS - 1 if unit[0] else KEYS - PARTS) + 1)
                    to_upper(l, 0, unit[0])
                    unit[0] += 1

            for l in range(LAYERS):
                def out_of(name, dst, func=ACT.Copy, cols=512):
                    uppers_to(l, name)
                    b = full(act, l, name)
                    src = b[:, 0:cols]
                    if len(dst.shape) == 3:
                        src = src.rearrange("p (a n) -> p a n", a=dst.shape[1])
                    elif len(dst.shape) == 4:
                        src = src.rearrange("p (a b n) -> p a b n", a=dst.shape[1], b=dst.shape[2])
                    done_reading(act.activation(dst, src, func), l, name)

                def block_out(name, dst, func=ACT.Copy):
                    for t in range(TILES):
                        out_of(f"{name}{t}", dst[:, t, :], func)

                def gate_out(n):
                    block_out(f"gate{n}", gates[:, :, n * 512:(n + 1) * 512], ACT.Sigmoid)

                unit[0] = 0
                norm(2 * l)
                upper_hT(l, 0, 0)
                uppers_to(l, "n1.00", most=2)
                upper_hT(l, 0, 1)
                uppers_to(l, "n1.00")
                if l == 0:
                    uppers_to(l, "iq.1")
                    tables()
                for pair in range(2):
                    uppers_to(l, f"af{pair}")
                    b = full(act, l, f"af{pair}")
                    act.activation(zT[:, pair * 512:(pair + 1) * 512], b[:, :], ACT.Copy)
                    done_reading(act.activation(key[:, pair * 512:(pair + 1) * 512], b[:, :], ACT.Sigmoid, scale=-1.0),
                                 l, f"af{pair}")
                for pair in range(2):
                    out_of(f"aq{pair}", qs[:, pair * 512:(pair + 1) * 512], ACT.Silu)
                for t in range(TILES):
                    out_of(f"iqT{t}", iqT[:, :, t * P:(t + 1) * P])
                out_of("ikT", ikT, cols=S)
                block_out("ag", mixer["ag"], ACT.Silu)
                block_out("ai", mixer["ai"])
                wait_read(act, l, "ck1")
                for t in range(TILES):
                    keys = (t + 1) * P
                    for n in range(4):
                        use = 8 * l + 4 * t + n
                        if n + 4 * t >= 2:
                            act.wait_ge(relu_used, use - 1)
                        uppers_to(l, f"logit{t}{n}")
                        b = full(act, l, f"logit{t}{n}")
                        dst = tmp[:, (n % 2) * 512:(n % 2 + 1) * 512].rearrange("p (m k) -> p m k", m=2)[:, :, 0:keys]
                        src = b[:, :].rearrange("p (m k) -> p m k", m=2)[:, :, 0:keys]
                        done_reading(act.activation(dst, src, ACT.Relu, scale=IDX_DIM ** -0.5), l, f"logit{t}{n}")
                for t in range(TILES):
                    out_of(f"cqT{t}", cqT[:, :, t * P:(t + 1) * P])
                for t in range(TILES):
                    out_of(f"ckT{t}", ckT[:, :, t * P:(t + 1) * P])
                block_out("cv", mixer["cv"])
                block_out("bu", mixer["bu"], ACT.Gelu_apprx_tanh)
                block_out("bv", mixer["bv"], ACT.Gelu_apprx_tanh)
                wait_read(act, l, "bv1")
                for t in range(TILES):
                    link(act.activation(gates[:, t, 1024:1536], mixer["bv"][:, t, :], ACT.Square,
                                        accum_out=stat[:, 8 + t:9 + t]))
                act.sem_inc(vsq, 1)
                act.wait_ge(vms, l + 1)
                act.activation(stat[:, 12:14], stat[:, 10:12], ACT.Sqrt).then_inc(vroot, 1)

                def softplus(use, name):
                    act.wait_ge(soft_in, use)
                    link(act.activation(logf, logf, ACT.Exp))
                    uppers_to(l, name)
                    act.activation(logf, logf, ACT.Ln, bias=1.0).then_inc(soft_out, 1)

                def decay(q):
                    act.wait_ge(decay_arg, (NLEV + 1) * l + q + 1)
                    act.activation(lev[q % 3], lev[q % 3], ACT.Exp).then_inc(decay_exp, 1)

                uppers_to(l, "gate0.0")
                softplus(1 if l == 0 else 2 * l, "gate0.1")
                gate_out(0)
                uppers_to(l, "gate1.0")
                if l > 0:
                    softplus(2 * l + 1, "gate1.1")
                decay(0)
                decay(1)
                gate_out(1)
                b = full(act, l, "cross")
                done_reading(act.activation(crossT, b[:, :].rearrange("p (h n) -> p h n", h=HEADS), ACT.Copy), l, "cross")
                for n in (2, 3, 4):
                    uppers_to(l, f"gate{n}.0")
                    decay(2 * n - 2)
                    decay(2 * n - 1)
                    gate_out(n)
                for t in range(TILES):
                    keys = (t + 1) * P
                    act.wait_ge(neg_max, TILES * l + t + 1)
                    for h in range(HEADS):
                        c = HEADS * t + h
                        act.activation(prob[:, t, h, 0:keys], prob[:, t, h, 0:keys], ACT.Exp, scale=P ** -0.5,
                                       bias=stat[:, 24 + c:25 + c], accum_out=stat[:, 32 + c:33 + c]).then_inc(probs, 1)
                for t in range(TILES):
                    out_of(f"hout{t}", oh[:, t, :])
                uppers_to(l, "gate5.0")
                act.wait_ge(oms, l + 1)
                act.activation(stat[:, 56:64], stat[:, 48:56], ACT.Sqrt).then_inc(oroot, 1)
                gate_out(5)
                out_of("pT0", pT0)
                for pair in range(2):
                    out_of(f"pT1{pair}", pT1[:, 2 * pair:2 * pair + 2, :, :])

                def upper_of(name, at, t):
                    uppers_to(l, name)
                    b = full(act, l, name)
                    act.activation(tile_of(hT_upper, at, t), b[:, :].rearrange("p (k t) -> p k t", k=4), ACT.Copy)\
                       .then_inc(T_upper_ready, 1)

                for n in range(BRANCHES):
                    if AT_YT[n] in AT_YT[:n]:
                        last = f"br{AT_YT.index(AT_YT[n])}11"
                        uppers_to(l, last)
                        full(act, l, last)
                    for t in range(TILES):
                        upper_of(f"y{n}{t}", AT_YT[n], t)
                for n in range(BRANCHES):
                    for half in range(2):
                        uppers_to(l, f"br{n}{half}1")
                for half in range(2):
                    for t in range(TILES):
                        upper_of(f"mT{half}{t}", AT_MT[half], t)
                roots_next()
                uppers_to(l, "out10")
                norm(2 * l + 1)
                upper_hT(l, 1, 0)
                uppers_to(l, "out11", most=1)
                upper_hT(l, 1, 1)
                uppers_to(l, "out11")
                for n in range(4):
                    for pair in range(2):
                        out_of(f"qry{n}{pair}", qryT[:, 4 * n + 2 * pair:4 * n + 2 * pair + 2, :])
                assert unit[0] == U_UNIT
                for k in range(PARTS):
                    act.wait_ge(products_done, plan.unit_step(l, U_UNIT + k - PARTS) + 1)
                    to_upper(l, 0, U_UNIT + k)
                for t in range(TILES):
                    for n in range(4):
                        out_of(f"sc{t}{n}", sc[:, t, 4 * n:4 * n + 4, :])
                def u_column(i, j):
                    steps = 5 if AHEAD <= j < AHEAD + GROUPS else 1
                    act.wait_ge(products_done, i * (steps * TURN) + (plan.u_index(l, j) + 1))
                    b = bank[6 + j % 2]
                    dst = G[:, bass.ds(i * TURN + j, 1), :].rearrange("p a t -> p (a t)") if j < AHEAD else b[:, S:2 * S]
                    act.activation(dst, b[:, 0:S], ACT.Gelu_apprx_tanh).then_inc(gelu_done, 1)
                    to_upper(l, i, U_UNIT + j + PARTS)

                for t in range(TILES):
                    columns(act, EXPS[t - 1] if t else 0, EXPS[t], u_column)
                    act.wait_ge(best_diff, TILES * l + t + 1)
                    act.activation(gate_k[:, t, :, :], gate_k[:, t, :, :], ACT.Exp).then_inc(best_exp, 1)
                columns(act, EXPS[-1], PICKED, u_column)
                out_of("IJT", picks[:, 0:2, :])
                out_of("gT", gT, cols=S)
                columns(act, PICKED, AHEAD, u_column)
                columns(act, AHEAD, AHEAD + GROUPS, u_column)

                def v_column(i, j):
                    if j >= 2:
                        act.wait_ge(products_done, i * TURN + (plan.v_index(l, j - 2) + 1))
                    act.activation(w_upper[:, j % 2, :], G[:, bass.ds(i * TURN + j, 1), :].rearrange("p a t -> p (a t)"),
                                   ACT.Copy).then_inc(w_upper_ready, 1)
                    if 2 <= j < KEYS - 1:
                        to_upper(l, i, V_UNIT + j + 1)

                columns(act, AHEAD + GROUPS, KEYS - 1, u_column)
                act.wait_ge(gates_in, GROUPS * (l + 1))
                for j in range(2):
                    v_column(0, j)
                u_column(0, KEYS - 1)
                act.wait_ge(gelu_in, GATED * (l + 1))
                roots_next()
                columns(act, 2, KEYS, v_column, tail=1)
            norm(2 * LAYERS)

        @block.vector
        def _(dve):
            chain = [0]

            def link(ins):
                chain[0] += 1
                ins.then_inc(dve_chain, 1)
                dve.wait_ge(dve_chain, chain[0])

            def norm_tile(n, dst, t):
                dve.wait_ge(squares, TILES * n + t + 1)
                dve.tensor_scalar(stat[:, 2 + t:3 + t], stat[:, t:t + 1], 1.0 / D, EPS, ALU.mult, ALU.add)\
                   .then_inc(meansq, 1)
                dve.wait_ge(roots, TILES * n + t + 1)
                link(dve.reciprocal(stat[:, 6 + t:7 + t], stat[:, 4 + t:5 + t]))
                if n < 2 * LAYERS:
                    dve.tensor_scalar(dst[:, t, :], xs[:, t, :], stat[:, 6 + t:7 + t], None, ALU.mult).then_inc(xn_ready, 1)
                else:
                    dve.scalar_tensor_tensor(out=dst[:, t, :], in0=xs[:, t, :], scalar=stat[:, 6 + t:7 + t], in1=frow,
                                             op0=ALU.mult, op1=ALU.mult).then_inc(final_out, 1)

            def gain_tile(l, which, t):
                for half in range(2):
                    name = f"n{which + 1}.{t}{half}"
                    b = full(dve, l, name)
                    gain = gcol[:, 2 * l + which, 4 * half:4 * half + 4].unsqueeze(2).to_broadcast([P, 4, P])
                    done_reading(dve.tensor_tensor(hT[:, 4 * half:4 * half + 4, t * P:(t + 1) * P],
                                                   b[:, :].rearrange("p (c t) -> p c t", c=4), gain, ALU.mult), l, name)

            def lower_hT(l, which, t):
                for half in range(2):
                    dve.wait_ge(hT_upper_ready, 4 * (2 * l + which) + 2 * t + half + 1)
                    ins = dve.tensor_tensor(quarter(hT_lower, t, half), hT[:, 4 * half:4 * half + 4, t * P:(t + 1) * P],
                                            quarter(hT_upper, t, half).bitcast(F32), ALU.subtract)
                ins.then_inc(hT_split, 1)

            def norm_to_hT(l, which, before_last=lambda: None):
                norm_tile(2 * l + which, xn, 0)
                before_last()
                if which == 0:
                    norm_tile(2 * l, xn, 1)
                    gain_tile(l, 0, 0)
                else:
                    gain_tile(l, 1, 0)
                    norm_tile(2 * l + 1, xn, 1)
                lower_hT(l, which, 0)
                gain_tile(l, which, 1)
                lower_hT(l, which, 1)

            def rope(l, name, t, src, dst, heads, half, extra=None):
                first = 0 if half == 64 else 64
                table = lambda f: trig[:, f, t, first:first + half].unsqueeze(1)
                n = heads * half
                both = tmp[:, 0:2 * n].rearrange("p (h s d) -> p h s d", h=heads, s=2)
                cross = tmp[:, 512:512 + 2 * n].rearrange("p (h s d) -> p h s d", h=heads, s=2)
                cos = table(0).unsqueeze(1).to_broadcast([P, heads, 2, half])
                sin = table(1).to_broadcast([P, heads, half])
                dve.tensor_tensor(both, src, cos, ALU.mult)
                dve.tensor_tensor(cross[:, :, 0, :], src[:, :, 1, :], sin, ALU.mult)
                link(dve.tensor_tensor(cross[:, :, 1, :], src[:, :, 0, :], sin, ALU.mult))
                dve.tensor_tensor(dst[:, :, 0, :], both[:, :, 0, :], cross[:, :, 0, :], ALU.subtract)
                ins = dve.tensor_tensor(dst[:, :, 1, :], both[:, :, 1, :], cross[:, :, 1, :], ALU.add)
                return ins

            scale_a = P ** -0.5
            log_lb, log_rest, rest = lb[:, 6, :], lb[:, 7, :], lb[:, 4, :]

            def tables():
                dve.memset(zero64[:, :], 0.0)
                dve.wait_ge(table_in, 16 * 3)
                dve.tensor_copy(mask[:, :, :].rearrange("p k n -> p (k n)"), lev[0][:, 0:NLEV * P])
                posf = stat[:, 94:96]
                link(dve.tensor_copy(posf, stat[:, 92:94].bitcast(I32)))
                two_pi = 2.0 * np.pi
                c1 = 6.28125
                c2 = float(np.uint32(int(np.float32(two_pi - c1).view(np.uint32)) & 0xFFFFE000).view(np.float32))
                c3 = float(two_pi - c1 - c2)
                magic = 1.5 * 2.0 ** 23
                turns = tmp[:, 0:192].rearrange("p (t n) -> p t n", t=TILES)
                for f in range(2):
                    shift = 0.25 if f == 0 else 0.0
                    for t in range(TILES):
                        link(dve.tensor_scalar(trig[:, f, t, :], freq, posf[:, t:t + 1], None, ALU.mult))
                    link(dve.tensor_scalar(turns, trig[:, f, :, :], 1.0 / two_pi, shift, ALU.mult, ALU.add))
                    link(dve.tensor_scalar(turns, turns, magic, None, ALU.add))
                    link(dve.tensor_scalar(turns, turns, -magic, None, ALU.add))
                    for c in (c1, c2, c3):
                        link(dve.scalar_tensor_tensor(out=trig[:, f, :, :], in0=turns, scalar=-c, in1=trig[:, f, :, :],
                                                      op0=ALU.mult, op1=ALU.add))
                    if f == 0:
                        link(dve.tensor_scalar(trig[:, f, :, :], trig[:, f, :, :], np.pi / 2, None, ALU.add))
                dve.tensor_scalar(trig[:, :, :, :], trig[:, :, :, :], 3.1415925, -3.1415925, ALU.min, ALU.max).then_inc(trig_in, 1)

                link(dve.tensor_tensor(lb[:, 4, :], lb[:, 0, :], lb[:, 1, :], ALU.max))
                for n in range(LAYERS):
                    ins = dve.tensor_tensor(lb[:, n, :], lb[:, n, :], lb[:, 4, :], ALU.subtract)
                    link(ins)
                dve.sem_inc(lb_in, 1)
                dve.wait_ge(lb_out, 1)
                link(dve.tensor_tensor(lb[:, 4, :], lb[:, 2, :], lb[:, 3, :], ALU.add))
                dve.sem_inc(lb_in, 1)
                dve.wait_ge(lb_out, 2)
                dve.tensor_tensor(log_lb, lb[:, 1, :], lb[:, 5, :], ALU.subtract)
                link(dve.tensor_tensor(log_rest, lb[:, 0, :], lb[:, 5, :], ALU.subtract))
                link(dve.reciprocal(lb[:, 5, :], lb[:, 4, :]))
                for n in (2, 3):
                    link(dve.tensor_tensor(lb[:, n, :], lb[:, n, :], lb[:, 5, :], ALU.mult))
                link(dve.tensor_tensor(rest, lb[:, 2, :], lb[:, 3, :], ALU.add))
                link(dve.tensor_tensor(rest, rest, lb[:, 2, :], ALU.subtract))
                link(dve.tensor_scalar(rest, rest, -scale_a, scale_a, ALU.mult, ALU.add))
                dve.wait_ge(trig_out, 1)

            by_head = lambda c: c.unsqueeze(2).to_broadcast([P, HEADS, S])
            heads_of = lambda ap: ap.rearrange("p (h t) -> p h t", h=HEADS)

            for l in range(LAYERS):
                if l == 0:
                    dve.wait_ge(const_in, 16 * 2)
                norm_to_hT(l, 0)
                if l == 0:
                    tables()
                for t in range(TILES):
                    b = full(dve, l, f"iq{t}")
                    view = lambda ap: ap.rearrange("p (h s d) -> p h s d", h=IDX_HEADS, s=2)
                    done_reading(rope(l, "iq", t, view(b[:, :]), view(mixer["iq"][:, t, :]), IDX_HEADS, 32), l, f"iq{t}")
                    wait_read(dve, l, f"iq{t}")
                for t in range(TILES):
                    b = full(dve, l, f"small{t}")
                    view = lambda ap: ap.rearrange("p (h s d) -> p h s d", h=1, s=2)
                    link(rope(l, "ik", t, view(b[:, 0:IDX_DIM]), view(ikn[:, t, 0:IDX_DIM]), 1, 32))
                    dve.tensor_copy(ikn[:, t, IDX_DIM:2 * IDX_DIM], ikn[:, t, 0:IDX_DIM])
                    done_reading(dve.tensor_scalar(wi[:, t, :], b[:, IDX_DIM:SMALL_COLS], IDX_HEADS ** -0.5, None, ALU.mult),
                                 l, f"small{t}")
                    wait_read(dve, l, f"small{t}")
                for name in ("cq", "ck"):
                    for t in range(TILES):
                        b = full(dve, l, f"{name}{t}")
                        view = lambda ap: ap.rearrange("p (h s d) -> p h s d", h=HEADS, s=2)
                        done_reading(rope(l, name, t, view(b[:, :]), view(mixer[name][:, t, :]), HEADS, 64), l, f"{name}{t}")
                        wait_read(dve, l, f"{name}{t}")
                for t in range(TILES):
                    keys = (t + 1) * P
                    for n in range(4):
                        wait_read(dve, l, f"logit{t}{n}")
                        for m in range(2):
                            head = 4 * (n // 2) + 2 * m + n % 2
                            src = tmp[:, (n % 2) * 512 + m * S:(n % 2) * 512 + m * S + keys]
                            if n == 0 and m == 0:
                                ins = dve.tensor_scalar(score[:, t, 0:keys], src, wi[:, t, head:head + 1], None, ALU.mult)
                            else:
                                ins = dve.scalar_tensor_tensor(out=score[:, t, 0:keys], in0=src, scalar=wi[:, t, head:head + 1],
                                                               in1=score[:, t, 0:keys], op0=ALU.mult, op1=ALU.add)
                            link(ins)
                        dve.sem_inc(relu_used, 1)
                for t in range(TILES):
                    keys = (t + 1) * P
                    link(dve.memset(score[0:CHUNK, t, keys - CHUNK:keys], NEG))
                for r in range(DSA_TOPK // 8):
                    for t in range(TILES):
                        keys = (t + 1) * P
                        ins = dve.max(out=top8[:, 8 * t:8 * t + 8], in_=score[:, t, 0:keys])
                    link(ins)
                    for t in range(TILES):
                        keys = (t + 1) * P
                        ins = dve.match_replace(out=score[:, t, 0:keys], in_to_replace=top8[:, 8 * t:8 * t + 8],
                                                in_values=score[:, t, 0:keys], imm_value=MARK)
                    link(ins)
                for t in range(TILES):
                    keys = (t + 1) * P
                    link(dve.tensor_scalar(score[:, t, 0:keys], score[:, t, 0:keys], MARK, MASKED, ALU.not_equal, ALU.mult))

                dve.wait_ge(vsq, l + 1)
                dve.tensor_scalar(stat[:, 10:12], stat[:, 8:10], 1.0 / W, EPS, ALU.mult, ALU.add).then_inc(vms, 1)
                dve.wait_ge(vroot, l + 1)
                link(dve.reciprocal(stat[:, 14:16], stat[:, 12:14]))
                dve.wait_ge(layer_in, 80 * (l + 1))
                for t in range(TILES):
                    v = mixer["bv"][:, t, :]
                    dve.scalar_tensor_tensor(out=v, in0=v, scalar=stat[:, 14 + t:15 + t], in1=grow, op0=ALU.mult,
                                             op1=ALU.mult).then_inc(v_normed, 1)

                wait_read(dve, l, "aq1")
                z = zT
                dve.scalar_tensor_tensor(out=logf, in0=z, scalar=-1.0, in1=z, op0=ALU.mult, op1=ALU.min)\
                   .then_inc(soft_in, 1)
                if l == 0:
                    dve.tensor_scalar(key, key, scale_a, None, ALU.mult).then_inc(decayed, 1)
                else:
                    dve.tensor_tensor(heads_of(key), heads_of(key), by_head(rest), ALU.mult).then_inc(decayed, 1)
                dve.wait_ge(soft_out, 1 if l == 0 else 2 * l)
                link(dve.scalar_tensor_tensor(out=z, in0=z, scalar=0.0, in1=logf, op0=ALU.min, op1=ALU.subtract))
                if l > 0:
                    link(dve.tensor_tensor(heads_of(z), heads_of(z), by_head(log_rest), ALU.add))
                    link(dve.tensor_tensor(heads_of(bcum), heads_of(z), by_head(log_lb), ALU.subtract))
                    dve.scalar_tensor_tensor(out=logf, in0=bcum, scalar=-1.0, in1=bcum, op0=ALU.mult, op1=ALU.min)\
                       .then_inc(soft_in, 1)
                    link(dve.tensor_tensor(heads_of(z), heads_of(z), by_head(log_lb), ALU.max))
                    dve.wait_ge(soft_out, 2 * l + 1)
                    link(dve.tensor_tensor(z, z, logf, ALU.add))
                for c in range(HEADS * S // CHUNK):
                    ins = dve.tensor_tensor_scan(bcum[:, c * CHUNK:(c + 1) * CHUNK], z[:, c * CHUNK:(c + 1) * CHUNK],
                                                 zero64[:, :], 0.0, ALU.add, ALU.add)
                link(ins)

                def exponents(q):
                    if q >= 3:
                        full(dve, l, "cross" if q == 3 else f"lev{q - 4}1")
                    e = lev[q % 3]
                    if q == 0:
                        eh = e.rearrange("p (h c n) -> p h c n", h=HEADS, c=4)
                        bh = bcum.rearrange("p (h c n) -> p h c n", h=HEADS, c=4)
                        end = lambda c: bh[:, :, c, CHUNK - 1:CHUNK].to_broadcast([P, HEADS, CHUNK])
                        dve.tensor_tensor(eh[:, :, 1, :], end(1), bh[:, :, 1, :], ALU.subtract)
                        dve.tensor_copy(eh[:, :, 2, :], bh[:, :, 2, :])
                        dve.tensor_tensor(eh[:, :, 3, :], bh[:, :, 3, :], end(2), ALU.add)
                        link(dve.tensor_tensor(eh[:, :, 0, :], end(0), bh[:, :, 0, :], ALU.subtract))
                        dve.tensor_tensor(eh[:, :, 0, :], eh[:, :, 0, :], end(1), ALU.add).then_inc(decay_arg, 1)
                        return
                    half = HALVES[q - 1]
                    n = HEADS * S // (2 * half)
                    eb = e.rearrange("p (n s i) -> p n s i", n=n, s=2)
                    bb = bcum.rearrange("p (n s i) -> p n s i", n=n, s=2)
                    last = bb[:, :, 0, half - 1:half].to_broadcast([P, n, half])
                    dve.tensor_tensor(eb[:, :, 0, :], last, bb[:, :, 0, :], ALU.subtract)
                    if half == CHUNK:
                        dve.tensor_copy(eb[:, :, 1, :], bb[:, :, 1, :]).then_inc(decay_arg, 1)
                    else:
                        dve.tensor_tensor(eb[:, :, 1, :], bb[:, :, 1, :], last, ALU.subtract).then_inc(decay_arg, 1)

                def decayed_rows(q):
                    dve.wait_ge(decay_exp, (NLEV + 1) * l + q + 1)
                    half = P if q == 0 else HALVES[q - 1]
                    n = HEADS * S // (2 * half)
                    view = lambda ap: ap.rearrange("p (n s i) -> p n s i", n=n, s=2)
                    e = view(lev[q % 3])
                    dve.tensor_tensor(e[:, :, 0, :], e[:, :, 0, :], view(key)[:, :, 0, :], ALU.mult)
                    dve.tensor_tensor(e[:, :, 1, :], e[:, :, 1, :], view(qs)[:, :, 1, :], ALU.mult).then_inc(decayed, 1)

                def into_pairs(k):
                    wait_read(dve, l, f"lev{k - 1}1" if k else "diag1")
                    for t in range(TILES):
                        b = full(dve, l, f"lev{k}{t}")
                        m = mask[:, k, :].unsqueeze(1).to_broadcast([P, HEADS, P])
                        done_reading(dve.copy_predicated(pairT[:, t, :, :], m, b[:, :].rearrange("p (h n) -> p h n", h=HEADS)),
                                     l, f"lev{k}{t}")

                dve.wait_ge(decayed, (NLEV + 2) * l + 1)
                exponents(0)
                exponents(1)
                decayed_rows(0)
                exponents(2)
                decayed_rows(1)
                for t in range(TILES):
                    b = full(dve, l, f"diag{t}")
                    ins = dve.tensor_tensor(pairT[:, t, :, :], b[:, :].rearrange("p (h n) -> p h n", h=HEADS),
                                            ident.unsqueeze(1).to_broadcast([P, HEADS, P]), ALU.mult)
                    done_reading(ins, l, f"diag{t}")
                for k in range(NLEV):
                    if k + 3 <= NLEV:
                        exponents(k + 3)
                    if k + 2 <= NLEV:
                        decayed_rows(k + 2)
                    into_pairs(k)

                for t in range(TILES):
                    keys = (t + 1) * P
                    for pair in range(2):
                        b = full(dve, l, f"att{t}{pair}")
                        bias = score[:, t, 0:keys].unsqueeze(1).to_broadcast([P, 2, keys])
                        ins = dve.tensor_tensor(prob[:, t, 2 * pair:2 * pair + 2, 0:keys],
                                                b[:, :].rearrange("p (m k) -> p m k", m=2)[:, :, 0:keys], bias, ALU.add)
                        done_reading(ins, l, f"att{t}{pair}")
                    wait_read(dve, l, f"att{t}1")
                    link(dve.tensor_reduce(stat[:, 16 + 4 * t:20 + 4 * t], prob[:, t, :, 0:keys], AX.X, ALU.max))
                    dve.tensor_scalar(stat[:, 24 + 4 * t:28 + 4 * t], stat[:, 16 + 4 * t:20 + 4 * t], -(P ** -0.5), None,
                                      ALU.mult).then_inc(neg_max, 1)
                for t in range(TILES):
                    b = full(dve, l, f"mix{t}")
                    for g in range(HEADS):
                        u = mixer["bu"][:, t, g * P:(g + 1) * P]
                        ins = dve.scalar_tensor_tensor(out=u, in0=b[:, g * P:(g + 1) * P], scalar=bs[:, g:g + 1], in1=u,
                                                       op0=ALU.add, op1=ALU.mult)
                    done_reading(ins, l, f"mix{t}")
                wait_read(dve, l, "hout1")
                per_head = lambda ap: ap.rearrange("p t (h n) -> p (t h) n", h=HEADS)
                link(dve.tensor_tensor(osq, oh, oh, ALU.mult))
                link(dve.tensor_reduce(stat[:, 48:56], per_head(osq), AX.X, ALU.add))
                dve.tensor_scalar(stat[:, 48:56], stat[:, 48:56], 1.0 / P, EPS, ALU.mult, ALU.add).then_inc(oms, 1)
                dve.wait_ge(oroot, l + 1)
                link(dve.reciprocal(stat[:, 64:72], stat[:, 56:64]))
                link(dve.tensor_tensor(per_head(oh), per_head(oh), stat[:, 64:72].unsqueeze(2).to_broadcast([P, 8, P]), ALU.mult))
                link(dve.tensor_tensor(per_head(oh), per_head(oh), hrow.unsqueeze(1).to_broadcast([P, 8, P]), ALU.mult))
                dve.tensor_tensor(mixer["ag"], mixer["ag"], oh, ALU.mult).then_inc(ya_ready, 1)
                lowered = [0]

                def lower_of(name, at, t):
                    lowered[0] += 1
                    dve.wait_ge(T_upper_ready, TILES * (BRANCHES + 2) * l + lowered[0])
                    b = full(dve, l, name)
                    done_reading(dve.tensor_tensor(tile_of(hT_lower, at, t), b[:, :].rearrange("p (k t) -> p k t", k=4),
                                                   tile_of(hT_upper, at, t).bitcast(F32), ALU.subtract), l, name)

                for n in range(2):
                    for t in range(TILES):
                        lower_of(f"y{n}{t}", AT_YT[n], t)
                dve.wait_ge(probs, 8 * (l + 1))
                link(dve.reciprocal(stat[:, 40:48], stat[:, 32:40]))
                for t in range(TILES):
                    b = full(dve, l, f"aout{t}")
                    r = stat[:, 40 + 4 * t:44 + 4 * t].unsqueeze(2).to_broadcast([P, HEADS, P])
                    done_reading(dve.tensor_tensor(yc[:, t, :].rearrange("p (h n) -> p h n", h=HEADS),
                                                   b[:, :].rearrange("p (h n) -> p h n", h=HEADS), r, ALU.mult), l, f"aout{t}")

                for n in range(BRANCHES):
                    if n == 1:
                        for t in range(TILES):
                            lower_of(f"y2{t}", AT_YT[2], t)
                    for half in range(2):
                        for t in range(TILES):
                            name = f"br{n}{half}{t}"
                            b = full(dve, l, name)
                            gate = gates[:, t, n * D + half * 512:n * D + (half + 1) * 512]
                            part = mixsum[:, t, half * 512:(half + 1) * 512]
                            dst = part if n == 0 else gate
                            done_reading(dve.tensor_tensor(dst, b[:, :], gate, ALU.mult), l, name)
                            if n > 0:
                                wait_read(dve, l, name)
                                ins = dve.tensor_tensor(part, part, gate, ALU.add)
                                if n == BRANCHES - 1:
                                    ins.then_inc(mix_done, 1)
                                else:
                                    link(ins)
                for half in range(2):
                    for t in range(TILES):
                        lower_of(f"mT{half}{t}", AT_MT[half], t)

                def add_out(half, t):
                    name = f"out{half}{t}"
                    b = full(dve, l, name)
                    part = xs[:, t, half * 512:(half + 1) * 512]
                    done_reading(dve.tensor_tensor(part, part, b[:, :], ALU.add), l, name)

                for half, t in ((0, 0), (0, 1), (1, 0)):
                    add_out(half, t)
                norm_to_hT(l, 1, before_last=lambda: add_out(1, 1))

                for t in range(TILES):
                    wait_read(dve, l, f"sc{t}3")
                    for n in range(HP):
                        ins = dve.max(out=topv[:, t, n, 0:8], in_=sc[:, t, n, :])
                    link(ins)
                    for n in range(HP):
                        ins = dve.max_index(out=topi[:, t, n, 0:8].bitcast(U32), in_max=topv[:, t, n, 0:8], in_values=sc[:, t, n, :])
                    link(ins)
                    for n in range(HP):
                        ins = dve.match_replace(out=sc[:, t, n, :], in_to_replace=topv[:, t, n, 0:8], in_values=sc[:, t, n, :],
                                                imm_value=TINY)
                    link(ins)
                    for n in range(HP):
                        ins = dve.max(out=topv[:, t, n, 8:16], in_=sc[:, t, n, :])
                    link(ins)
                    for n in range(HP):
                        ins = dve.max_index(out=topi[:, t, n, 8:16].bitcast(U32), in_max=topv[:, t, n, 8:16], in_values=sc[:, t, n, :])
                    link(ins)
                    halves = topv[:, t, :, :].rearrange("p (h s) k -> p h s k", s=2)
                    for h in range(PEER_HEADS):
                        ins = dve.tensor_tensor(cand[:, t, h, :].rearrange("p (a b) -> p a b", a=TOPK),
                                                halves[:, h, 0, :].unsqueeze(2).to_broadcast([P, TOPK, TOPK]),
                                                halves[:, h, 1, :].unsqueeze(1).to_broadcast([P, TOPK, TOPK]), ALU.add)
                    link(ins)
                    for h in range(PEER_HEADS):
                        ins = dve.max(out=bestv[:, t, h, 0:8], in_=cand[:, t, h, :])
                    link(ins)
                    for h in range(PEER_HEADS):
                        ins = dve.max_index(out=bestp[:, t, h, 0:8].bitcast(U32), in_max=bestv[:, t, h, 0:8], in_values=cand[:, t, h, :])
                    link(ins)
                    for h in range(PEER_HEADS):
                        ins = dve.match_replace(out=cand[:, t, h, :], in_to_replace=bestv[:, t, h, 0:8], in_values=cand[:, t, h, :],
                                                imm_value=TINY)
                    link(ins)
                    for h in range(PEER_HEADS):
                        ins = dve.max(out=bestv[:, t, h, 8:16], in_=cand[:, t, h, :])
                    link(ins)
                    dve.tensor_tensor(gate_k[:, t, :, :], bestv[:, t, :, :], bestv[:, t, :, 0:1].to_broadcast([P, PEER_HEADS, TOPK]),
                                      ALU.subtract).then_inc(best_diff, 1)
                    for h in range(PEER_HEADS):
                        ins = dve.max_index(out=bestp[:, t, h, 8:16].bitcast(U32), in_max=bestv[:, t, h, 8:16], in_values=cand[:, t, h, :])
                    link(ins)
                    flat = bestp[:, t, :, :].rearrange("p h k -> p (h k)").bitcast(U32)
                    dve.tensor_scalar(half_pos[:, 0, :].bitcast(U32), flat, 4, None, ALU.logical_shift_right)
                    link(dve.tensor_scalar(half_pos[:, 1, :].bitcast(U32), flat, 15, None, ALU.bitwise_and))
                    dve.tensor_copy(half_f, half_pos.bitcast(U32))
                    link(dve.tensor_copy(topf[:, t, :, :], topi[:, t, :, :].bitcast(U32)))
                    onehot = cand[:, t, :, :].rearrange("p h (k a) -> p h k a", k=TOPK)
                    numbers = topf[:, t, :, :].rearrange("p (h s) k -> p h s k", s=2)
                    for s in range(2):
                        place = half_f[:, s, :].rearrange("p (h k) -> p h k", h=PEER_HEADS).unsqueeze(3)\
                                               .to_broadcast([P, PEER_HEADS, TOPK, TOPK])
                        steps = iota[:, 0:TOPK].unsqueeze(1).unsqueeze(1).to_broadcast([P, PEER_HEADS, TOPK, TOPK])
                        number = numbers[:, :, s, :].unsqueeze(2).to_broadcast([P, PEER_HEADS, TOPK, TOPK])
                        link(dve.tensor_tensor(onehot, place, steps, ALU.is_equal))
                        link(dve.tensor_tensor(onehot, onehot, number, ALU.mult))
                        link(dve.tensor_reduce(pick_ij[:, t, s, :].rearrange("p (h k) -> p h k", h=PEER_HEADS), onehot, AX.X, ALU.add))
                    dve.wait_ge(best_exp, TILES * l + t + 1)
                    link(dve.tensor_reduce(stat[:, 72:80], gate_k[:, t, :, :], AX.X, ALU.add))
                    link(dve.reciprocal(stat[:, 80:88], stat[:, 72:80]))
                    dve.tensor_tensor(gate_k[:, t, :, :], gate_k[:, t, :, :],
                                      stat[:, 80:88].unsqueeze(2).to_broadcast([P, PEER_HEADS, TOPK]), ALU.mult).then_inc(picked, 1)

                dve.wait_ge(picked, TILES * (l + 1))
                dve.wait_ge(products_done, plan.base[l, "seed"] + 4)
                link(dve.memset(arena[:, AHEAD * S:KEYS * S], 1.0))
                wait_read(dve, l, "gT")

                def one_hots(i, g):
                    for m in range(4):
                        if g > 0:
                            dve.wait_ge(products_done, i * (5 * TURN) + (plan.token_index(l, g - 1, m) + 1))
                        tok = lambda ap: ap[:, bass.ds(i * (4 * TURN) + 4 * g + m, 1)]
                        dve.tensor_scalar(hot[:, 0, m, :], iota, tok(IT), tok(gT), ALU.is_equal, ALU.mult)
                    dve.tensor_tensor(hot[:, 1, :, :], iota.unsqueeze(1).to_broadcast([P, 4, P]),
                                      JT[:, bass.ds(i * (4 * TURN) + 4 * g, 4)].unsqueeze(2).to_broadcast([P, 4, P]),
                                      ALU.is_equal).then_inc(hot_ready, 1)

                def gates_into(i, g):
                    dve.wait_ge(products_done, i * (5 * TURN) + (plan.token_index(l, g, 3) + 1))
                    if g > 0:
                        dve.wait_ge(gates_in, i * TURN + (GROUPS * l + g))
                    else:
                        dve.wait_ge(gelu_done, KEYS * l + AHEAD)
                    part = G[:, :, bass.ds(i * (4 * TURN) + 4 * g, 4)]
                    dve.tensor_tensor(part, part, bank[4 + g % 2][:, :].rearrange("p (t j) -> p j t", t=4),
                                      ALU.mult).then_inc(gates_in, 1)

                def gelu_column(i, j):
                    dve.wait_ge(gelu_done, i * TURN + (KEYS * l + j + 1))
                    part = G[:, bass.ds(i * TURN + j, 1), :].rearrange("p a t -> p (a t)")
                    dve.tensor_tensor(part, part, bank[6 + j % 2][:, S:2 * S], ALU.mult).then_inc(gelu_in, 1)

                def group(i, g):
                    one_hots(i, g)
                    if g > 0:
                        gates_into(i, g - 1)
                        dve.wait_ge(gates_in, i * TURN + (GROUPS * l + g))
                        gelu_column(i, AHEAD + g - 1)
                        dve.wait_ge(gelu_in, i * TURN + (GATED * l + g))

                columns(dve, 0, GROUPS, group, straight=TURN)
                gates_into(0, GROUPS - 1)
                dve.wait_ge(gates_in, GROUPS * (l + 1))
                columns(dve, AHEAD + GROUPS - 1, KEYS - 2, gelu_column)

                def lower_v(i, j):
                    n = l * ITEMS + V_ITEM + j // 2
                    k = slot_of(l, V_UNIT + j)
                    dve.wait_ge(upper_ready, i * TURN + (UNITS * l + V_UNIT + j + 1))
                    dve.tensor_tensor(lower[:, k, :], ring[:, n % SLOTS, (j % 2) * D:(j % 2 + 1) * D],
                                      upper[:, k, :].bitcast(F32), ALU.subtract).then_inc(v_ready, 1)

                def v_column(i, j):
                    dve.wait_ge(w_upper_ready, i * TURN + (KEYS * l + j + 1))
                    dve.tensor_tensor(w_lower[:, j % 2, :], G[:, bass.ds(i * TURN + j, 1), :].rearrange("p a t -> p (a t)"),
                                      w_upper[:, j % 2, :].bitcast(F32), ALU.subtract).then_inc(w_ready, 1)
                    if 2 <= j < KEYS - 1:
                        lower_v(i, j + 1)

                lower_v(0, 0)
                gelu_column(0, KEYS - 2)
                v_column(0, 0)
                lower_v(0, 1)
                v_column(0, 1)
                gelu_column(0, KEYS - 1)
                lower_v(0, 2)
                columns(dve, 2, KEYS, v_column, tail=1)
                for t in range(TILES):
                    dve.wait_ge(products_done, plan.v_index(l, KEYS - TILES + t) + 1)
                    for half in range(2):
                        dve.tensor_copy(xs[:, t, half * 512:(half + 1) * 512], bank[2 * half + t][:, :])\
                           .then_inc(read["x_done"], 1)

            dve.wait_ge(layer_in, 80 * LAYERS + 16)
            for t in range(TILES):
                norm_tile(2 * LAYERS, xfin, t)


def _blocks_of_w_in(w_in):
    names = ["aq", "af", "ai", "ag", "bu", "bv", "cq", "ck", "cv", "iq"]
    blocks = {n: w_in[:, :, k * W:(k + 1) * W] for k, n in enumerate(names)}
    at = len(names) * W
    blocks["small"] = w_in[:, :, at:at + SMALL_COLS]
    for n in range(6):
        blocks[f"gate{n}"] = w_in[:, :, at + SMALL_COLS + n * W:at + SMALL_COLS + (n + 1) * W]
    return blocks


def _rows_to_partitions(w):
    layers, rows, columns = w.shape
    return w.reshape(layers, rows // P, P, columns).transpose(0, 2, 1, 3).reshape(layers, P, -1)


def kernel(**inputs):
    import numpy as _np
    import concourse.bacc as _bacc
    from concourse import mybir as _mybir
    from concourse.bass_utils import run_bass_kernel_spmd as _run

    a = {n: _np.asarray(v) for n, v in inputs.items()}
    blocks = _blocks_of_w_in(a["w_in"])
    stream = _np.empty((LAYERS, ITEMS, P, ITEM), _np.float32)

    def put(name, w):
        columns = w.shape[2]
        if name in BY_COLUMN:
            parts = [_np.concatenate([_rows_to_partitions(w[:, :, m * P:(m + 1) * P]) for m in (2 * q, 2 * q + 1)], 2)
                     for q in range(2)]
        elif name[:2] == "br":
            parts = [_rows_to_partitions(w[:, :, q * columns // 2:(q + 1) * columns // 2]) for q in range(2)]
        else:
            parts = [_rows_to_partitions(w[:, q * D // 2:(q + 1) * D // 2]) for q in range(2)]
        for q in range(2):
            stream[:, FIRST[name] + q] = parts[q]

    for name in BLOCKS:
        put(name, blocks[name])
    for n in range(BRANCHES):
        put(f"br{n}", a["w_branch"][:, n])
    for n in range(2):
        put(f"out{n}", a["w_out"][:, :, n * W:(n + 1) * W])
    for n in range(4):
        put(f"qry{n}", a["peer_w_q"][:, :, n * W:(n + 1) * W])
    stream[:, KEY_ITEM] = a["peer_sub_keys"].transpose(0, 4, 1, 2, 3).reshape(LAYERS, P, HP * KEYS)
    u = a["peer_u"].reshape(LAYERS, KEYS, KEYS // 2, 2, KC, P).transpose(0, 2, 5, 3, 4, 1)
    stream[:, U_ITEM:V_ITEM] = u.reshape(LAYERS, KEYS // 2, P, ITEM)
    v = a["peer_v"].reshape(LAYERS, KEYS, KEYS // 2, 2 * D).transpose(0, 2, 1, 3)
    stream[:, V_ITEM:] = v

    half_c, half_i = P // 2, IDX_DIM // 2
    inv = lambda half: (10000.0 ** (-_np.arange(half, dtype=_np.float32) / _np.float32(half)).astype(_np.float64))\
        .astype(_np.float32)
    consts = _np.zeros((P, 2 * P + 96), _np.float32)
    consts[:, 0:P] = _np.eye(P)
    consts[:, P:2 * P] = _np.arange(P)
    consts[:, 2 * P:] = _np.concatenate([inv(half_c), inv(half_i)])
    s, t = _np.meshgrid(_np.arange(P), _np.arange(P), indexing="ij")
    masks = _np.stack([(s // (2 * h) == t // (2 * h)) & (s % (2 * h) < h) & (t % (2 * h) >= h) for h in HALVES], 1)

    gains = _np.stack([a["norm1_gain"], a["norm2_gain"]], 1)
    arrays = {
        "x": a["x"].reshape(S, D),
        "pos": a["positions"].reshape(TILES, P).T,
        "stream": stream.reshape(LAYERS * ITEMS, P, ITEM),
        "small": _rows_to_partitions(blocks["small"]),
        "wsT": a["gmlp_w_s"].transpose(0, 3, 1, 2).reshape(LAYERS, P, HEADS * P),
        "bsT": a["gmlp_b_s"].transpose(0, 2, 1),
        "cols": gains.reshape(2 * LAYERS, KC, P).transpose(2, 0, 1).reshape(P, 2 * LAYERS * KC),
        "lbl": a["hgrn_lb_logits"].reshape(LAYERS, HEADS, P).transpose(2, 0, 1).reshape(P, LAYERS * HEADS),
        "hgain": a["hgrn_norm_gain"],
        "ggain": a["gmlp_norm_gain"],
        "fgain": a["final_gain"].reshape(1, D),
        "consts": consts,
        "masks": masks.astype(_np.float32).reshape(P, NLEV * P),
    }
    nc = _bacc.Bacc("TRN2", target_bir_lowering=False, num_devices=1)
    args = []
    for name, v in arrays.items():
        arrays[name] = v = _np.ascontiguousarray(v)
        args.append(nc.dram_tensor(f"{name}_dram", v.shape, _mybir.dt.from_np(v.dtype), kind="ExternalInput").ap())
    args.append(nc.dram_tensor("out_dram", (S, D), F32, kind="ExternalOutput").ap())
    trunk_kernel(nc, *args)
    r = _run(nc, [{f"{n}_dram": v for n, v in arrays.items()}], core_ids=[0])
    return r.results[0]["out_dram"].reshape(1, S, D)
```
